# Optimizing a Trainium2 kernel written in Bass

```python
import math
import jax, jax.numpy as jnp
from jax import lax
import numpy as np

D_MODEL = 2048
BATCH = 1
SEQ = 256
DEPTH = 1

SSM_WIDTH = D_MODEL // 2
SSM_GROUP = 16
SSM_GROUPS = SSM_WIDTH // SSM_GROUP
SSM_STATE = 64
ATTN_WIDTH = D_MODEL - SSM_WIDTH
HEAD_DIM = 128
N_HEADS = ATTN_WIDTH // HEAD_DIM
DILATED_BRANCHES = ((128, 1), (512, 4), (2048, 16))
FFN_HIDDEN = ((8 * D_MODEL + 3 * 256 - 1) // (3 * 256)) * 256
IN_PROJ_WIDTH = SSM_WIDTH + 3 * ATTN_WIDTH
N_MOD = 6
DT_MIN = 1e-3
DT_MAX = 1e-1
NORM_EPS = 1e-6
MASK_VALUE = -1e30


def _rms(x, w):
    xf = x.astype(jnp.float32)
    y = xf * lax.rsqrt(jnp.mean(xf * xf, axis=-1, keepdims=True) + NORM_EPS)
    return y * w.astype(jnp.float32)

def _modulate(y, shift, scale):
    return y * (1.0 + scale.astype(jnp.float32)[:, None, :]) + shift.astype(jnp.float32)[:, None, :]

def _complex_linear_combine(e1, e2):
    a1r, a1i, b1r, b1i = e1
    a2r, a2i, b2r, b2i = e2
    ar = a1r * a2r - a1i * a2i
    ai = a1r * a2i + a1i * a2r
    br = a2r * b1r - a2i * b1i + b2r
    bi = a2r * b1i + a2i * b1r + b2i
    return ar, ai, br, bi

def _s5_mixer(u, a_re, a_im, log_dt, b_re, b_im, c_re, c_im, d, w_glu):
    B, S, _ = u.shape
    f32 = jnp.float32
    uf = u.astype(f32).reshape(B, S, SSM_GROUPS, SSM_GROUP)
    a_re = a_re.astype(f32)
    a_im = a_im.astype(f32)
    dt = jnp.exp(log_dt.astype(f32))[:, None]
    mag = jnp.exp(a_re * dt)
    abar_re = mag * jnp.cos(a_im * dt)
    abar_im = mag * jnp.sin(a_im * dt)
    num_re = abar_re - 1.0
    num_im = abar_im
    den = a_re * a_re + a_im * a_im
    z_re = (num_re * a_re + num_im * a_im) / den
    z_im = (num_im * a_re - num_re * a_im) / den
    b_re = b_re.astype(f32)
    b_im = b_im.astype(f32)
    bbar_re = z_re[..., None] * b_re - z_im[..., None] * b_im
    bbar_im = z_re[..., None] * b_im + z_im[..., None] * b_re
    bu_re = jnp.einsum('bsgc,gnc->sbgn', uf, bbar_re)
    bu_im = jnp.einsum('bsgc,gnc->sbgn', uf, bbar_im)
    a_seq_re = jnp.broadcast_to(abar_re[None, None], (S, 1, SSM_GROUPS, SSM_STATE))
    a_seq_im = jnp.broadcast_to(abar_im[None, None], (S, 1, SSM_GROUPS, SSM_STATE))
    _, _, h_re, h_im = lax.associative_scan(
        _complex_linear_combine, (a_seq_re, a_seq_im, bu_re, bu_im), axis=0)
    y = (jnp.einsum('sbgn,gcn->bsgc', h_re, c_re.astype(f32))
         - jnp.einsum('sbgn,gcn->bsgc', h_im, c_im.astype(f32))
         + d.astype(f32) * uf)
    y = jax.nn.gelu(y.reshape(B, S, SSM_WIDTH))
    return y * jax.nn.sigmoid(y @ w_glu.astype(f32))

def _dilated_branch(q, k, v, slopes, window, dilation):
    B, S, H, E = q.shape
    blk = window // dilation
    span = blk * dilation
    s_pad = ((S + span - 1) // span) * span
    pad = s_pad - S
    L = s_pad // dilation
    nb = L // blk

    def strided_blocks(t):
        t = jnp.pad(t, ((0, 0), (0, pad), (0, 0), (0, 0)))
        t = t.reshape(B, L, dilation, H, E).transpose(0, 2, 3, 1, 4)
        return t.reshape(B, dilation, H, nb, blk, E)

    qb, kb, vb = strided_blocks(q), strided_blocks(k), strided_blocks(v)

    def with_prev(t):
        prev = jnp.concatenate([jnp.zeros_like(t[:, :, :, :1]), t[:, :, :, :-1]], axis=3)
        return jnp.concatenate([prev, t], axis=4)

    kc, vc = with_prev(kb), with_prev(vb)
    scores = jnp.einsum('bdhnqe,bdhnke->bdhnqk', qb, kc)
    qi = jnp.arange(blk)[:, None]
    ki = jnp.arange(2 * blk)[None, :]
    dist = qi + blk - ki
    band = (dist >= 0) & (dist <= blk)
    first = (jnp.arange(nb) == 0)[:, None, None]
    valid = band[None] & ~(first & (ki < blk)[None])
    bias = -slopes[:, None, None, None] * (dilation * dist).astype(jnp.float32)[None, None]
    scores = jnp.where(valid, scores + bias, MASK_VALUE)
    m = jnp.max(scores, axis=-1)
    p = jnp.exp(scores - m[..., None])
    l = jnp.sum(p, axis=-1)
    o = jnp.einsum('bdhnqk,bdhnke->bdhnqe', p, vc)

    m = m.reshape(B, dilation, H, L).transpose(0, 3, 1, 2).reshape(B, s_pad, H)[:, :S]
    l = l.reshape(B, dilation, H, L).transpose(0, 3, 1, 2).reshape(B, s_pad, H)[:, :S]
    o = o.reshape(B, dilation, H, L, E).transpose(0, 3, 1, 2, 4).reshape(B, s_pad, H, E)[:, :S]
    return m, l, o

def _dilated_attention(q, k, v, q_norm_w, k_norm_w):
    B, S, _ = q.shape
    q = _rms(q.reshape(B, S, N_HEADS, HEAD_DIM), q_norm_w) * (HEAD_DIM ** -0.5)
    k = _rms(k.reshape(B, S, N_HEADS, HEAD_DIM), k_norm_w)
    v = v.astype(jnp.float32).reshape(B, S, N_HEADS, HEAD_DIM)
    slopes = jnp.exp2(-8.0 * jnp.arange(1, N_HEADS + 1, dtype=jnp.float32) / N_HEADS)
    outs = [_dilated_branch(q, k, v, slopes, w, dl) for (w, dl) in DILATED_BRANCHES]
    ms = jnp.stack([o[0] for o in outs])
    ls = jnp.stack([o[1] for o in outs])
    os_ = jnp.stack([o[2] for o in outs])
    w = jnp.exp(ms - jnp.max(ms, axis=0, keepdims=True))
    num = jnp.sum(w[..., None] * os_, axis=0)
    den = jnp.sum(w * ls, axis=0)
    return (num / den[..., None]).reshape(B, S, ATTN_WIDTH)

def first_inputs(seed: int = 0) -> dict:
    key = jax.random.key(seed)
    ks = jax.random.split(key, 24)
    f32 = jnp.float32
    nrm = lambda k, shape, s: jax.random.normal(k, shape, f32) * s
    D, G, N, C = D_MODEL, SSM_GROUPS, SSM_STATE, SSM_GROUP
    x = jax.random.normal(ks[0], (BATCH, SEQ, D), f32)
    c = jax.random.normal(ks[1], (BATCH, D), f32)
    w_ada = nrm(ks[2], (DEPTH, D, N_MOD * D), 0.5 * D ** -0.5)
    b_ada = nrm(ks[3], (DEPTH, N_MOD * D), 0.05)
    norm1_w = 1.0 + nrm(ks[4], (DEPTH, D), 0.02)
    w_in = nrm(ks[5], (DEPTH, D, IN_PROJ_WIDTH), D ** -0.5)
    ssm_a_re = -0.5 + nrm(ks[6], (DEPTH, G, N), 0.01)
    ssm_a_im = jnp.pi * jnp.arange(N, dtype=f32)[None, None, :] + nrm(ks[7], (DEPTH, G, N), 0.01)
    ssm_log_dt = jax.random.uniform(ks[8], (DEPTH, G), f32, math.log(DT_MIN), math.log(DT_MAX))
    ssm_b_re = nrm(ks[9], (DEPTH, G, N, C), (2 * C) ** -0.5)
    ssm_b_im = nrm(ks[10], (DEPTH, G, N, C), (2 * C) ** -0.5)
    ssm_c_re = nrm(ks[11], (DEPTH, G, C, N), (2 * N) ** -0.5)
    ssm_c_im = nrm(ks[12], (DEPTH, G, C, N), (2 * N) ** -0.5)
    ssm_d = nrm(ks[13], (DEPTH, G, C), 1.0)
    ssm_w_glu = nrm(ks[14], (DEPTH, SSM_WIDTH, SSM_WIDTH), SSM_WIDTH ** -0.5)
    q_norm_w = 1.0 + nrm(ks[15], (DEPTH, HEAD_DIM), 0.02)
    k_norm_w = 1.0 + nrm(ks[16], (DEPTH, HEAD_DIM), 0.02)
    w_out = nrm(ks[17], (DEPTH, D, D), D ** -0.5)
    norm2_w = 1.0 + nrm(ks[18], (DEPTH, D), 0.02)
    w_ffn_gate = nrm(ks[19], (DEPTH, D, FFN_HIDDEN), D ** -0.5)
    w_ffn_up = nrm(ks[20], (DEPTH, D, FFN_HIDDEN), D ** -0.5)
    w_ffn_down = nrm(ks[21], (DEPTH, FFN_HIDDEN, D), FFN_HIDDEN ** -0.5)
    return {"x": x, "c": c, "w_ada": w_ada, "b_ada": b_ada, "norm1_w": norm1_w,
            "w_in": w_in, "ssm_a_re": ssm_a_re, "ssm_a_im": ssm_a_im,
            "ssm_log_dt": ssm_log_dt, "ssm_b_re": ssm_b_re, "ssm_b_im": ssm_b_im,
            "ssm_c_re": ssm_c_re, "ssm_c_im": ssm_c_im, "ssm_d": ssm_d,
            "ssm_w_glu": ssm_w_glu, "q_norm_w": q_norm_w, "k_norm_w": k_norm_w,
            "w_out": w_out, "norm2_w": norm2_w, "w_ffn_gate": w_ffn_gate,
            "w_ffn_up": w_ffn_up, "w_ffn_down": w_ffn_down}

def first_block(x, c, w_ada, b_ada, norm1_w, w_in, ssm_a_re, ssm_a_im, ssm_log_dt,
              ssm_b_re, ssm_b_im, ssm_c_re, ssm_c_im, ssm_d, ssm_w_glu,
              q_norm_w, k_norm_w, w_out, norm2_w, w_ffn_gate, w_ffn_up, w_ffn_down):
    cond = jax.nn.silu(c)
    splits = [SSM_WIDTH, SSM_WIDTH + ATTN_WIDTH, SSM_WIDTH + 2 * ATTN_WIDTH]
    for i in range(DEPTH):
        mod = cond @ w_ada[i] + b_ada[i]
        shift1, scale1, gate1, shift2, scale2, gate2 = jnp.split(mod, N_MOD, axis=-1)

        h = _modulate(_rms(x, norm1_w[i]), shift1, scale1).astype(x.dtype)
        proj = h @ w_in[i]
        u, q, k, v = jnp.split(proj, splits, axis=-1)
        y_ssm = _s5_mixer(u, ssm_a_re[i], ssm_a_im[i], ssm_log_dt[i], ssm_b_re[i], ssm_b_im[i],
                          ssm_c_re[i], ssm_c_im[i], ssm_d[i], ssm_w_glu[i])
        y_att = _dilated_attention(q, k, v, q_norm_w[i], k_norm_w[i])
        mixed = jnp.concatenate([y_ssm, y_att], axis=-1).astype(x.dtype) @ w_out[i]
        x = x + gate1[:, None, :] * mixed

        h2 = _modulate(_rms(x, norm2_w[i]), shift2, scale2).astype(x.dtype)
        ffn = (jax.nn.silu(h2 @ w_ffn_gate[i]) * (h2 @ w_ffn_up[i])) @ w_ffn_down[i]
        x = x + gate2[:, None, :] * ffn
    return x


GRID_W = 64
MEM_LEN = 256
EPS = 1e-6

NA_HEADS = 8
NA_HEAD_DIM = 128
NA_WIDTH = NA_HEADS * NA_HEAD_DIM
NA_ROWS_MAX = 8
NA_COLS = 16

MLA_HEADS = 8
MLA_Q_RANK = 512
MLA_KV_RANK = 256
MLA_NOPE_DIM = 128
MLA_ROPE_DIM = 64
MLA_V_DIM = 128
MLA_QK_DIM = MLA_NOPE_DIM + MLA_ROPE_DIM
MLA_WIDTH = MLA_HEADS * MLA_V_DIM
ROPE_THETA = 10000.0
Q_BLOCK = 128

D_MIX = NA_WIDTH + MLA_WIDTH
IN_WIDTH = 3 * NA_WIDTH + MLA_Q_RANK + MLA_KV_RANK + MLA_ROPE_DIM

X_HEADS = 4
X_HEAD_DIM = D_MODEL // X_HEADS

D_FF = ((8 * D_MODEL + 3 * 256 - 1) // (3 * 256)) * 256


def rmsnorm(x, g):
    xf = x.astype(jnp.float32)
    y = xf * lax.rsqrt(jnp.mean(xf * xf, axis=-1, keepdims=True) + EPS)
    return (y * g.astype(jnp.float32)).astype(x.dtype)

def rope_tables(seq_len):
    inv = 1.0 / (ROPE_THETA ** (jnp.arange(0, MLA_ROPE_DIM, 2, dtype=jnp.float32) / MLA_ROPE_DIM))
    ang = jnp.arange(seq_len, dtype=jnp.float32)[:, None] * inv[None, :]
    return jnp.cos(ang), jnp.sin(ang)

def apply_rope(x, cos, sin):
    xf = x.astype(jnp.float32)
    x1, x2 = jnp.split(xf, 2, axis=-1)
    return jnp.concatenate([x1 * cos - x2 * sin, x1 * sin + x2 * cos], axis=-1).astype(x.dtype)

def neighbourhood_attention(q, k, v, rpb):
    B, S, H, dh = q.shape
    rows = S // GRID_W
    kr = min(NA_ROWS_MAX, rows)
    qg = q.reshape(B, rows, GRID_W, H, dh)
    kg = k.reshape(B, rows, GRID_W, H, dh)
    vg = v.reshape(B, rows, GRID_W, H, dh)
    row_start = jnp.clip(jnp.arange(rows) - kr // 2, 0, rows - kr)
    col_start = np.clip(np.arange(GRID_W) - NA_COLS // 2, 0, GRID_W - NA_COLS)
    col_idx = col_start[:, None] + np.arange(NA_COLS)[None, :]
    dc = col_idx - np.arange(GRID_W)[:, None] + (NA_COLS - 1)
    bias_c = rpb[:, :, dc]
    scale = dh ** -0.5

    def one_row(r):
        rs = row_start[r]
        kb = lax.dynamic_slice_in_dim(kg, rs, kr, axis=1)[:, :, col_idx]
        vb = lax.dynamic_slice_in_dim(vg, rs, kr, axis=1)[:, :, col_idx]
        qr = lax.dynamic_index_in_dim(qg, r, axis=1, keepdims=False)
        s = jnp.einsum('bqhd,brqkhd->bhqrk', qr, kb).astype(jnp.float32) * scale
        dr = rs + jnp.arange(kr) - r + (NA_ROWS_MAX - 1)
        bias = jnp.transpose(bias_c[:, dr], (0, 2, 1, 3)).astype(jnp.float32)
        s = s + bias[None]
        p = jax.nn.softmax(s.reshape(B, H, GRID_W, kr * NA_COLS), axis=-1)
        p = p.reshape(B, H, GRID_W, kr, NA_COLS).astype(v.dtype)
        return jnp.einsum('bhqrk,brqkhd->bqhd', p, vb)

    out = lax.map(one_row, jnp.arange(rows))
    return jnp.moveaxis(out, 0, 1).reshape(B, S, H * dh)

def latent_attention(c_q, c_kv, k_rope, q_norm, kv_norm, w_uq, w_ukv, cos, sin):
    B, S, _ = c_q.shape
    q = (rmsnorm(c_q, q_norm) @ w_uq).reshape(B, S, MLA_HEADS, MLA_QK_DIM)
    q_nope, q_rope = q[..., :MLA_NOPE_DIM], q[..., MLA_NOPE_DIM:]
    q_rope = apply_rope(q_rope, cos[:, None, :], sin[:, None, :])
    kv = (rmsnorm(c_kv, kv_norm) @ w_ukv).reshape(B, S, MLA_HEADS, MLA_NOPE_DIM + MLA_V_DIM)
    k_nope, v = kv[..., :MLA_NOPE_DIM], kv[..., MLA_NOPE_DIM:]
    k_r = apply_rope(k_rope, cos, sin)
    nb = S // Q_BLOCK
    qn_b = jnp.moveaxis(q_nope.reshape(B, nb, Q_BLOCK, MLA_HEADS, MLA_NOPE_DIM), 1, 0)
    qr_b = jnp.moveaxis(q_rope.reshape(B, nb, Q_BLOCK, MLA_HEADS, MLA_ROPE_DIM), 1, 0)
    scale = MLA_QK_DIM ** -0.5

    def block(args):
        qn, qr = args
        s = (jnp.einsum('bqhd,bkhd->bhqk', qn, k_nope)
             + jnp.einsum('bqhr,bkr->bhqk', qr, k_r)).astype(jnp.float32) * scale
        p = jax.nn.softmax(s, axis=-1).astype(v.dtype)
        return jnp.einsum('bhqk,bkhd->bqhd', p, v)

    out = lax.map(block, (qn_b, qr_b))
    return jnp.moveaxis(out, 0, 1).reshape(B, S, MLA_WIDTH)

def memory_attention(h, mem_n, w_q, w_k, w_v, w_o):
    B, S, _ = h.shape
    M = mem_n.shape[1]
    q = (h @ w_q).reshape(B, S, X_HEADS, X_HEAD_DIM)
    k = (mem_n @ w_k).reshape(B, M, X_HEADS, X_HEAD_DIM)
    v = (mem_n @ w_v).reshape(B, M, X_HEADS, X_HEAD_DIM)
    s = jnp.einsum('bqhd,bkhd->bhqk', q, k).astype(jnp.float32) * (X_HEAD_DIM ** -0.5)
    p = jax.nn.softmax(s, axis=-1).astype(v.dtype)
    o = jnp.einsum('bhqk,bkhd->bqhd', p, v).reshape(B, S, D_MODEL)
    return o @ w_o

def swiglu(h, w_gate, w_up, w_down):
    return (jax.nn.silu(h @ w_gate) * (h @ w_up)) @ w_down

def second_inputs(seed: int = 0) -> dict:
    key = jax.random.key(seed)
    ks = jax.random.split(key, 24)

    def dense(k, shape, fan_in):
        return jax.random.normal(k, shape, jnp.float32) * (fan_in ** -0.5)

    def gain(k, shape):
        return 1.0 + 0.02 * jax.random.normal(k, shape, jnp.float32)

    L = DEPTH
    return {
        "x": jax.random.normal(ks[0], (BATCH, SEQ, D_MODEL), jnp.float32),
        "mem": jax.random.normal(ks[1], (BATCH, MEM_LEN, D_MODEL), jnp.float32),
        "ln_mix": gain(ks[2], (L, D_MODEL)),
        "w_in": dense(ks[3], (L, D_MODEL, IN_WIDTH), D_MODEL),
        "q_norm": gain(ks[4], (L, MLA_Q_RANK)),
        "kv_norm": gain(ks[5], (L, MLA_KV_RANK)),
        "w_uq": dense(ks[6], (L, MLA_Q_RANK, MLA_HEADS * MLA_QK_DIM), MLA_Q_RANK),
        "w_ukv": dense(ks[7], (L, MLA_KV_RANK, MLA_HEADS * (MLA_NOPE_DIM + MLA_V_DIM)), MLA_KV_RANK),
        "na_rpb": 0.1 * jax.random.normal(ks[8], (L, NA_HEADS, 2 * NA_ROWS_MAX - 1, 2 * NA_COLS - 1), jnp.float32),
        "na_out_norm": gain(ks[9], (L, NA_WIDTH)),
        "mla_out_norm": gain(ks[10], (L, MLA_WIDTH)),
        "w_out": dense(ks[11], (L, D_MIX, D_MODEL), D_MIX),
        "ln_mem": gain(ks[12], (L, D_MODEL)),
        "mem_norm": gain(ks[13], (L, D_MODEL)),
        "w_xq": dense(ks[14], (L, D_MODEL, D_MODEL), D_MODEL),
        "w_xk": dense(ks[15], (L, D_MODEL, D_MODEL), D_MODEL),
        "w_xv": dense(ks[16], (L, D_MODEL, D_MODEL), D_MODEL),
        "w_xo": dense(ks[17], (L, D_MODEL, D_MODEL), D_MODEL),
        "ln_ffn": gain(ks[18], (L, D_MODEL)),
        "w_gate": dense(ks[19], (L, D_MODEL, D_FF), D_MODEL),
        "w_up": dense(ks[20], (L, D_MODEL, D_FF), D_MODEL),
        "w_down": dense(ks[21], (L, D_FF, D_MODEL), D_FF),
        "final_norm": gain(ks[22], (D_MODEL,)),
    }

def second_block(x, mem, ln_mix, w_in, q_norm, kv_norm, w_uq, w_ukv, na_rpb, na_out_norm,
              mla_out_norm, w_out, ln_mem, mem_norm, w_xq, w_xk, w_xv, w_xo, ln_ffn,
              w_gate, w_up, w_down, final_norm):
    B, S, _ = x.shape
    cos, sin = rope_tables(S)
    o1 = NA_WIDTH
    o2 = 2 * NA_WIDTH
    o3 = 3 * NA_WIDTH
    o4 = o3 + MLA_Q_RANK
    o5 = o4 + MLA_KV_RANK
    for l in range(DEPTH):
        h = rmsnorm(x, ln_mix[l])
        proj = h @ w_in[l]
        q_na = proj[..., :o1].reshape(B, S, NA_HEADS, NA_HEAD_DIM)
        k_na = proj[..., o1:o2].reshape(B, S, NA_HEADS, NA_HEAD_DIM)
        v_na = proj[..., o2:o3].reshape(B, S, NA_HEADS, NA_HEAD_DIM)
        c_q = proj[..., o3:o4]
        c_kv = proj[..., o4:o5]
        k_rope = proj[..., o5:]
        y_na = neighbourhood_attention(q_na, k_na, v_na, na_rpb[l])
        y_mla = latent_attention(c_q, c_kv, k_rope, q_norm[l], kv_norm[l], w_uq[l], w_ukv[l], cos, sin)
        y = jnp.concatenate([rmsnorm(y_na, na_out_norm[l]), rmsnorm(y_mla, mla_out_norm[l])], axis=-1)
        x = x + y @ w_out[l]
        h = rmsnorm(x, ln_mem[l])
        x = x + memory_attention(h, rmsnorm(mem, mem_norm[l]), w_xq[l], w_xk[l], w_xv[l], w_xo[l])
        h = rmsnorm(x, ln_ffn[l])
        x = x + swiglu(h, w_gate[l], w_up[l], w_down[l])
    return rmsnorm(x, final_norm)


def setup_inputs(seed=0):
    out = dict(first_inputs(seed))
    for name, value in second_inputs(seed + 1).items():
        if name != "x":
            out[name + "_2"] = value
    return out


def reference(
    x, c, w_ada, b_ada, norm1_w, w_in, ssm_a_re, ssm_a_im, ssm_log_dt, ssm_b_re, ssm_b_im,
    ssm_c_re, ssm_c_im, ssm_d, ssm_w_glu, q_norm_w, k_norm_w, w_out, norm2_w, w_ffn_gate,
    w_ffn_up, w_ffn_down, mem_2, ln_mix_2, w_in_2, q_norm_2, kv_norm_2, w_uq_2, w_ukv_2,
    na_rpb_2, na_out_norm_2, mla_out_norm_2, w_out_2, ln_mem_2, mem_norm_2, w_xq_2, w_xk_2,
    w_xv_2, w_xo_2, ln_ffn_2, w_gate_2, w_up_2, w_down_2, final_norm_2,
):
    x = first_block(
        x, c, w_ada, b_ada, norm1_w, w_in, ssm_a_re, ssm_a_im, ssm_log_dt, ssm_b_re, ssm_b_im,
        ssm_c_re, ssm_c_im, ssm_d, ssm_w_glu, q_norm_w, k_norm_w, w_out, norm2_w, w_ffn_gate,
        w_ffn_up, w_ffn_down,
    )
    return second_block(
        x, mem_2, ln_mix_2, w_in_2, q_norm_2, kv_norm_2, w_uq_2, w_ukv_2, na_rpb_2,
        na_out_norm_2, mla_out_norm_2, w_out_2, ln_mem_2, mem_norm_2, w_xq_2, w_xk_2, w_xv_2,
        w_xo_2, ln_ffn_2, w_gate_2, w_up_2, w_down_2, final_norm_2,
    )


_drawn_inputs = setup_inputs


def setup_inputs(seed=0):
    import zlib

    import numpy as np

    out = dict(_drawn_inputs(seed))
    spreads = {}
    factors = {'norm1_w': 8.0,
     'ssm_a_re': 64.0,
     'ssm_a_im': 43.096,
     'ssm_log_dt': 60.272,
     'ssm_b_re': 60.352,
     'ssm_b_im': 64.0,
     'ssm_c_re': 60.232,
     'ssm_c_im': 64.0,
     'q_norm_w': 8.0,
     'k_norm_w': 8.0,
     'norm2_w': 7.186,
     'q_norm_2': 7.149,
     'kv_norm_2': 4.162,
     'na_out_norm_2': 5.143,
     'mla_out_norm_2': 5.336,
     'ln_mem_2': 8.0,
     'mem_norm_2': 8.0,
     'ln_ffn_2': 5.092,
     'final_norm_2': 8.068}
    for name, (base, spread) in spreads.items():
        noise = np.random.default_rng([zlib.crc32(name.encode()), seed]).standard_normal(out[name].shape)
        drawn = base * np.exp(spread * noise) if base else spread * noise
        out[name] = __import__('jax').numpy.asarray(drawn.astype(out[name].dtype))
    for name, factor in factors.items():
        out[name] = (out[name] * factor).astype(out[name].dtype)
    return out
```

```python
from contextlib import ExitStack

import concourse.bass as bass
from concourse import mybir
from concourse.alu_op_type import AluOpType as ALU

F32 = mybir.dt.float32
F32R = mybir.dt.float32r
BF16 = mybir.dt.bfloat16
ACT = mybir.ActivationFunctionType
AX = mybir.AxisListType

P = 128
D = 2048
S = 256
RT = S // P
KD = D // P
CW = 512
UK = 4
RING = 4
LOOKAHEAD = 3
EPS = 1e-6

SSM_W = 1024
GROUPS, GC, NST = 64, 16, 64
STILES = GROUPS * NST // P
HEADS, HD = 8, 128
X_HEADS, XHD = 4, 512
XKT = XHD // P
FF = 5632
FCH = FF // CW
THIRDS = ((0, 4), (4, 4), (8, 3))
GRID_W, NA_ROWS, NA_COLS, NA_RMAX = 64, 4, 16, 8
NA_DR, NA_DC = 2 * NA_RMAX - 1, 2 * NA_COLS - 1
TOEP_W = 128
TOEP_AT = (GRID_W - 1) - (NA_COLS - 1)
NOPE, ROPE, VD = 128, 64, 128
HROPE = ROPE // 2
QK = NOPE + ROPE
Q_RANK, KV_RANK = 512, 256
NA_W = 1024
IN2 = 3 * NA_W + Q_RANK + KV_RANK + ROPE
C_Q = 3 * NA_W
C_KV = C_Q + Q_RANK
C_KR = C_KV + KV_RANK
TWO_PI = 6.283185307179586
PI_HEAD = 6.28125
PI_REST = TWO_PI - PI_HEAD
MAGIC = 12582912.0

VECS = (("norm1_w", 16), ("norm2_w", 16), ("ln_mix_2", 16), ("ln_mem_2", 16), ("mem_norm_2", 16), ("ln_ffn_2", 16),
        ("na_out_norm_2", 8), ("mla_out_norm_2", 8), ("ssm_d", 8), ("q_norm_2", 4), ("kv_norm_2", 2),
        ("q_norm_w", 1), ("k_norm_w", 1))
VAT = {}
_at = 0
for _n, _k in VECS:
    VAT[_n] = _at
    _at += _k

NT = dict(mem=(16, 1), h1=(16, 1), yatt=(8, 0), h2=(16, 1), hmix=(16, 1), cq=(4, 1), ckv=(2, 1), yna=(8, 1),
          ymla=(8, 1), hmem=(16, 1), ocross=(16, 0), hffn=(16, 1))
PAIR0, STAT0, XN0 = {}, {}, {}
_p = _s = _x = 0
for _n, (_k, _st) in NT.items():
    PAIR0[_n], STAT0[_n], XN0[_n] = _p, _s, _x
    _p += _k // 2
    _s += _st
    _x += _st * (_k // 2)
STAT0["final"] = _s

UNIT0, CHUNK0 = {}, {}
_u = _q = 0
for _n, _uu, _qq in (("xk_ada", 48, 4), ("xv", 16, 4), ("in_ada", 96, 8), ("glu", 4, 2), ("out1", 16, 4),
                     ("ffn1", 132, 34), ("in2", 32, 8), ("uq", 4, 4), ("ukv", 4, 4), ("out2", 16, 4),
                     ("xq", 16, 4), ("xo", 16, 4), ("ffn2", 132, 34)):
    UNIT0[_n], CHUNK0[_n] = _u, _q
    _u += _uu
    _q += _qq
UNITS, CHUNKS = _u, _q
HEAD0 = dict(dil=0, na=8, mla=16, cross=24)
ARENA = 207 * 1024 + 512
UNIT0["end"], CHUNK0["end"] = UNITS, CHUNKS
PAR = {n: i for i, n in enumerate(
    "dt ard mag th k r sin sh sh2 phl den rden cos nr ni t1 t2 zr zi".split())}


def build(nc, A, out):
    with ExitStack() as ctx:
        base = (nc.sbuf_base + 63) // 64 * 64
        size = ARENA
        ctx.enter_context(nc.sbuf_tensor("arena", [P, size // 4 + 16], F32))

        def sb(name, offset, shape, dt=F32):
            count = 1
            for n in shape[1:]:
                count *= n
            assert offset + count * (2 if dt == BF16 else 4) <= size, name
            return nc.alloc_sbuf_tensor_at(name, shape, dt, offset=base + offset)

        KB = 1024
        raw = [sb(f"raw{s}", 8 * KB * s, [P, UK, CW]) for s in range(RING)]
        whi = [sb(f"whi{s}", 8 * KB * (4 + s), [P, UK, CW], F32R) for s in range(RING)]
        wlo = [sb(f"wlo{s}", 8 * KB * (8 + s), [P, UK, CW], F32R) for s in range(RING)]
        x = sb("x", 96 * KB, [P, RT, D])
        sa_hi = sb("sa_hi", 112 * KB, [P, 8, S], F32R)
        sa_lo = sb("sa_lo", 120 * KB, [P, 8, S], F32R)
        s2_hi = sb("s2_hi", 128 * KB, [P, 8, S], F32R)
        s2_lo = sb("s2_lo", 136 * KB, [P, 8, S], F32R)
        qkT = [sb(f"qkT{b}", (128 + 2 * b) * KB, [P, 2, S]) for b in range(2)]
        xqT = sb("xqT", 128 * KB, [P, XKT, S])
        sp = [sb(f"sp{b}", (132 + 2 * b) * KB, [P, RT, S]) for b in range(2)]
        pT = [sb(f"pT{b}", (136 + 2 * b) * KB, [P, RT, S]) for b in range(2)]
        rT = [sb(f"rT{b}", (140 + b) * KB, [ROPE, S]) for b in range(2)]
        sqs = sb("sqs", 132 * KB, [P, SSM_W])
        krT = sb("krT", 142 * KB, [ROPE, S])
        xn = [sb(f"xn{b}", (144 + 2 * b) * KB, [P, RT, 2 * P]) for b in range(2)]
        full = [sb(f"full{b}", (148 + 2 * b) * KB, [P, 2, S]) for b in range(2)]
        junk = sb("junk", 144 * KB, [P, RT, D], BF16)
        at = [152 * KB]

        def small(name, shape, dt=F32):
            count = 1
            for n in shape[1:]:
                count *= n
            t = sb(name, at[0], shape, dt)
            at[0] += (4 * count + 31) // 32 * 32
            return t

        ident = small("ident", [P, P])
        vcol = small("vcol", [P, P])
        modc = small("modc", [P, 96])
        scol = [small(f"scol{b}", [P, KD]) for b in range(2)]
        ccol = small("ccol", [P, 2 * KD + P], F32R)
        qscol = small("qscol", [P, 1])
        ss = small("ss", [P, RT])
        var = small("var", [P, RT])
        rstd = small("rstd", [P, RT])
        neghalf = small("neghalf", [P, 2 * RT * HEADS])
        mx = small("mx", [P, 2, RT])
        negm = small("negm", [P, 2, RT])
        rsum = small("rsum", [P, 2, RT])
        rden = small("rden", [P, 2, RT])
        qk_ss = small("qk_ss", [P, RT, 2 * HEADS])
        qk_rs = small("qk_rs", [P, RT, 2 * HEADS])
        parity = small("parity", [P, 2])
        PH = 155 * KB + 512
        assert at[0] <= PH, at[0]
        mem = sb("mem", PH, [P, RT, D])
        kvst = [sb(f"kvst{b}", PH + (16 + 4 * b) * KB, [P, RT, CW]) for b in range(2)]
        vrow = sb("vrow", PH + 24 * KB, [P, P])
        crow = sb("crow", PH + 25 * KB, [KD, P])
        csil = sb("csil", PH + 26 * KB, [KD, P])
        cT = sb("cT", PH + 27 * KB, [P, KD])
        adast = [sb(f"adast{b}", PH + (44 + 2 * b) * KB, [2, CW]) for b in range(2)]
        mrow = [sb(f"mrow{n}", PH + (48 + n) * KB, [64, 2, P]) for n in range(2)]
        mbias = [sb(f"mbias{n}", PH + 50 * KB + 512 * n, [64, P]) for n in range(2)]
        proj = sb("proj", PH, [P, RT, 4 * SSM_W])
        uT = sb("uT", PH + 32 * KB, [P, 8, S])
        dist = sb("dist", PH + 40 * KB, [P, RT, S])
        mult = sb("mult", PH + 42 * KB, [P, RT, S])
        bt = [sb(f"bt{c}", PH + 4 * KB * c, [P, 8, P]) for c in range(2)]
        ct = [sb(f"ct{c}", PH + (8 + 4 * c) * KB, [P, 8, P]) for c in range(2)]
        bb = [sb(f"bb{c}", PH + (16 + 4 * c) * KB, [P, STILES, 2 * GC]) for c in range(2)]
        bn = [sb(f"bn{c}", PH + (24 + 2 * c) * KB, [P, STILES, GC]) for c in range(2)]
        cn = [sb(f"cn{c}", PH + (28 + 2 * c) * KB, [P, 8, NST]) for c in range(2)]
        cc = [sb(f"cc{c}", PH + (40 + 4 * c) * KB, [P, 8, P]) for c in range(2)]
        btmp = sb("btmp", PH + 40 * KB, [P, 4, STILES, GC])
        turn = sb("turn", PH + 16 * KB, [P, 4, S])
        half = sb("half", PH + 20 * KB, [P, 4, S])
        co = sb("co", PH + 24 * KB, [P, 4, S])
        si = sb("si", PH + 28 * KB, [P, 4, S])
        prod = sb("prod", PH + 40 * KB, [P, 4, S])
        rot = sb("rot", PH + 44 * KB, [P, 4, S])
        iota = sb("iota", PH + 48 * KB, [P, S])
        yt = sb("yt", PH + 49 * KB, [P, S])
        gt = sb("gt", PH + 50 * KB, [P, S])
        SP_ = 144 * KB
        srow = sb("srow", SP_, [96, P])
        dtr = sb("dtr", SP_ + 512, [96, 2])
        scolp = sb("scolp", SP_ + 1024, [P, 96])
        NPAR = 24
        par = sb("par", SP_ + 2 * KB, [P, NPAR, STILES])
        phh = sb("phh", SP_ + 6 * KB, [P, STILES], F32R)
        y2_hi = sb("y2_hi", PH, [P, 8, S], F32R)
        y2_lo = sb("y2_lo", PH + 8 * KB, [P, 8, S], F32R)
        sig = sb("sig", PH + 16 * KB, [P, 8, S])
        gate1_b = sb("gate1_b", PH + 24 * KB, [P, D])
        act_hi = sb("act_hi", PH, [P, 16, S], F32R)
        act_lo = sb("act_lo", PH + 16 * KB, [P, 16, S], F32R)
        fg = sb("fg", PH + 32 * KB, [P, RT, CW])
        rtmp = sb("rtmp", PH + 40 * KB, [P, RT, CW])
        wide_b = sb("wide_b", PH + 44 * KB, [P, D])
        proj2 = sb("proj2", PH, [P, RT, IN2])
        q_mla = sb("q_mla", PH + 31 * KB, [P, RT, HEADS, QK])
        bias = [sb(f"bias{b}", PH + (43 + 2 * b) * KB, [P, RT, S]) for b in range(2)]
        colmask = sb("colmask", PH + 47 * KB, [P, S])
        ropec = sb("ropec", PH + 48 * KB, [P, RT, HROPE])
        ropes = sb("ropes", PH + 48 * KB + 256, [P, RT, HROPE])
        zrow = sb("zrow", PH + 48 * KB + 512, [HEADS * NA_DR, TOEP_W])
        kr = sb("kr", PH + 49 * KB, [P, RT, ROPE])
        xq = sb("xq", PH, [P, RT, D])
        xkT = sb("xkT", PH + 16 * KB, [P, KD, S])
        xkv = sb("xkv", PH + 32 * KB, [P, RT, D])

        bank = [ctx.enter_context(nc.psum_tensor(f"bank{i}", [P, CW], F32)) for i in range(8)]

        scr_k = nc.dram_tensor("scr_k", (S, D), F32).ap().rearrange("(t p) n -> p t n", p=P)
        scr_v = nc.dram_tensor("scr_v", (S, D), F32).ap().rearrange("(t p) n -> p t n", p=P)
        scr_ada = nc.dram_tensor("scr_ada", (2, 6 * D), F32).ap()
        scr_gate = nc.dram_tensor("scr_gate", (64, P), F32).ap()
        scr_toep = nc.dram_tensor("scr_toep", (HEADS * NA_DR, GRID_W * GRID_W), F32).ap()
        scr_rpb = nc.dram_tensor("scr_rpb", (HEADS * NA_DR, TOEP_W), F32).ap()

        def sem(name):
            return ctx.enter_context(nc.semaphore(name))

        landed = [sem(f"landed{s}") for s in range(RING)]
        hi_done = sem("hi_done")
        lo_done = sem("lo_done")
        used = sem("used")
        acc_free = [sem(f"acc_free{p}") for p in range(2)]
        x_upd = sem("x_upd")
        gated = sem("gated")
        ada_full = sem("ada_full")
        ada_free = [sem(f"ada_free{b}") for b in range(2)]
        adast_free = [sem(f"adast_free{b}") for b in range(2)]
        kvst_free = [sem(f"kvst_free{b}") for b in range(2)]
        nt_sq = [sem("nt_sq0"), sem("nt_sq1")]
        nt_var, nt_rstd, nt_xn, nt_tp, nt_full, nt_hi, nt_out = (
            sem(n) for n in ("nt_var", "nt_rstd", "nt_xn", "nt_tp", "nt_full", "nt_hi", "nt_out"))
        tp_done, tp_out = sem("tp_done"), sem("tp_out")
        (at_t, at_qk, at_rope, at_s, at_sb, at_mx, at_m, at_e, at_pm, at_r, at_pt, at_pc, at_o, at_y) = (
            sem(n) for n in ("at_t", "at_qk", "at_rope", "at_s", "at_sb", "at_mx", "at_m", "at_e", "at_pm", "at_r",
                             "at_pt", "at_pc", "at_o", "at_y"))
        ld = {n: sem("ld_" + n) for n in (
            "x", "mem", "vec", "c", "mrow0", "mrow1", "masks", "spar", "sdt", "sb", "sc", "iota", "gate1", "gate2",
            "rpb0", "rpb1", "rpb2", "toep", "bias0", "bias1", "na_const", "xk", "xv", "final", "parity", "gstore")}
        (s_id, s_half, s_vec, s_vcol, s_csil, s_ct, s_cT, s_ccol, s_mod, s_modT, s_modc, s_qk, s_qkv, s_qkr, s_qkn,
         s_kr, s_zero, s_fin, s_out) = (
            sem(n) for n in ("s_id", "s_half", "s_vec", "s_vcol", "s_csil", "s_ct", "s_cT", "s_ccol", "s_mod", "s_modT",
                             "s_modc", "s_qk", "s_qkv", "s_qkr", "s_qkn", "s_kr", "s_zero", "s_fin", "s_out"))
        link_dve = sem("link_dve")
        (ss_par, ss_parT, ss_pc, ss_exp, ss_bb, ss_btp, ss_btc, ss_ang, ss_sin, ss_tab, ss_bu, ss_rot, ss_scan,
         ss_prod, ss_y, ss_yt, ss_gt, ss_g, ss_trig, ss_gs) = (
            sem(n) for n in ("ss_par", "ss_parT", "ss_pc", "ss_exp", "ss_bb", "ss_btp", "ss_btc", "ss_ang", "ss_sin",
                             "ss_tab", "ss_bu", "ss_rot", "ss_scan", "ss_prod", "ss_y", "ss_yt", "ss_gt", "ss_g",
                             "ss_trig", "ss_gs"))
        ss_d, s_kb, s_krt, s_krT, gl_y2 = (sem(n) for n in ("ss_d", "s_kb", "s_krt", "s_krT", "gl_y2"))
        ff_tp, ff_hi, ff_lo = (sem(n) for n in ("ff_tp", "ff_hi", "ff_lo"))

        def sa(k):
            return (sa_hi[:, k, :], sa_lo[:, k, :]) if k < 8 else (s2_hi[:, k - 8, :], s2_lo[:, k - 8, :])

        def vec(name, k=0):
            return vcol[:, VAT[name] + k:VAT[name] + k + 1]

        def chunks_out(eng, q):
            eng.wait_ge(acc_free[0], 2 + 2 * ((q + 1) // 2))
            eng.wait_ge(acc_free[1], 2 + 2 * (q // 2))

        NTSRC = {
            "mem": lambda t, c, w: mem[:, t, c:c + w], "h1": lambda t, c, w: x[:, t, c:c + w],
            "yatt": lambda t, c, w: proj[:, t, SSM_W + c:SSM_W + c + w],
            "cq": lambda t, c, w: proj2[:, t, C_Q + c:C_Q + c + w],
            "ckv": lambda t, c, w: proj2[:, t, C_KV + c:C_KV + c + w],
            "yna": lambda t, c, w: proj2[:, t, c:c + w],
            "ymla": lambda t, c, w: q_mla[:, t, c // VD:(c + w) // VD, 0:VD],
            "ocross": lambda t, c, w: xq[:, t, c:c + w]}
        for n in ("h2", "hmix", "hmem", "hffn", "final"):
            NTSRC[n] = NTSRC["h1"]
        NTSCALE = {"mem": "mem_norm_2", "hmix": "ln_mix_2", "cq": "q_norm_2", "ckv": "kv_norm_2",
                   "yna": "na_out_norm_2", "ymla": "mla_out_norm_2", "hmem": "ln_mem_2", "hffn": "ln_ffn_2"}
        NTK0 = {"yatt": 8, "ckv": 4, "ymla": 8}

        QKSRC = {
            "dil": [lambda t, h, w=w: proj[:, t, SSM_W * w + h * HD:SSM_W * w + h * HD + HD] for w in (1, 2)],
            "na": [lambda t, h, w=w: proj2[:, t, NA_W * w + h * HD:NA_W * w + h * HD + HD] for w in (0, 1)],
            "mla": [lambda t, h: q_mla[:, t, h, 0:NOPE],
                    lambda t, h: proj2[:, t, NA_W + h * (NOPE + VD):NA_W + h * (NOPE + VD) + NOPE]]}
        VSRC = {
            "dil": lambda t, h: proj[:, t, 3 * SSM_W + h * HD:3 * SSM_W + h * HD + HD],
            "na": lambda t, h: proj2[:, t, 2 * NA_W + h * HD:2 * NA_W + h * HD + HD],
            "mla": lambda t, h: proj2[:, t, NA_W + h * (NOPE + VD) + NOPE:NA_W + (h + 1) * (NOPE + VD)],
            "cross": lambda t, h: xkv[:, t, h * XHD:h * XHD + XHD]}
        YDST = {"dil": QKSRC["dil"][0], "na": QKSRC["na"][0], "mla": QKSRC["mla"][0],
                "cross": lambda t, h: xq[:, t, h * XHD:h * XHD + XHD]}

        block = ctx.enter_context(nc.Block())

        def bcast(ap, *dims):
            return bass.AP(ap.tensor, ap.offset, [list(ap.ap[0])] + [list(d) for d in dims])

        def src_ready(eng, name):
            if name == "mem":
                eng.wait_ge(ld["mem"], 16)
            elif name == "h1":
                eng.wait_ge(ld["x"], 16)
            elif name in ("yatt", "yna", "ymla", "ocross"):
                eng.wait_ge(at_y, {"yatt": 8, "yna": 16, "ymla": 24, "ocross": 28}[name])
            elif name == "h2":
                eng.wait_ge(x_upd, 2 + 2 * 4)
            elif name == "hmix":
                eng.wait_ge(x_upd, 2 + 2 * 4 + 2 * 12)
            else:
                chunks_out(eng, CHUNK0[{"cq": "uq", "ckv": "uq", "hmem": "xq", "hffn": "ffn2", "final": "end"}[name]])

        def heads(kind):
            return range(HEAD0[kind], HEAD0[kind] + (X_HEADS if kind == "cross" else HEADS))

        @block.sync
        def _(sp_):
            sp_.dma_start(mem[:, :, :], A["mem_2"].rearrange("b (t p) n -> p (b t) n", p=P)).then_inc(ld["mem"], 16)
            sp_.dma_start(crow[:, :], A["c"].rearrange("b (k p) -> (b k) p", p=P)).then_inc(ld["c"], 16)
            for name, k in VECS:
                w = A[name]
                flat = bass.AP(w.tensor, w.offset, [[P, k], [1, P]])
                sp_.dma_start(vrow[VAT[name]:VAT[name] + k, :], flat).then_inc(ld["vec"], 16)
            sp_.dma_start(x[:, :, :], A["x"].rearrange("b (t p) n -> p (b t) n", p=P)).then_inc(ld["x"], 16)

            def kview(name):
                w = A[name]
                return w.rearrange("d (k p) n -> p (d k) n", p=P)

            def load(blk, j, w, k, kt, col, cols):
                u = 4 * blk + j
                sp_.wait_ge(lo_done, u + 1)
                sp_.dma_start(raw[j % RING][:, 0:kt, 0:cols], w[:, k:k + kt, bass.ds(col, cols)])\
                   .then_inc(landed[j % RING], 16)

            def load_chunk(blk, j, w, col, units=4, cols=CW, kt=UK, k0=0):
                for n in range(units):
                    load(blk, j + n, w, k0 + n * kt, kt, col, cols)

            ada, wk, wv = kview("w_ada"), kview("w_xk_2"), kview("w_xv_2")
            with sp_.Fori(0, 2) as i:
                blk = UNIT0["xk_ada"] // 4 + i * 6
                for c in range(2):
                    for a in range(2):
                        load_chunk(blk, 12 * c + 4 * a, ada, i * (4 * CW) + (2 * c + a) * CW)
                    load_chunk(blk, 12 * c + 8, wk, i * (2 * CW) + c * CW)
            with sp_.Fori(0, 2) as i:
                for c in range(2):
                    load_chunk(UNIT0["xv"] // 4 + i * 2, 4 * c, wv, i * (2 * CW) + c * CW)
            w = kview("w_in")
            with sp_.Fori(0, 4) as i:
                blk = UNIT0["in_ada"] // 4 + i * 6
                for c in range(2):
                    load_chunk(blk, 12 * c, w, i * (2 * CW) + c * CW)
                    for a in range(2):
                        load_chunk(blk, 12 * c + 4 + 4 * a, ada, i * (4 * CW) + (8 + 2 * c + a) * CW)
            w = kview("ssm_w_glu")
            for c in range(2):
                load_chunk(UNIT0["glu"] // 4, 2 * c, w, c * CW, units=2)

            def square(stage, name):
                w = kview(name)
                with sp_.Fori(0, 2) as i:
                    for c in range(2):
                        load_chunk(UNIT0[stage] // 4 + i * 2, 4 * c, w, i * (2 * CW) + c * CW)

            def ffn(stage, gate, up, down):
                g, u, dn = kview(gate), kview(up), kview(down)
                blk = UNIT0[stage] // 4
                for c0, n in THIRDS:
                    with sp_.Fori(0, n) as i:
                        load_chunk(blk + i * 2, 0, g, i * CW + c0 * CW)
                        load_chunk(blk + i * 2, 4, u, i * CW + c0 * CW)
                    blk += 2 * n
                    if n == 4:
                        with sp_.Fori(0, 2) as i:
                            for c in range(2):
                                load_chunk(blk + i * 2, 4 * c, dn, i * (2 * CW) + c * CW, k0=4 * c0)
                    else:
                        for c in range(4):
                            load_chunk(blk, n * c, dn, c * CW, units=n, k0=4 * c0)
                    blk += n

            square("out1", "w_out")
            ffn("ffn1", "w_ffn_gate", "w_ffn_up", "w_ffn_down")
            w = kview("w_in_2")
            with sp_.Fori(0, 3) as i:
                for c in range(2):
                    load_chunk(UNIT0["in2"] // 4 + i * 2, 4 * c, w, i * (2 * CW) + c * CW)
            load_chunk(UNIT0["in2"] // 4 + 6, 0, w, 6 * CW)
            load_chunk(UNIT0["in2"] // 4 + 6, 4, w, 7 * CW, cols=IN2 - 7 * CW)
            w = kview("w_uq_2")
            for c in range(4):
                load_chunk(UNIT0["uq"] // 4, c, w, c * 2 * QK, units=1, cols=2 * QK)
            w = kview("w_ukv_2")
            for c in range(4):
                load_chunk(UNIT0["ukv"] // 4, c, w, c * CW, units=1, kt=2)
            square("out2", "w_out_2")
            square("xq", "w_xq_2")
            square("xo", "w_xo_2")
            ffn("ffn2", "w_gate_2", "w_up_2", "w_down_2")
            sp_.wait_ge(s_fin, 2)
            sp_.dma_start(out.rearrange("b (t p) n -> p (b t) n", p=P), x[:, :, :]).then_inc(s_out, 16)
            sp_.wait_ge(s_out, 16)
            for b in range(2):
                sp_.wait_ge(adast_free[b], 16 + 16 * 12)
                sp_.wait_ge(kvst_free[b], 16 + 16 * 4)
            sp_.wait_ge(ld["gstore"], 16)
            sp_.wait_ge(ld["toep"], 16)

        @block.gpsimd
        def _(pool):
            pool.memset(ident[:, :], 0.0).then_inc(s_id, 1)
            pool.memset(neghalf[:, :], -0.5).then_inc(s_half, 1)
            pool.wait_ge(s_id, 1)
            pool.affine_select(out=ident[:, :], in_=ident[:, :], compare_op=ALU.not_equal, fill=1.0, base=0,
                               pattern=[[-1, P]], channel_multiplier=1).then_inc(s_id, 1)
            pool.wait_ge(s_half, 1)
            pool.dma_start(parity[:, :], A["const_parity"]).then_inc(ld["parity"], 16)
            bias_rows = A["b_ada"].rearrange("d (r f) -> (d r) f", f=P)
            ada_rows = scr_ada.rearrange("c (r f) -> r c f", f=P)
            pool.dma_start(mbias[0][0:32, :], bias_rows[0:32, :]).then_inc(ld["mrow0"], 16)
            pool.dma_start(mbias[1][:, :], bias_rows[32:96, :]).then_inc(ld["mrow1"], 16)

            def power(n):
                pool.wait_ge(nt_var, n + 1)
                pool.tensor_tensor(rstd[:, :], var[:, :], neghalf[:, 0:RT], ALU.pow).then_inc(nt_rstd, 1)

            power(STAT0["mem"])
            for b in range(2):
                pool.wait_ge(adast_free[b], 16 + 16 * 4)
            pool.dma_start(mrow[0][0:32, :, :], ada_rows[0:32, :, :]).then_inc(ld["mrow0"], 16)
            power(STAT0["h1"])
            pool.wait_ge(nt_out, PAIR0["yatt"])
            pool.dma_start(dist[:, :, :], A["const_dist"].rearrange("(t p) n -> p t n", p=P)).then_inc(ld["masks"], 16)
            pool.dma_start(mult[:, :, :], A["const_mult"].rearrange("(t p) n -> p t n", p=P)).then_inc(ld["masks"], 16)
            for b in range(2):
                pool.wait_ge(adast_free[b], 16 + 16 * 12)
            pool.dma_start(mrow[1][:, :, :], ada_rows[32:96, :, :]).then_inc(ld["mrow1"], 16)
            pool.wait_ge(s_qkv, 1)
            pool.tensor_tensor(qk_rs[:, :, :].rearrange("p t h -> p (t h)"), qk_ss[:, :, :].rearrange("p t h -> p (t h)"),
                               neghalf[:, :], ALU.pow).then_inc(s_qkr, 1)
            pool.wait_ge(s_mod, 2)
            pool.dma_start(scr_gate, mrow[1][:, 0, :]).then_inc(ld["gstore"], 16)
            pool.wait_ge(nt_out, PAIR0["yatt"] + 4)
            for n, name in enumerate(("ssm_a_re", "ssm_a_im")):
                a = A[name]
                pool.dma_start(srow[32 * n:32 * n + 32, :], bass.AP(a.tensor, a.offset, [[P, 32], [1, P]]))\
                    .then_inc(ld["spar"], 16)
            pool.dma_start(dtr[64:96, :], A["ssm_log_dt"].rearrange("d (t g) -> (d t) g", g=2)).then_inc(ld["sdt"], 16)
            for n, name in enumerate(("ssm_b_re", "ssm_b_im")):
                a = A[name]
                pool.dma_start(bn[n][:, :, :], bass.AP(a.tensor, a.offset, [[GC, P], [P * GC, STILES], [1, GC]]))\
                    .then_inc(ld["sb"], 16)
            for n, name in enumerate(("ssm_c_re", "ssm_c_im")):
                a = A[name]
                pool.dma_start(cn[n][:, :, :], bass.AP(a.tensor, a.offset, [[NST, P], [P * NST, 8], [1, NST]]))\
                    .then_inc(ld["sc"], 16)
            pool.dma_start(iota[:, :], A["const_iota"]).then_inc(ld["iota"], 16)
            pool.wait_ge(ld["gstore"], 16)
            pool.wait_ge(ss_g, 8)
            pool.dma_start(gate1_b[:, :], bass.AP(scr_gate.tensor, scr_gate.offset, [[0, P], [1, D]]))\
                .then_inc(ld["gate1"], 16)
            power(STAT0["h2"])
            pool.dma_start(wide_b[:, :], bass.AP(scr_gate.tensor, scr_gate.offset + 48 * P, [[0, P], [1, D]]))\
                .then_inc(ld["gate2"], 16)
            power(STAT0["hmix"])
            pool.wait_ge(x_upd, 2 + 2 * 16)
            pool.memset(zrow[:, :], 0.0).then_inc(s_zero, 1)
            pool.wait_ge(s_zero, 1)
            pool.dma_start(zrow[:, TOEP_AT:TOEP_AT + NA_DC], A["na_rpb_2"].rearrange("d h r c -> (d h r) c"))\
                .then_inc(ld["rpb1"], 16)
            pool.wait_ge(ld["rpb1"], 16)
            pool.dma_start(scr_rpb, zrow[:, :]).then_inc(ld["rpb2"], 16)
            pool.wait_ge(ld["rpb2"], 16)
            rows = HEADS * NA_DR
            pool.dma_start(bass.AP(scr_toep.tensor, scr_toep.offset, [[GRID_W * GRID_W, rows], [GRID_W, GRID_W], [1, GRID_W]]),
                           bass.AP(scr_rpb.tensor, scr_rpb.offset + GRID_W - 1,
                                   [[TOEP_W, rows], [-1, GRID_W], [1, GRID_W]])).then_inc(ld["toep"], 16)
            pool.dma_start(colmask[:, :], A["const_colmask"]).then_inc(ld["na_const"], 16)
            pool.dma_start(ropec[:, :, :], A["const_cos"].rearrange("(t p) n -> p t n", p=P)).then_inc(ld["na_const"], 16)
            pool.dma_start(ropes[:, :, :], A["const_sin"].rearrange("(t p) n -> p t n", p=P)).then_inc(ld["na_const"], 16)
            pool.wait_ge(ld["na_const"], 48)
            pool.wait_ge(ld["toep"], 16)

            def bias_load(h):
                n, b = HEAD0["na"] + h, h % 2
                if h >= 2:
                    pool.wait_ge(at_sb, n - 1)
                for t in range(RT):
                    for r in range(2):
                        first = (h * NA_DR + NA_RMAX - 1 - 2 * t - r) * GRID_W * GRID_W
                        pool.dma_start(bias[b][GRID_W * r:GRID_W * r + GRID_W, t, :].rearrange("p (a c) -> p a c", c=GRID_W),
                                       bass.AP(scr_toep.tensor, scr_toep.offset + first,
                                               [[GRID_W, GRID_W], [GRID_W * GRID_W, NA_ROWS], [1, GRID_W]]))\
                            .then_inc(ld[f"bias{b}"], 16)

            bias_load(0)
            power(STAT0["cq"])
            power(STAT0["ckv"])
            for h in range(HEADS):
                if h + 1 < HEADS:
                    bias_load(h + 1)
                b = h % 2
                pool.wait_ge(ld[f"bias{b}"], 64 * (h // 2 + 1))
                pool.tensor_tensor(bias[b][:, :, :], bias[b][:, :, :], bcast(colmask[:, :], [0, RT], [1, S]), ALU.add)\
                    .then_inc(s_kb, 1)
            power(STAT0["yna"])
            power(STAT0["ymla"])
            pool.wait_ge(nt_out, PAIR0["hmem"])
            pool.wait_ge(at_y, 24)
            for b in range(2):
                pool.wait_ge(kvst_free[b], 16 + 16 * 4)
            pool.dma_start(xkv[:, :, :], scr_k).then_inc(ld["xk"], 16)
            pool.wait_ge(tp_done, 4 + 8)
            pool.dma_start(xkv[:, :, :], scr_v).then_inc(ld["xv"], 16)
            power(STAT0["hmem"])
            power(STAT0["hffn"])
            pool.wait_ge(nt_out, PAIR0["hffn"])
            a = A["final_norm_2"]
            pool.dma_start(wide_b[:, :], bass.AP(a.tensor, a.offset, [[0, P], [1, D]])).then_inc(ld["final"], 16)
            power(STAT0["final"])

        @block.tensor
        def _(pe):
            pe.sem_inc(used, RING)
            pe.sem_inc(ff_tp, 2)

            def split_ready(u):
                pe.wait_ge(lo_done, u + RING + 1)

            def chunk(blk, j, half_q, c, units=4, cols=CW, kt=UK, stat=sa, k0=0, before=()):
                pair = c % 2
                pe.wait_ge(acc_free[pair], 2 * (half_q + c // 2) + 2)
                for n in range(units):
                    s = (j + n) % RING
                    split_ready(4 * blk + j + n)
                    for kk in range(kt):
                        k = n * kt + kk
                        if k in before:
                            before[k]()
                        first, last = k == 0, k == units * kt - 1
                        shi, slo = stat(k0 + k)
                        for t in range(RT):
                            o = bank[2 * pair + t][:, 0:cols]
                            rows = slice(t * P, t * P + P)
                            pe.matmul(o, shi[:, rows], whi[s][:, kk, 0:cols], start=first, stop=False)
                            pe.matmul(o, shi[:, rows], wlo[s][:, kk, 0:cols], start=False, stop=False)
                            mm = pe.matmul(o, slo[:, rows], whi[s][:, kk, 0:cols], start=False, stop=last)
                    mm.then_inc(used, 1)

            def ada_chunk(blk, j, half_a, a):
                b = a % 2
                pe.wait_ge(ada_free[b], half_a + a // 2 + 1)
                for n in range(4):
                    s = (j + n) % RING
                    split_ready(4 * blk + j + n)
                    for kk in range(UK):
                        k = n * UK + kk
                        two = ccol[:, 2 * k:2 * k + P]
                        pe.matmul(bank[6 + b][:, :], two, whi[s][:, kk, :], start=(k == 0), stop=False)
                        mm = pe.matmul(bank[6 + b][:, :], two, wlo[s][:, kk, :], start=False, stop=(k == KD - 1))
                    mm.then_inc(used, 1)

            def turn_pair(name, j):
                n, stat = PAIR0[name] + j, NT[name][1]
                if stat:
                    pe.wait_ge(nt_xn, XN0[name] + j + 1)
                elif j == 0:
                    src_ready(pe, name)
                if n >= 2:
                    pe.wait_ge(nt_full, n - 1)
                for kk in range(2):
                    for t in range(RT):
                        src = xn[n % 2][:, t, kk * P:kk * P + P] if stat else NTSRC[name](t, (2 * j + kk) * P, P)
                        mm = pe.transpose(bank[4 + n % 2][:, kk * S + t * P:kk * S + t * P + P], src, ident[:, :])
                mm.then_inc(nt_tp, 1)

            def norm_turn(name):
                for j in range(NT[name][0] // 2):
                    turn_pair(name, j)

            def turn_on_the_way(pairs, ahead):
                def step(p):
                    for q, (name, m) in enumerate(pairs):
                        if q - ahead[q] == p or (p == 0 and q - ahead[q] < 0):
                            turn_pair(name, m)
                    name, m = pairs[p]
                    pe.wait_ge(nt_out, PAIR0[name] + m + 1)
                return {2 * p: (lambda p=p: step(p)) for p in range(len(pairs))}

            def eight(name):
                return turn_on_the_way([(name, m) for m in range(8)], [2] * 8)

            def turn_plain(src, pairs, n0):
                for j in range(pairs):
                    n = n0 + j
                    if n >= 2:
                        pe.wait_ge(tp_out, n - 1)
                    for kk in range(2):
                        for t in range(RT):
                            mm = pe.transpose(bank[6 + n % 2][:, kk * S + t * P:kk * S + t * P + P],
                                              src(t, (2 * j + kk) * P), ident[:, :])
                    mm.then_inc(tp_done, 1)

            def stat_ready(name):
                pe.wait_ge(nt_out, PAIR0[name] + NT[name][0] // 2)

            pe.wait_ge(s_id, 2)
            pe.wait_ge(ld["vec"], 16 * len(VECS))
            pe.transpose(bank[6][:, 0:P], vrow[:, :], ident[:, :]).then_inc(s_vec, 1)
            pe.wait_ge(s_csil, 1)
            pe.transpose(bank[7][:, 0:KD], csil[:, :], ident[0:KD, 0:KD]).then_inc(s_ct, 1)
            norm_turn("mem")
            stat_ready("mem")
            pe.wait_ge(s_ccol, 2)
            pe.wait_ge(s_vcol, 1)
            with pe.Fori(0, 2) as i:
                blk, hq, ha = UNIT0["xk_ada"] // 4 + i * 6, CHUNK0["xk_ada"] // 2 + i, i * 2
                for c in range(2):
                    for a in range(2):
                        ada_chunk(blk, 12 * c + 4 * a, ha, 2 * c + a)
                    chunk(blk, 12 * c + 8, hq, c)
            with pe.Fori(0, 2) as i:
                for c in range(2):
                    chunk(UNIT0["xv"] // 4 + i * 2, 4 * c, CHUNK0["xv"] // 2 + i, c)
            pe.wait_ge(s_mod, 1)
            for b in range(2):
                pe.wait_ge(ada_free[b], 1 + 4)
            pe.transpose(bank[6][:, 0:32], mrow[0][0:32, 0, :], ident[0:32, 0:32]).then_inc(s_modT, 1)
            norm_turn("h1")
            stat_ready("h1")
            pe.wait_ge(s_modc, 1)
            with pe.Fori(0, 4) as i:
                blk, hq, ha = UNIT0["in_ada"] // 4 + i * 6, CHUNK0["in_ada"] // 2 + i, 4 + i * 2
                for c in range(2):
                    chunk(blk, 12 * c, hq, c)
                    for a in range(2):
                        ada_chunk(blk, 12 * c + 4 + 4 * a, ha, 2 * c + a)
            pe.wait_ge(s_mod, 2)
            for b in range(2):
                pe.wait_ge(ada_free[b], 1 + 12)
            pe.transpose(bank[6][:, 0:64], mrow[1][:, 0, :], ident[0:64, 0:64]).then_inc(s_modT, 1)
            pe.wait_ge(s_modc, 2)
            chunks_out(pe, CHUNK0["glu"])
            turn_plain(lambda t, c: proj[:, t, c:c + P], 4, 0)
            pe.wait_ge(tp_out, 4)

            def head_turn(kind, n):
                b, h = n % 2, n - HEAD0[kind]
                if kind == "cross":
                    pe.wait_ge(at_qk, n)
                elif n >= 2:
                    pe.wait_ge(at_qk, n - 1)
                if kind == "mla":
                    if h >= 2:
                        pe.wait_ge(at_rope, h - 1)
                    pe.wait_ge(at_y, n - 3 if h >= 2 else HEAD0["mla"])
                if kind == "cross":
                    for kt in range(XKT):
                        for t in range(RT):
                            mm = pe.transpose(bank[kt // 2][:, kt % 2 * S + t * P:kt % 2 * S + t * P + P],
                                              xq[:, t, h * XHD + kt * P:h * XHD + kt * P + P], ident[:, :])
                    mm.then_inc(at_t, 1)
                    return
                for w, src in enumerate(QKSRC[kind]):
                    for t in range(RT):
                        mm = pe.transpose(bank[b][:, w * S + t * P:w * S + t * P + P], src(t, h), ident[:, :])
                if kind == "mla":
                    for t in range(RT):
                        mm = pe.transpose(bank[6 + b][0:ROPE, (2 + t) * P:(3 + t) * P],
                                          q_mla[:, t, h, NOPE:QK], ident[:, :])
                mm.then_inc(at_t, 1)

            def head_scores(kind, n):
                b, h = n % 2, n - HEAD0[kind]
                pe.wait_ge(at_qk, n + 1)
                if kind == "mla":
                    pe.wait_ge(at_rope, h + 1)
                if n >= 2:
                    pe.wait_ge(at_e, n - 1)
                for t in range(RT):
                    rows = slice(t * P, t * P + P)
                    o = bank[2 + b][:, t * S:t * S + S]
                    if kind == "cross":
                        for kt in range(XKT):
                            mm = pe.matmul(o, xqT[:, kt, rows], xkT[:, h * XKT + kt, :], start=(kt == 0),
                                           stop=(kt == XKT - 1))
                    else:
                        mm = pe.matmul(o, qkT[b][:, 0, rows], qkT[b][:, 1, :], start=True, stop=(kind != "mla"))
                        if kind == "mla":
                            mm = pe.matmul(o, rT[b][:, rows], krT[:, :], start=False, stop=True)
                mm.then_inc(at_s, 1)

            def head_turn_p(kind, n):
                b = n % 2
                if kind == "dil":
                    pe.wait_ge(at_pm, n + 1)
                else:
                    pe.wait_ge(at_e, n + 1)
                if n >= 2:
                    pe.wait_ge(at_pc, n - 1)
                for t in range(RT):
                    for kt in range(RT):
                        mm = pe.transpose(bank[4 + b][:, kt * S + t * P:kt * S + t * P + P],
                                          sp[b][:, t, kt * P:kt * P + P], ident[:, :])
                mm.then_inc(at_pt, 1)

            def head_values(kind, n):
                b, h = n % 2, n - HEAD0[kind]
                pe.wait_ge(at_pc, n + 1)
                if kind == "cross":
                    pe.wait_ge(at_y, n)
                elif n >= 2:
                    pe.wait_ge(at_y, n - 1)
                if kind == "mla":
                    pe.wait_ge(at_rope, min(h + 3, HEADS))
                for t in range(RT):
                    o = bank[6 + t][:, :] if kind == "cross" else bank[6 + b][:, t * P:t * P + P]
                    for kt in range(RT):
                        mm = pe.matmul(o, pT[b][:, kt, t * P:t * P + P], VSRC[kind](kt, h), start=(kt == 0),
                                       stop=(kt == RT - 1))
                mm.then_inc(at_o, 1)

            def attend(kind):
                ns = heads(kind)
                head_turn(kind, ns[0])
                head_scores(kind, ns[0])
                head_turn(kind, ns[1])
                for n in ns:
                    if n + 1 in ns:
                        head_scores(kind, n + 1)
                    if n + 2 in ns:
                        head_turn(kind, n + 2)
                    head_turn_p(kind, n)
                    if n > ns[0]:
                        head_values(kind, n - 1)
                head_values(kind, ns[-1])
                pe.wait_ge(at_y, ns[-1] + 1)

            pe.wait_ge(s_qkn, 1)
            attend("dil")
            norm_turn("yatt")

            pe.wait_ge(nt_full, PAIR0["h2"])
            pe.wait_ge(ss_par, 1)
            pe.transpose(bank[6][:, 0:96], srow[:, :], ident[0:96, 0:96]).then_inc(ss_parT, 1)
            for m in range(8):
                src, n = (bb, m // 2) if m < 4 else (cc, (m - 4) // 2)
                pe.wait_ge(ss_bb, n + 1 if m < 4 else n + 3)
                if m >= 2:
                    pe.wait_ge(ss_btc, m - 1)
                for q in range(4):
                    k = 4 * (m % 2) + q
                    s = bb[n][:, 4 * k:4 * k + 4, :] if m < 4 else cc[n][:, k, :]
                    mm = pe.transpose(bank[4 + m % 2][:, q * P:q * P + P], s, ident[:, :])
                mm.then_inc(ss_btp, 1)
            pe.wait_ge(ss_btc, 8)

            def drive(j):
                k, q = j // 4, j % 4
                if j >= 4:
                    pe.wait_ge(ss_d, 12 * (j - 4) + 4)
                rows = slice(32 * q, 32 * q + 32)
                for c in range(2):
                    mm = pe.matmul(bank[q][:, c * S:c * S + S], bt[c][rows, k, :], uT[rows, k, :], start=True, stop=True)
                mm.then_inc(ss_bu, 1)

            def readout(j):
                k, q = j // 4, j % 4
                pe.wait_ge(ss_d, 12 * j + 12)
                if k >= 2 and q == 0:
                    pe.wait_ge(ss_yt, k - 1)
                o = bank[4 + k % 2][32 * q:32 * q + 32, 0:S]
                for m in range(4):
                    mm = pe.matmul(o, ct[m // 2][:, k, 32 * q:32 * q + 32], prod[:, m, :], start=(m == 0), stop=(m == 3))
                mm.then_inc(ss_y, 1)

            drive(0)
            for j in range(STILES):
                if j + 1 < STILES:
                    drive(j + 1)
                readout(j)

            pe.wait_ge(ss_g, 8)
            for c in range(2):
                pe.wait_ge(acc_free[c], 2 * (CHUNK0["glu"] // 2) + 2)
                split_ready(UNIT0["glu"] + 2 * c + 1)
                for m in range(4):
                    o = bank[2 * c + m // 2][:, m % 2 * S:m % 2 * S + S]
                    cols = slice(m * P, m * P + P)
                    for k in range(8):
                        s, kk = 2 * c + k // UK, k % UK
                        pe.matmul(o, whi[s][:, kk, cols], sa_hi[:, k, :], start=(k == 0), stop=False)
                        pe.matmul(o, whi[s][:, kk, cols], sa_lo[:, k, :], start=False, stop=False)
                        mm = pe.matmul(o, wlo[s][:, kk, cols], sa_hi[:, k, :], start=False, stop=(k == 7))
                mm.then_inc(used, 2)

            def square(stage, stat=sa, before=()):
                for c in range(4):
                    chunk(UNIT0[stage] // 4, 4 * c, CHUNK0[stage] // 2, c, stat=stat, before=() if c else before)

            def ffn(stage, f0, norm):
                blk, hq = UNIT0[stage] // 4, CHUNK0[stage] // 2

                def turn_hidden(f, free):
                    pe.wait_ge(acc_free[1], free)
                    for hf in range(2):
                        pe.wait_ge(ff_lo, 2 * f + hf + 1)
                        for kk in range(2):
                            for t in range(RT):
                                mm = pe.transpose(bank[4 + hf][:, kk * S + t * P:kk * S + t * P + P],
                                                  fg[:, t, (2 * hf + kk) * P:(2 * hf + kk) * P + P], ident[:, :])
                        mm.then_inc(ff_tp, 1)

                for c0, n in THIRDS:
                    chunk(blk, 0, hq, 0, before=() if c0 else eight(norm))
                    chunk(blk, 4, hq, 1)
                    with pe.Fori(1, n) as i:
                        chunk(blk + i * 2, 0, hq + i, 0)
                        turn_hidden(i + (f0 + c0 - 1), 2 * (hq + i) + 2)
                        chunk(blk + i * 2, 4, hq + i, 1)
                    blk, hq, f_end = blk + 2 * n, hq + n, f0 + c0 + n
                    def acts(k):
                        return act_hi[:, k, :], act_lo[:, k, :]
                    on_the_way = {UK: lambda: turn_hidden(f_end - 1, 2 * hq + 2),
                                  UK * (n - 1): lambda: pe.wait_ge(ff_lo, 2 * f_end + 2)}
                    pe.wait_ge(ff_lo, 2 * f_end)
                    for c in range(4):
                        chunk(blk, n * c, hq, c, units=n, stat=acts, before=() if c else on_the_way)
                    blk, hq = blk + n, hq + 2

            pe.wait_ge(gl_y2, 2)
            square("out1", lambda k: (y2_hi[:, k, :], y2_lo[:, k, :]) if k < 8 else sa(k))
            ffn("ffn1", 0, "h2")
            chunk(UNIT0["in2"] // 4, 0, CHUNK0["in2"] // 2, 0, before=eight("hmix"))
            chunk(UNIT0["in2"] // 4, 4, CHUNK0["in2"] // 2, 1)
            with pe.Fori(1, 3) as i:
                for c in range(2):
                    chunk(UNIT0["in2"] // 4 + i * 2, 4 * c, CHUNK0["in2"] // 2 + i, c)
            chunk(UNIT0["in2"] // 4 + 6, 0, CHUNK0["in2"] // 2 + 3, 0)
            chunk(UNIT0["in2"] // 4 + 6, 4, CHUNK0["in2"] // 2 + 3, 1, cols=IN2 - 7 * CW)
            norm_turn("cq")
            norm_turn("ckv")
            stat_ready("ckv")
            for c in range(4):
                chunk(UNIT0["uq"] // 4, c, CHUNK0["uq"] // 2, c, units=1, cols=2 * QK)
            chunks_out(pe, CHUNK0["ukv"])
            attend("na")
            for c in range(4):
                chunk(UNIT0["ukv"] // 4, c, CHUNK0["ukv"] // 2, c, units=1, kt=2, k0=4)
            chunks_out(pe, CHUNK0["out2"])
            pe.wait_ge(s_kr, 1)
            for t in range(RT):
                mm = pe.transpose(bank[7][0:ROPE, (2 + t) * P:(3 + t) * P], kr[:, t, :], ident[:, :])
            mm.then_inc(s_krt, 1)
            pe.wait_ge(s_krT, 1)
            attend("mla")
            square("out2", before=turn_on_the_way([(name, m) for name in ("yna", "ymla") for m in range(4)],
                                                  [2, 2, 2, 2, 1, 1, 2, 2]))
            pe.wait_ge(ld["xk"], 16)
            turn_plain(lambda t, c: xkv[:, t, c:c + P], 8, 4)
            square("xq", before=eight("hmem"))
            pe.wait_ge(tp_out, 12)
            chunks_out(pe, CHUNK0["xo"])
            pe.wait_ge(ld["xv"], 16)
            attend("cross")
            square("xo", before=eight("ocross"))
            ffn("ffn2", FCH, "hffn")

        @block.scalar
        def _(act):
            for b in range(2):
                act.sem_inc(ada_free[b], 1)
                act.sem_inc(adast_free[b], 16)
                act.sem_inc(kvst_free[b], 16)

            def pump(blk, j):
                j += LOOKAHEAD
                s, blk = j % RING, blk + j // RING
                if isinstance(blk, int) and RING * blk + s >= UNITS:
                    return
                act.wait_ge(landed[s], 16 * blk + 16)
                act.wait_ge(used, RING * blk + s + 1)
                act.activation(whi[s][:, :, :], raw[s][:, :, :], ACT.Copy).then_inc(hi_done, 1)

            def pumps(blk, j, n):
                for m in range(n):
                    pump(blk, j + m)

            def unit_used(blk, j):
                act.wait_ge(used, RING + 4 * blk + j + 1)

            def norm_turn(name):
                k_tiles, stat = NT[name]
                s, p0 = STAT0[name], PAIR0[name]
                width = k_tiles * P
                if stat:
                    norm_squares(name, s, p0, width)
                for j in range(k_tiles // 2):
                    n, b = p0 + j, (p0 + j) % 2
                    act.wait_ge(nt_tp, n + 1)
                    if n >= 2:
                        act.wait_ge(nt_out, n - 1)
                    if name in ("yatt", "ocross"):
                        act.activation(full[b][:, :, :], bank[4 + b][:, :].rearrange("p (k s) -> p k s", k=2), ACT.Copy)\
                            .then_inc(nt_full, 1)
                        continue
                    for kk in range(2):
                        k = 2 * j + kk
                        o, i = full[b][:, kk, :], bank[4 + b][:, kk * S:kk * S + S]
                        if name in ("h1", "h2"):
                            m, shift = (0, 0) if name == "h1" else (1, 48)
                            ins = act.activation(o, i, ACT.Identity, scale=scol[m][:, k:k + 1],
                                                 bias=modc[:, shift + k:shift + k + 1])
                        else:
                            ins = act.activation(o, i, ACT.Copy, scale=vec(NTSCALE[name], k))
                    ins.then_inc(nt_full, 1)

            def norm_squares(name, s, p0, width):
                src_ready(act, name)
                if p0:
                    act.wait_ge(nt_out, p0)
                    act.wait_ge(nt_tp, p0)
                if s:
                    act.wait_ge(nt_var, s)
                src, o = NTSRC[name](0, 0, width), junk[:, 0, 0:width]
                if name == "ymla":
                    o = o.rearrange("p (a b) -> p a b", b=VD)
                act.activation(o, src, ACT.Square, accum_out=ss[:, 0:1]).then_inc(nt_sq[0], 1)

            def copy_out(blk, j, c, dst, cols=CW):
                unit_used(blk, j)
                act.activation(dst, bank[2 * (c % 2)][:, 0:cols], ACT.Copy).then_inc(acc_free[c % 2], 1)

            act.wait_ge(ld["c"], 16)
            act.activation(csil[:, :], crow[:, :], ACT.Silu).then_inc(s_csil, 1)
            act.wait_ge(s_vcol, 1)
            norm_turn("mem")
            pumps(0, -LOOKAHEAD, LOOKAHEAD)

            def ada_out(blk, j, half_a, a, col):
                b = a % 2
                unit_used(blk, j)
                act.wait_ge(adast_free[b], 16 * (half_a + a // 2 + 1))
                act.activation(adast[b][:, :], bank[6 + b][0:2, :], ACT.Copy).then_inc(ada_free[b], 1)
                act.wait_ge(ada_free[b], half_a + a // 2 + 2)
                act.dma_start(scr_ada[:, bass.ds(col, CW)], adast[b][:, :]).then_inc(adast_free[b], 16)

            def kv_out(blk, j, hq, c, scr, col):
                act.wait_ge(kvst_free[c], 16 * hq + 16)
                copy_out(blk, j, c, kvst[c][:, 0, :])
                act.wait_ge(acc_free[c], 2 * hq + 4)
                act.dma_start(scr[:, :, bass.ds(col, CW)], kvst[c][:, :, :]).then_inc(kvst_free[c], 16)

            with act.Fori(0, 2) as i:
                blk, hq, ha = UNIT0["xk_ada"] // 4 + i * 6, CHUNK0["xk_ada"] // 2 + i, i * 2
                for c in range(2):
                    for a in range(2):
                        pumps(blk, 12 * c + 4 * a, 4)
                        ada_out(blk, 12 * c + 4 * a + 3, ha, 2 * c + a, i * (4 * CW) + (2 * c + a) * CW)
                    pumps(blk, 12 * c + 8, 4)
                    kv_out(blk, 12 * c + 11, hq, c, scr_k, i * (2 * CW) + c * CW)
            with act.Fori(0, 2) as i:
                blk, hq = UNIT0["xv"] // 4 + i * 2, CHUNK0["xv"] // 2 + i
                for c in range(2):
                    pumps(blk, 4 * c, 4)
                    kv_out(blk, 4 * c + 3, hq, c, scr_v, i * (2 * CW) + c * CW)
            act.wait_ge(s_modc, 1)
            norm_turn("h1")
            for b in range(2):
                act.wait_ge(kvst_free[b], 16 + 16 * 4)
            with act.Fori(0, 4) as i:
                blk, hq, ha = UNIT0["in_ada"] // 4 + i * 6, CHUNK0["in_ada"] // 2 + i, 4 + i * 2
                for c in range(2):
                    pumps(blk, 12 * c, 4)
                    copy_out(blk, 12 * c + 3, c, proj[:, 0, bass.ds(i * (2 * CW) + c * CW, CW)])
                    for a in range(2):
                        pumps(blk, 12 * c + 4 + 4 * a, 4)
                        ada_out(blk, 12 * c + 7 + 4 * a, ha, 2 * c + a, i * (4 * CW) + (8 + 2 * c + a) * CW)

            def turn_plain(pairs, n0, dst):
                for j in range(pairs):
                    n = n0 + j
                    act.wait_ge(tp_done, n + 1)
                    act.activation(dst[:, 2 * j:2 * j + 2, :], bank[6 + n % 2][:, :].rearrange("p (k s) -> p k s", k=2),
                                   ACT.Copy).then_inc(tp_out, 1)

            turn_plain(4, 0, uT)
            def head_in(kind, n):
                b = n % 2
                act.wait_ge(at_t, n + 1)
                if kind == "cross":
                    act.wait_ge(at_s, n)
                    act.activation(xqT[:, 0:2, :], bank[0][:, :].rearrange("p (k s) -> p k s", k=2), ACT.Copy)
                    act.activation(xqT[:, 2:4, :], bank[1][:, :].rearrange("p (k s) -> p k s", k=2), ACT.Copy)\
                        .then_inc(at_qk, 1)
                    return
                if n >= 2:
                    act.wait_ge(at_s, n - 1)
                if kind == "dil":
                    act.activation(qkT[b][:, 0, :], bank[b][:, 0:S], ACT.Copy, scale=qscol[:, :])
                    act.activation(qkT[b][:, 1, :], bank[b][:, S:2 * S], ACT.Copy).then_inc(at_qk, 1)
                else:
                    act.activation(qkT[b][:, :, :], bank[b][:, :].rearrange("p (k s) -> p k s", k=2), ACT.Copy)\
                        .then_inc(at_qk, 1)

            def head_exp(kind, n):
                b = n % 2
                act.wait_ge(at_m, n + 1)
                if n >= 2:
                    act.wait_ge(at_pt, n - 1)
                    act.wait_ge(at_r, n - 1)
                for t in range(RT):
                    src = sp[b][:, t, :] if kind in ("dil", "na") else bank[2 + b][:, t * S:t * S + S]
                    scale = {"mla": QK ** -0.5, "cross": XHD ** -0.5}.get(kind, 1.0)
                    acc = {} if kind == "dil" else dict(accum_out=rsum[:, b, t:t + 1])
                    ins = act.activation(sp[b][:, t, :], src, ACT.Exp, bias=negm[:, b, t:t + 1], scale=scale, **acc)
                ins.then_inc(at_e, 1)

            def head_out(kind, n):
                b, h = n % 2, n - HEAD0[kind]
                act.wait_ge(at_r, n + 1)
                act.wait_ge(at_o, n + 1)
                for t in range(RT):
                    o = bank[6 + t][:, :] if kind == "cross" else bank[6 + b][:, t * P:t * P + P]
                    ins = act.activation(YDST[kind](t, h), o, ACT.Copy, scale=rden[:, b, t:t + 1])
                ins.then_inc(at_y, 1)

            def attend(kind):
                ns = heads(kind)
                head_in(kind, ns[0])
                head_in(kind, ns[1])
                head_exp(kind, ns[0])
                for n in ns:
                    if n + 2 in ns:
                        head_in(kind, n + 2)
                    if n + 1 in ns:
                        head_exp(kind, n + 1)
                    if n > ns[0]:
                        head_out(kind, n - 1)
                head_out(kind, ns[-1])

            act.wait_ge(s_qkn, 1)
            attend("dil")
            norm_turn("yatt")
            def p_(name):
                return par[:, PAR[name], :]
            act.wait_ge(ss_pc, 1)
            act.activation(p_("dt"), scolp[:, 64:96], ACT.Exp).then_inc(ss_exp, 1)
            act.wait_ge(ss_trig, 1)
            act.activation(p_("mag"), p_("ard"), ACT.Exp).then_inc(ss_exp, 1)
            act.wait_ge(ss_trig, 2)
            act.activation(p_("sin"), p_("r"), ACT.Sin)
            act.activation(p_("sh"), p_("r"), ACT.Sin, scale=0.5).then_inc(ss_exp, 1)
            act.wait_ge(ss_exp, 3)
            act.activation(p_("sh2"), p_("sh"), ACT.Square).then_inc(ss_exp, 1)
            for m in range(8):
                act.wait_ge(ss_btp, m + 1)
                dst = (bt if m < 4 else ct)[(m % 4) // 2]
                act.activation(dst[:, 4 * (m % 2):4 * (m % 2) + 4, :],
                               bank[4 + m % 2][:, :].rearrange("p (k s) -> p k s", k=4), ACT.Copy).then_inc(ss_btc, 1)

            def sines(k):
                act.wait_ge(ss_ang, k + 1)
                if k:
                    act.wait_ge(ss_d, 48 * k)
                act.activation(si[:, :, :], turn[:, :, :], ACT.Sin, scale=6.283185)
                act.activation(half[:, :, :], turn[:, :, :], ACT.Sin, scale=3.1415925).then_inc(ss_sin, 1)
                act.wait_ge(ss_sin, 2 * k + 1)
                act.activation(half[:, :, :], half[:, :, :], ACT.Square).then_inc(ss_sin, 1)

            for k in range(8):
                sines(k)
                act.wait_ge(ss_yt, k + 1)
                act.activation(gt[:, :], yt[:, :], ACT.Gelu_apprx_tanh).then_inc(ss_gt, 1)

            blk = UNIT0["glu"] // 4
            for c in range(2):
                pumps(blk, 2 * c, 2)
                act.wait_ge(used, RING + 4 * blk + 2 * c + 2)
                for m in range(2):
                    act.activation(sig[:, 4 * c + 2 * m:4 * c + 2 * m + 2, :],
                                   bank[2 * c + m][:, :].rearrange("p (k s) -> p k s", k=2), ACT.Sigmoid)\
                        .then_inc(acc_free[c], 1)

            def pump_square(stage):
                with act.Fori(0, 2) as i:
                    pumps(UNIT0[stage] // 4 + i * 2, 0, 8)

            def silu_gate(blk):
                unit_used(blk, 3)
                for t in range(RT):
                    act.activation(fg[:, t, :], bank[t][:, :], ACT.Silu).then_inc(acc_free[0], 1)

            def hidden_heads(f, k):
                for hf in range(2):
                    act.wait_ge(ff_tp, 2 * f + hf + 3)
                    act.activation(act_hi[:, bass.ds(k + 2 * hf, 2), :],
                                   bank[4 + hf][:, :].rearrange("p (k s) -> p k s", k=2), ACT.Copy).then_inc(ff_hi, 1)

            def ffn(stage, f0):
                blk, hq = UNIT0[stage] // 4, CHUNK0[stage] // 2
                for c0, n in THIRDS:
                    pumps(blk, 0, 4)
                    silu_gate(blk)
                    pumps(blk, 4, 4)
                    with act.Fori(1, n) as i:
                        pumps(blk + i * 2, 0, 4)
                        hidden_heads(i + (f0 + c0 - 1), i * 4 - 4)
                        silu_gate(blk + i * 2)
                        pumps(blk + i * 2, 4, 4)
                    blk, hq = blk + 2 * n, hq + n
                    pumps(blk, 0, 1)
                    hidden_heads(f0 + c0 + n - 1, 4 * n - 4)
                    pumps(blk, 1, 4 * n - 1)
                    blk += n

            pump_square("out1")
            norm_turn("h2")
            ffn("ffn1", 0)
            norm_turn("hmix")
            with act.Fori(0, 3) as i:
                for c in range(2):
                    blk = UNIT0["in2"] // 4 + i * 2
                    pumps(blk, 4 * c, 4)
                    copy_out(blk, 4 * c + 3, c, proj2[:, 0, bass.ds(i * (2 * CW) + c * CW, CW)])
            blk = UNIT0["in2"] // 4 + 6
            for c in range(2):
                cols = (CW, IN2 - 7 * CW)[c]
                pumps(blk, 4 * c, 4)
                copy_out(blk, 4 * c + 3, c, proj2[:, 0, (6 + c) * CW:(6 + c) * CW + cols], cols)
            norm_turn("cq")
            norm_turn("ckv")
            for c in range(4):
                pumps(UNIT0["uq"] // 4, c, 1)
                copy_out(UNIT0["uq"] // 4, c, c, q_mla[:, 0, 2 * c:2 * c + 2, :].rearrange("p a b -> p (a b)"), 2 * QK)
            attend("na")
            for c in range(4):
                pumps(UNIT0["ukv"] // 4, c, 1)
                copy_out(UNIT0["ukv"] // 4, c, c, proj2[:, 0, NA_W + c * CW:NA_W + c * CW + CW])
            act.wait_ge(s_krT, 1)
            attend("mla")
            norm_turn("yna")
            norm_turn("ymla")
            pump_square("out2")
            turn_plain(8, 4, xkT)
            norm_turn("hmem")
            with act.Fori(0, 2) as i:
                for c in range(2):
                    blk = UNIT0["xq"] // 4 + i * 2
                    pumps(blk, 4 * c, 4)
                    copy_out(blk, 4 * c + 3, c, xq[:, 0, bass.ds(i * (2 * CW) + c * CW, CW)])
            attend("cross")
            norm_turn("ocross")
            pump_square("xo")
            norm_turn("hffn")
            ffn("ffn2", FCH)
            norm_squares("final", STAT0["final"], PAIR0["hffn"] + 8, D)

        @block.vector
        def _(dve):
            dve.sem_inc(lo_done, RING)
            dve.sem_inc(x_upd, 2)
            dve.sem_inc(ff_lo, 2)
            for p in range(2):
                dve.sem_inc(acc_free[p], 2)
            linked = [0]

            def link(ins):
                linked[0] += 1
                ins.then_inc(link_dve, 1)
                dve.wait_ge(link_dve, linked[0])

            def pump(blk, j):
                j += LOOKAHEAD
                s, blk = j % RING, blk + j // RING
                if isinstance(blk, int) and RING * blk + s >= UNITS:
                    return
                dve.wait_ge(hi_done, RING * blk + s + 1)
                dve.wait_ge(used, RING * blk + s + 1)
                dve.tensor_tensor(wlo[s][:, :, :], raw[s][:, :, :], whi[s][:, :, :].bitcast(F32), ALU.subtract)\
                    .then_inc(lo_done, 1)

            def pumps(blk, j, n):
                for m in range(n):
                    pump(blk, j + m)

            def unit_used(blk, j):
                dve.wait_ge(used, RING + 4 * blk + j + 1)

            def stats(name, s, p0, width):
                src_ready(dve, name)
                if p0:
                    dve.wait_ge(nt_out, p0)
                    dve.wait_ge(nt_tp, p0)
                if s:
                    dve.wait_ge(nt_var, s)
                src, o = NTSRC[name](1, 0, width), junk[:, 1, 0:width]
                if name == "ymla":
                    o = o.rearrange("p (a b) -> p a b", b=VD)
                dve.tensor_tensor_reduce(o, src, src, 1.0, 0.0, ALU.mult, ALU.add, ss[:, 1:2]).then_inc(nt_sq[1], 1)
                for t in range(RT):
                    dve.wait_ge(nt_sq[t], s + 1)
                if s:
                    dve.wait_ge(nt_rstd, s)
                dve.tensor_scalar(var[:, :], ss[:, :], 1.0 / width, EPS, ALU.mult, ALU.add).then_inc(nt_var, 1)
                dve.wait_ge(nt_rstd, s + 1)

            def norm_turn(name, units_used):
                k_tiles, stat = NT[name]
                pairs, p0 = k_tiles // 2, PAIR0[name]
                if stat:
                    stats(name, STAT0[name], p0, k_tiles * P)

                def normed(j):
                    n = p0 + j
                    if n >= 2:
                        dve.wait_ge(nt_tp, n - 1)
                    for t in range(RT):
                        src, o = NTSRC[name](t, 2 * j * P, 2 * P), xn[n % 2][:, t, :]
                        if name == "ymla":
                            o = o.rearrange("p (a b) -> p a b", b=VD)
                        ins = dve.tensor_scalar(o, src, rstd[:, t:t + 1], None, ALU.mult)
                    ins.then_inc(nt_xn, 1)

                if stat:
                    normed(0)
                    if pairs > 1:
                        normed(1)
                if units_used:
                    dve.wait_ge(used, RING + units_used)
                k0 = NTK0.get(name, 0)
                for j in range(pairs):
                    n, b, k = p0 + j, (p0 + j) % 2, k0 + 2 * j
                    hi, lo = (sa_hi, sa_lo) if k < 8 else (s2_hi, s2_lo)
                    k %= 8
                    dve.wait_ge(nt_full, n + 1)
                    dve.tensor_copy(hi[:, k:k + 2, :], full[b][:, :, :]).then_inc(nt_hi, 1)
                    if stat and j + 2 < pairs:
                        normed(j + 2)
                    dve.wait_ge(nt_hi, n + 1)
                    dve.tensor_tensor(lo[:, k:k + 2, :], full[b][:, :, :], hi[:, k:k + 2, :].bitcast(F32), ALU.subtract)\
                        .then_inc(nt_out, 1)

            def copy_out(blk, j, c, dst, cols=CW):
                unit_used(blk, j)
                dve.tensor_copy(dst, bank[2 * (c % 2) + 1][:, 0:cols]).then_inc(acc_free[c % 2], 1)

            def add_out(blk, j, hq, c, col):
                unit_used(blk, j)
                dve.wait_ge(acc_free[c % 2], 2 * (hq + c // 2) + 2)
                for t in range(RT):
                    xs = x[:, t, bass.ds(col, CW)]
                    dve.tensor_tensor(xs, bank[2 * (c % 2) + t][:, :], xs, ALU.add).then_inc(acc_free[c % 2], 1)

            def gated_out(blk, j, hq, c, col, gate, g):
                unit_used(blk, j)
                for t in range(RT):
                    dve.wait_ge(x_upd, 2 * g + t + 1)
                    dve.tensor_tensor(rtmp[:, t, :], bank[2 * (c % 2) + t][:, :], gate[:, bass.ds(col, CW)], ALU.mult)\
                        .then_inc(acc_free[c % 2], 1)
                for t in range(RT):
                    dve.wait_ge(acc_free[c % 2], 2 * (hq + c // 2) + 3 + t)
                    xs = x[:, t, bass.ds(col, CW)]
                    dve.tensor_tensor(xs, rtmp[:, t, :], xs, ALU.add).then_inc(x_upd, 1)

            dve.wait_ge(s_vec, 1)
            dve.tensor_copy(vcol[:, :], bank[6][:, 0:P]).then_inc(s_vcol, 1)
            dve.wait_ge(s_ct, 1)
            dve.tensor_copy(cT[:, :], bank[7][:, 0:KD]).then_inc(s_cT, 1)
            dve.wait_ge(s_cT, 1)
            pairs_ = ccol[:, 0:2 * KD].rearrange("p (k c) -> p k c", c=2)
            dve.memset(ccol[:, 2 * KD:2 * KD + P].bitcast(F32), 0.0)
            dve.tensor_copy(pairs_[:, :, 0], cT[:, :]).then_inc(s_ccol, 1)
            dve.wait_ge(s_ccol, 1)
            dve.tensor_tensor(pairs_[:, :, 1], cT[:, :], pairs_[:, :, 0].bitcast(F32), ALU.subtract).then_inc(s_ccol, 1)
            dve.wait_ge(s_vcol, 1)
            link(dve.tensor_tensor(qscol[:, :], vec("q_norm_w"), vec("k_norm_w"), ALU.mult))
            link(dve.tensor_scalar(qscol[:, :], qscol[:, :], HD ** -0.5, None, ALU.mult))
            norm_turn("mem", 0)
            pumps(0, -LOOKAHEAD, LOOKAHEAD)
            with dve.Fori(0, 2) as i:
                blk, hq = UNIT0["xk_ada"] // 4 + i * 6, CHUNK0["xk_ada"] // 2 + i
                for c in range(2):
                    pumps(blk, 12 * c, 12)
                    dve.wait_ge(kvst_free[c], 16 * hq + 16)
                    copy_out(blk, 12 * c + 11, c, kvst[c][:, 1, :])
            with dve.Fori(0, 2) as i:
                blk, hq = UNIT0["xv"] // 4 + i * 2, CHUNK0["xv"] // 2 + i
                for c in range(2):
                    pumps(blk, 4 * c, 4)
                    dve.wait_ge(kvst_free[c], 16 * hq + 16)
                    copy_out(blk, 4 * c + 3, c, kvst[c][:, 1, :])

            def modulation(m, rows):
                dve.wait_ge(ld[f"mrow{m}"], 32)
                link(dve.tensor_tensor(mrow[m][0:rows, 0, :], mrow[m][0:rows, 0, :], mrow[m][0:rows, 1, :], ALU.add))
                dve.tensor_tensor(mrow[m][0:rows, 0, :], mrow[m][0:rows, 0, :], mbias[m][0:rows, :], ALU.add)\
                    .then_inc(s_mod, 1)
                dve.wait_ge(s_modT, m + 1)
                link(dve.tensor_copy(modc[:, 32 * m:32 * m + rows], bank[6][:, 0:rows]))
                at_ = (KD, 32 + 2 * KD)[m]
                link(dve.tensor_scalar(scol[m][:, :], modc[:, at_:at_ + KD], 1.0, None, ALU.add))
                name = ("norm1_w", "norm2_w")[m]
                dve.tensor_tensor(scol[m][:, :], scol[m][:, :], vcol[:, VAT[name]:VAT[name] + KD], ALU.mult)\
                    .then_inc(s_modc, 1)

            modulation(0, 32)
            norm_turn("h1", UNIT0["in_ada"])
            for b in range(2):
                dve.wait_ge(kvst_free[b], 16 + 16 * 4)
            with dve.Fori(0, 4) as i:
                blk = UNIT0["in_ada"] // 4 + i * 6
                for c in range(2):
                    pumps(blk, 12 * c, 4)
                    copy_out(blk, 12 * c + 3, c, proj[:, 1, bass.ds(i * (2 * CW) + c * CW, CW)])
                    pumps(blk, 12 * c + 4, 8)
            modulation(1, 64)
            chunks_out(dve, CHUNK0["glu"])
            dve.wait_ge(used, RING + UNIT0["glu"])
            for t in range(RT):
                for half_ in range(2):
                    cols = slice(SSM_W * (1 + half_), SSM_W * (2 + half_))
                    link(dve.tensor_tensor(sqs[:, :], proj[:, t, cols], proj[:, t, cols], ALU.mult))
                    link(dve.tensor_reduce(qk_ss[:, t, 8 * half_:8 * half_ + 8],
                                           sqs[:, :].rearrange("p (h e) -> p h e", e=HD), AX.X, ALU.add))
            dve.tensor_scalar(qk_ss[:, :, :], qk_ss[:, :, :], 1.0 / HD, EPS, ALU.mult, ALU.add).then_inc(s_qkv, 1)
            dve.wait_ge(s_qkr, 1)
            for t in range(RT):
                qk = proj[:, t, SSM_W:3 * SSM_W].rearrange("p (h e) -> p h e", e=HD)
                ins = dve.tensor_tensor(qk, qk, bcast(qk_rs[:, t, :], [1, 2 * HEADS], [0, HD]), ALU.mult)
            ins.then_inc(s_qkn, 1)
            dve.wait_ge(ld["masks"], 32)

            def head_max(kind, n):
                b, h = n % 2, n - HEAD0[kind]
                dve.wait_ge(at_s, n + 1)
                scores = bank[2 + b][:, :]
                if n >= 2:
                    dve.wait_ge(at_pt, n - 1)
                    dve.wait_ge(at_e, n - 1)
                flat = sp[b][:, :, :].rearrange("p t s -> p (t s)")
                if kind == "dil":
                    dve.scalar_tensor_tensor(out=flat, in0=dist[:, :, :].rearrange("p t s -> p (t s)"),
                                             scalar=-(2.0 ** -(h + 1)), in1=scores, op0=ALU.mult, op1=ALU.add)\
                        .then_inc(at_sb, 1)
                    dve.wait_ge(at_sb, n + 1)
                    scores = flat
                elif kind == "na":
                    dve.wait_ge(s_kb, h + 1)
                    dve.scalar_tensor_tensor(out=flat, in0=scores, scalar=HD ** -0.5,
                                             in1=bias[b][:, :, :].rearrange("p t s -> p (t s)"), op0=ALU.mult, op1=ALU.add)\
                        .then_inc(at_sb, 1)
                    dve.wait_ge(at_sb, n + 1)
                    scores = flat
                dve.tensor_reduce(mx[:, b, :], scores.rearrange("p (t s) -> p t s", t=RT), AX.X, ALU.max)\
                    .then_inc(at_mx, 1)
                dve.wait_ge(at_mx, n + 1)
                scale = {"mla": QK ** -0.5, "cross": XHD ** -0.5}.get(kind, 1.0)
                dve.tensor_scalar(negm[:, b, :], mx[:, b, :], -scale, None, ALU.mult).then_inc(at_m, 1)

            def head_sum(kind, n):
                b = n % 2
                dve.wait_ge(at_e, n + 1)
                if kind == "dil":
                    for t in range(RT):
                        ins = dve.scalar_tensor_tensor(out=sp[b][:, t, :], in0=sp[b][:, t, :], scalar=1.0,
                                                       in1=mult[:, t, :], op0=ALU.mult, op1=ALU.mult,
                                                       accum_out=rsum[:, b, t:t + 1])
                    ins.then_inc(at_pm, 1)
                    dve.wait_ge(at_pm, n + 1)
                if n >= 2:
                    dve.wait_ge(at_y, n - 1)
                dve.reciprocal(rden[:, b, :], rsum[:, b, :]).then_inc(at_r, 1)

            def head_pt(n):
                b = n % 2
                dve.wait_ge(at_pt, n + 1)
                if n >= 2:
                    dve.wait_ge(at_o, n - 1)
                dve.tensor_copy(pT[b][:, :, :], bank[4 + b][:, :].rearrange("p (k s) -> p k s", k=2)).then_inc(at_pc, 1)

            def head_rope(kind, n):
                if kind == "mla":
                    dve.wait_ge(at_t, n + 1)
                    dve.wait_ge(at_s, n - 1)
                    dve.tensor_copy(rT[n % 2][:, :], bank[6 + n % 2][0:ROPE, 2 * P:4 * P]).then_inc(at_rope, 1)

            def attend(kind):
                ns = heads(kind)
                head_rope(kind, ns[0])
                head_rope(kind, ns[1])
                head_max(kind, ns[0])
                for n in ns:
                    head_sum(kind, n)
                    if n + 2 in ns:
                        head_rope(kind, n + 2)
                    if n + 1 in ns:
                        head_max(kind, n + 1)
                    head_pt(n)

            attend("dil")
            norm_turn("yatt", UNIT0["glu"])

            def p_(name):
                return par[:, PAR[name], :]

            are, aim = scolp[:, 0:32], scolp[:, 32:64]
            dve.wait_ge(nt_tp, PAIR0["h2"])
            dve.wait_ge(ld["sdt"], 16)
            dve.wait_ge(ld["spar"], 32)
            dve.tensor_copy(srow[64:96, :].rearrange("p (g n) -> p g n", n=NST), bcast(dtr[64:96, :], [1, 2], [0, NST]))\
                .then_inc(ss_par, 1)
            dve.wait_ge(ss_parT, 1)
            dve.tensor_copy(scolp[:, :], bank[6][:, 0:96]).then_inc(ss_pc, 1)
            dve.wait_ge(ss_exp, 1)
            link(dve.tensor_tensor(p_("ard"), are, p_("dt"), ALU.mult))
            dve.tensor_tensor(p_("th"), aim, p_("dt"), ALU.mult).then_inc(ss_trig, 1)
            dve.wait_ge(ss_trig, 1)
            link(dve.tensor_scalar(p_("k"), p_("th"), 1.0 / TWO_PI, MAGIC, ALU.mult, ALU.add))
            link(dve.tensor_scalar(p_("k"), p_("k"), MAGIC, None, ALU.subtract))
            link(dve.scalar_tensor_tensor(out=p_("r"), in0=p_("k"), scalar=-PI_HEAD, in1=p_("th"), op0=ALU.mult, op1=ALU.add))
            link(dve.scalar_tensor_tensor(out=p_("r"), in0=p_("k"), scalar=-PI_REST, in1=p_("r"), op0=ALU.mult, op1=ALU.add))
            dve.tensor_scalar(p_("r"), p_("r"), 3.1415925, -3.1415925, ALU.min, ALU.max).then_inc(ss_trig, 1)
            dve.wait_ge(ss_trig, 2)
            link(dve.tensor_scalar(phh[:, :], p_("r"), 1.0 / TWO_PI, None, ALU.mult))
            head = phh[:, :].bitcast(F32)
            link(dve.scalar_tensor_tensor(out=p_("phl"), in0=head, scalar=-PI_HEAD, in1=p_("r"), op0=ALU.mult, op1=ALU.add))
            link(dve.scalar_tensor_tensor(out=p_("phl"), in0=head, scalar=-PI_REST, in1=p_("phl"), op0=ALU.mult, op1=ALU.add))
            link(dve.tensor_scalar(p_("phl"), p_("phl"), 1.0 / TWO_PI, None, ALU.mult))
            link(dve.tensor_tensor(p_("den"), are, are, ALU.mult))
            link(dve.tensor_tensor(p_("t1"), aim, aim, ALU.mult))
            link(dve.tensor_tensor(p_("den"), p_("den"), p_("t1"), ALU.add))
            link(dve.reciprocal(p_("rden"), p_("den")))
            dve.wait_ge(ss_exp, 4)
            link(dve.tensor_scalar(p_("cos"), p_("sh2"), -2.0, 1.0, ALU.mult, ALU.add))
            link(dve.tensor_tensor(p_("nr"), p_("mag"), p_("cos"), ALU.mult))
            link(dve.tensor_tensor(p_("ni"), p_("mag"), p_("sin"), ALU.mult))
            link(dve.tensor_scalar(p_("nr"), p_("nr"), 1.0, None, ALU.subtract))
            link(dve.tensor_tensor(p_("t1"), p_("nr"), are, ALU.mult))
            link(dve.tensor_tensor(p_("t2"), p_("ni"), aim, ALU.mult))
            link(dve.tensor_tensor(p_("t1"), p_("t1"), p_("t2"), ALU.add))
            link(dve.tensor_tensor(p_("zr"), p_("t1"), p_("rden"), ALU.mult))
            link(dve.tensor_tensor(p_("t1"), p_("ni"), are, ALU.mult))
            link(dve.tensor_tensor(p_("t2"), p_("nr"), aim, ALU.mult))
            link(dve.tensor_tensor(p_("t1"), p_("t1"), p_("t2"), ALU.subtract))
            link(dve.tensor_tensor(p_("zi"), p_("t1"), p_("rden"), ALU.mult))
            for c in range(2):
                link(dve.memset(bb[c][:, :, :], 0.0))
            dve.wait_ge(ld["sb"], 32)
            z3 = {c: bcast(p_(c), [1, STILES], [0, GC]) for c in ("zr", "zi")}
            for m, (b_, z) in enumerate(((0, "zr"), (1, "zi"), (1, "zr"), (0, "zi"))):
                link(dve.tensor_tensor(btmp[:, m], bn[b_][:, :, :], z3[z], ALU.mult))
            for c in range(2):
                for g in range(2):
                    rows, cols = slice(64 * g, 64 * g + 64), slice(GC * g, GC * g + GC)
                    ins = dve.tensor_tensor(bb[c][rows, :, cols], btmp[rows, 2 * c], btmp[rows, 2 * c + 1],
                                            (ALU.subtract, ALU.add)[c])
                ins.then_inc(ss_bb, 1)
            dve.wait_ge(ss_bb, 2)
            dve.wait_ge(ld["parity"], 16)
            dve.wait_ge(ld["sc"], 32)
            for c in range(2):
                for g in range(2):
                    ins = dve.tensor_scalar(cc[c][:, :, NST * g:NST * g + NST], cn[c][:, :, :], parity[:, g:g + 1],
                                            (1.0, -1.0)[c], ALU.mult, ALU.mult)
                ins.then_inc(ss_bb, 1)
            dve.wait_ge(ld["iota"], 16)
            dve.wait_ge(ss_btp, 8)

            def angles(k):
                if k:
                    dve.wait_ge(ss_sin, 2 * k)
                for q in range(4):
                    j = 4 * k + q
                    ins = dve.tensor_scalar(turn[:, q, :], iota[:, :], head[:, j:j + 1], None, ALU.mult)
                link(ins)
                link(dve.tensor_scalar(half[:, :, :], turn[:, :, :], MAGIC, MAGIC, ALU.add, ALU.subtract))
                link(dve.tensor_tensor(turn[:, :, :], turn[:, :, :], half[:, :, :], ALU.subtract))
                for q in range(4):
                    j = 4 * k + q
                    ins = dve.scalar_tensor_tensor(out=turn[:, q, :], in0=iota[:, :], scalar=p_("phl")[:, j:j + 1],
                                                   in1=turn[:, q, :], op0=ALU.mult, op1=ALU.add)
                link(ins)
                link(dve.tensor_scalar(half[:, :, :], turn[:, :, :], MAGIC, MAGIC, ALU.add, ALU.subtract))
                dve.tensor_tensor(turn[:, :, :], turn[:, :, :], half[:, :, :], ALU.subtract).then_inc(ss_ang, 1)
                dve.wait_ge(ss_sin, 2 * k + 2)
                dve.tensor_scalar(co[:, :, :], half[:, :, :], -2.0, 1.0, ALU.mult, ALU.add).then_inc(ss_tab, 1)
                dve.wait_ge(ss_tab, k + 1)

            def scan_tile(j):
                q = j % 4
                c_, s_ = co[:, q, :], si[:, q, :]
                br, bi = bank[q][:, 0:S], bank[q][:, S:2 * S]
                mag = par[:, PAR["mag"], j:j + 1].broadcast_to([P, S])
                n = 12 * j

                def step(ins):
                    ins.then_inc(ss_d, 1)

                dve.wait_ge(ss_bu, j + 1)
                if j:
                    dve.wait_ge(ss_d, n)
                step(dve.tensor_tensor(rot[:, 0, :], br, c_, ALU.mult))
                step(dve.tensor_tensor(rot[:, 1, :], bi, s_, ALU.mult))
                step(dve.tensor_tensor(rot[:, 2, :], bi, c_, ALU.mult))
                step(dve.tensor_tensor(rot[:, 3, :], br, s_, ALU.mult))
                dve.wait_ge(ss_d, n + 2)
                step(dve.tensor_tensor(rot[:, 0, :], rot[:, 0, :], rot[:, 1, :], ALU.add))
                dve.wait_ge(ss_d, n + 4)
                step(dve.tensor_tensor(rot[:, 2, :], rot[:, 2, :], rot[:, 3, :], ALU.subtract))
                dve.wait_ge(ss_d, n + 5)
                step(dve.tensor_tensor_scan(rot[:, 1, :], mag, rot[:, 0, :], 0.0, ALU.mult, ALU.add))
                dve.wait_ge(ss_d, n + 6)
                step(dve.tensor_tensor_scan(rot[:, 3, :], mag, rot[:, 2, :], 0.0, ALU.mult, ALU.add))
                if j:
                    dve.wait_ge(ss_y, j)
                dve.wait_ge(ss_d, n + 7)
                step(dve.tensor_tensor(prod[:, 0, :], rot[:, 1, :], c_, ALU.mult))
                step(dve.tensor_tensor(prod[:, 2, :], rot[:, 1, :], s_, ALU.mult))
                dve.wait_ge(ss_d, n + 8)
                step(dve.scalar_tensor_tensor(out=prod[:, 1, :], in0=rot[:, 3, :], scalar=-1.0, in1=s_, op0=ALU.mult,
                                              op1=ALU.mult))
                step(dve.tensor_tensor(prod[:, 3, :], rot[:, 3, :], c_, ALU.mult))

            for k in range(8):
                angles(k)
                for q in range(4):
                    scan_tile(4 * k + q)
                dve.wait_ge(ss_y, 4 * k + 4)
                if k:
                    dve.wait_ge(ss_gt, k)
                dve.scalar_tensor_tensor(out=yt[:, :], in0=uT[:, k, :], scalar=vec("ssm_d", k), in1=bank[4 + k % 2][:, 0:S],
                                         op0=ALU.mult, op1=ALU.add).then_inc(ss_yt, 1)
                dve.wait_ge(ss_gt, k + 1)
                link(dve.tensor_copy(sa_hi[:, k, :], gt[:, :]))
                dve.tensor_tensor(sa_lo[:, k, :], gt[:, :], sa_hi[:, k, :].bitcast(F32), ALU.subtract).then_inc(ss_g, 1)

            blk = UNIT0["glu"] // 4
            dve.wait_ge(ss_g, 8)
            for c in range(2):
                pumps(blk, 2 * c, 2)
            for c in range(2):
                kt = slice(4 * c, 4 * c + 4)
                g4 = rtmp[:, :, :].rearrange("p t (k s) -> p (t k) s", s=S)
                link(dve.tensor_tensor(g4, sa_hi[:, kt, :].bitcast(F32), sa_lo[:, kt, :].bitcast(F32), ALU.add))
                dve.wait_ge(acc_free[c], 2 * (CHUNK0["glu"] // 2) + 4)
                link(dve.tensor_tensor(sig[:, kt, :], sig[:, kt, :], g4, ALU.mult))
                link(dve.tensor_copy(y2_hi[:, kt, :], sig[:, kt, :]))
                dve.tensor_tensor(y2_lo[:, kt, :], sig[:, kt, :], y2_hi[:, kt, :].bitcast(F32), ALU.subtract)\
                    .then_inc(gl_y2, 1)
            dve.wait_ge(gl_y2, 2)
            dve.wait_ge(ld["gate1"], 16)
            with dve.Fori(0, 2) as i:
                for c in range(2):
                    blk = UNIT0["out1"] // 4 + i * 2
                    pumps(blk, 4 * c, 4)
                    gated_out(blk, 4 * c + 3, CHUNK0["out1"] // 2 + i, c, i * (2 * CW) + c * CW, gate1_b, i * 2 + c)

            def times_up(blk, hq):
                unit_used(blk, 7)
                dve.wait_ge(acc_free[0], 2 * hq + 4)
                for t in range(RT):
                    dve.tensor_tensor(fg[:, t, :], fg[:, t, :], bank[2 + t][:, :], ALU.mult).then_inc(acc_free[1], 1)

            def hidden_rests(f, k):
                for hf in range(2):
                    dve.wait_ge(ff_hi, 2 * f + hf + 1)
                    ks = bass.ds(k + 2 * hf, 2)
                    dve.tensor_tensor(act_lo[:, ks, :], bank[4 + hf][:, :].rearrange("p (k s) -> p k s", k=2),
                                      act_hi[:, ks, :].bitcast(F32), ALU.subtract).then_inc(ff_lo, 1)

            def ffn(stage, f0, residual):
                blk, hq = UNIT0[stage] // 4, CHUNK0[stage] // 2
                for third, (c0, n) in enumerate(THIRDS):
                    pumps(blk, 0, 8)
                    times_up(blk, hq)
                    with dve.Fori(1, n) as i:
                        pumps(blk + i * 2, 0, 4)
                        hidden_rests(i + (f0 + c0 - 1), i * 4 - 4)
                        pumps(blk + i * 2, 4, 4)
                        times_up(blk + i * 2, hq + i)
                    blk, hq = blk + 2 * n, hq + n
                    for c in range(4):
                        if c == 0:
                            pumps(blk, 0, 1)
                            hidden_rests(f0 + c0 + n - 1, 4 * n - 4)
                            pumps(blk, 1, n - 1)
                        else:
                            pumps(blk, n * c, n)
                        residual(blk, n * c + n - 1, hq, c, c * CW, third, c)
                    blk, hq = blk + n, hq + 2

            norm_turn("h2", UNIT0["ffn1"])
            dve.wait_ge(ld["gate2"], 16)
            ffn("ffn1", 0, lambda blk, j, hq, c, col, third, n:
                gated_out(blk, j, hq, c, col, wide_b, n + (4 + 4 * third)))
            norm_turn("hmix", UNIT0["in2"])
            with dve.Fori(0, 3) as i:
                for c in range(2):
                    blk = UNIT0["in2"] // 4 + i * 2
                    pumps(blk, 4 * c, 4)
                    copy_out(blk, 4 * c + 3, c, proj2[:, 1, bass.ds(i * (2 * CW) + c * CW, CW)])
            blk = UNIT0["in2"] // 4 + 6
            for c in range(2):
                cols = (CW, IN2 - 7 * CW)[c]
                pumps(blk, 4 * c, 4)
                copy_out(blk, 4 * c + 3, c, proj2[:, 1, (6 + c) * CW:(6 + c) * CW + cols], cols)
            norm_turn("cq", UNIT0["uq"])
            norm_turn("ckv", UNIT0["uq"])
            for c in range(4):
                pumps(UNIT0["uq"] // 4, c, 1)
                copy_out(UNIT0["uq"] // 4, c, c, q_mla[:, 1, 2 * c:2 * c + 2, :].rearrange("p a b -> p (a b)"), 2 * QK)
            attend("na")
            for c in range(4):
                pumps(UNIT0["ukv"] // 4, c, 1)
                copy_out(UNIT0["ukv"] // 4, c, c, proj2[:, 1, NA_W + c * CW:NA_W + c * CW + CW])

            def rope(rows, o1, o2, x1, x2, dims):
                cs, sn = (bcast(a[:, :, :], *dims) for a in (ropec, ropes))
                a, b_, c_, d_ = rows
                dve.tensor_tensor(a, x1, cs, ALU.mult)
                dve.tensor_tensor(b_, x2, sn, ALU.mult)
                dve.tensor_tensor(c_, x1, sn, ALU.mult)
                link(dve.tensor_tensor(d_, x2, cs, ALU.mult))
                dve.tensor_tensor(o1, a, b_, ALU.subtract)
                link(dve.tensor_tensor(o2, c_, d_, ALU.add))

            chunks_out(dve, CHUNK0["out2"])
            dve.wait_ge(ld["na_const"], 48)
            dve.wait_ge(at_y, 16)
            q1, q2 = q_mla[:, :, :, NOPE:NOPE + HROPE], q_mla[:, :, :, NOPE + HROPE:QK]
            tq = [a[:, :, :].rearrange("p t (h e) -> p t h e", e=HROPE) for a in (sp[0], sp[1], pT[0], pT[1])]
            rope(tq, q1, q2, q1, q2, ([HROPE, RT], [0, HEADS], [1, HROPE]))
            k1, k2 = proj2[:, :, C_KR:C_KR + HROPE], proj2[:, :, C_KR + HROPE:IN2]
            tk = [a[:, :, 0:HROPE] for a in (sp[0], sp[1], pT[0], pT[1])]
            rope(tk, kr[:, :, 0:HROPE], kr[:, :, HROPE:ROPE], k1, k2, ([HROPE, RT], [1, HROPE]))
            dve.sem_inc(s_kr, 1)
            dve.wait_ge(s_krt, 1)
            dve.tensor_copy(krT[:, :], bank[7][0:ROPE, 2 * P:4 * P]).then_inc(s_krT, 1)
            attend("mla")
            norm_turn("yna", UNIT0["out2"])
            norm_turn("ymla", UNIT0["out2"])

            def add_square(stage):
                with dve.Fori(0, 2) as i:
                    for c in range(2):
                        blk = UNIT0[stage] // 4 + i * 2
                        pumps(blk, 4 * c, 4)
                        add_out(blk, 4 * c + 3, CHUNK0[stage] // 2 + i, c, i * (2 * CW) + c * CW)

            add_square("out2")
            norm_turn("hmem", UNIT0["xq"])
            with dve.Fori(0, 2) as i:
                for c in range(2):
                    blk = UNIT0["xq"] // 4 + i * 2
                    pumps(blk, 4 * c, 4)
                    copy_out(blk, 4 * c + 3, c, xq[:, 1, bass.ds(i * (2 * CW) + c * CW, CW)])
            attend("cross")
            norm_turn("ocross", UNIT0["xo"])
            add_square("xo")
            norm_turn("hffn", UNIT0["ffn2"])
            ffn("ffn2", FCH, lambda blk, j, hq, c, col, third, n: add_out(blk, j, hq, c, col))
            stats("final", STAT0["final"], PAIR0["hffn"] + 8, D)
            dve.wait_ge(ld["final"], 16)
            for t in range(RT):
                link(dve.tensor_scalar(x[:, t, :], x[:, t, :], rstd[:, t:t + 1], None, ALU.mult))
                dve.tensor_tensor(x[:, t, :], x[:, t, :], wide_b[:, :], ALU.mult).then_inc(s_fin, 1)


_INS = ["x", "c", "w_ada", "b_ada", "norm1_w", "w_in", "ssm_a_re", "ssm_a_im", "ssm_log_dt", "ssm_b_re", "ssm_b_im",
        "ssm_c_re", "ssm_c_im", "ssm_d", "ssm_w_glu", "q_norm_w", "k_norm_w", "w_out", "norm2_w", "w_ffn_gate",
        "w_ffn_up", "w_ffn_down", "mem_2", "ln_mix_2", "w_in_2", "q_norm_2", "kv_norm_2", "w_uq_2", "w_ukv_2",
        "na_rpb_2", "na_out_norm_2", "mla_out_norm_2", "w_out_2", "ln_mem_2", "mem_norm_2", "w_xq_2", "w_xk_2",
        "w_xv_2", "w_xo_2", "ln_ffn_2", "w_gate_2", "w_up_2", "w_down_2", "final_norm_2"]


def shape_constants():
    import numpy as np

    t, s = np.arange(S)[:, None], np.arange(S)[None, :]
    d = t - s
    count = ((d >= 0) & (d <= 128)).astype(np.float32) + ((d >= 0) & (d % 4 == 0)) + ((d >= 0) & (d % 16 == 0))
    dist = np.where(count > 0, d, 1e33)
    col = np.arange(GRID_W)
    start = np.clip(col - NA_COLS // 2, 0, GRID_W - NA_COLS)[:, None]
    window = (col[None, :] >= start) & (col[None, :] < start + NA_COLS)
    inv = 1.0 / (np.float32(10000.0) ** (np.arange(0, ROPE, 2, dtype=np.float32) / ROPE))
    ang = np.arange(S, dtype=np.float32)[:, None] * inv[None, :].astype(np.float32)
    tables = {"dist": dist, "mult": count, "colmask": np.tile(np.where(window, 0.0, -1e30), (2, NA_ROWS)),
              "cos": np.cos(ang), "sin": np.sin(ang), "iota": np.tile(np.arange(S), (P, 1)),
              "parity": np.stack([np.arange(P) // GC % 2 == 0, np.arange(P) // GC % 2 == 1], 1)}
    return {"const_" + n: np.ascontiguousarray(a, dtype=np.float32) for n, a in tables.items()}


def kernel(**inputs):
    import numpy as np
    import concourse.bacc as bacc
    from concourse.bass_utils import run_bass_kernel_spmd

    nc = bacc.Bacc("TRN2", target_bir_lowering=False, num_devices=1)
    arrays = {"in_" + n: np.ascontiguousarray(inputs[n]) for n in _INS}
    arrays.update(shape_constants())
    aps = {n: nc.dram_tensor(n, a.shape, mybir.dt.from_np(a.dtype), kind="ExternalInput").ap() for n, a in arrays.items()}
    out = nc.dram_tensor("out", (1, S, D), F32, kind="ExternalOutput").ap()
    build(nc, {n.removeprefix("in_"): a for n, a in aps.items()}, out)
    r = run_bass_kernel_spmd(nc, [arrays], core_ids=[0])
    return r.results[0]["out"]
```

```python
from contextlib import ExitStack

import concourse.bass as bass
from concourse import mybir
from concourse.alu_op_type import AluOpType as ALU

F32 = mybir.dt.float32
F32R = mybir.dt.float32r
BF16 = mybir.dt.bfloat16
ACT = mybir.ActivationFunctionType
AX = mybir.AxisListType

P = 128
D = 2048
S = 256
RT = S // P
KD = D // P
CW = 512
UK = 4
RING = 4
LOOKAHEAD = 3
EPS = 1e-6

SSM_W = 1024
GROUPS, GC, NST = 64, 16, 64
STILES = GROUPS * NST // P
HEADS, HD = 8, 128
X_HEADS, XHD = 4, 512
XKT = XHD // P
FF = 5632
FCH = FF // CW
THIRDS = ((0, 4), (4, 4), (8, 3))
GRID_W, NA_ROWS, NA_COLS, NA_RMAX = 64, 4, 16, 8
NA_DR, NA_DC = 2 * NA_RMAX - 1, 2 * NA_COLS - 1
TOEP_W = 128
TOEP_AT = (GRID_W - 1) - (NA_COLS - 1)
NOPE, ROPE, VD = 128, 64, 128
HROPE = ROPE // 2
QK = NOPE + ROPE
Q_RANK, KV_RANK = 512, 256
NA_W = 1024
IN2 = 3 * NA_W + Q_RANK + KV_RANK + ROPE
C_Q = 3 * NA_W
C_KV = C_Q + Q_RANK
C_KR = C_KV + KV_RANK
TWO_PI = 6.283185307179586
PI_HEAD = 6.28125
PI_REST = TWO_PI - PI_HEAD
MAGIC = 12582912.0

VECS = (("norm1_w", 16), ("norm2_w", 16), ("ln_mix_2", 16), ("ln_mem_2", 16), ("mem_norm_2", 16), ("ln_ffn_2", 16),
        ("na_out_norm_2", 8), ("mla_out_norm_2", 8), ("ssm_d", 8), ("q_norm_2", 4), ("kv_norm_2", 2),
        ("q_norm_w", 1), ("k_norm_w", 1))
VAT = {}
_at = 0
for _n, _k in VECS:
    VAT[_n] = _at
    _at += _k

NT = dict(mem=(16, 1), h1=(16, 1), yatt=(8, 0), h2=(16, 1), hmix=(16, 1), cq=(4, 1), ckv=(2, 1), yna=(8, 1),
          ymla=(8, 1), hmem=(16, 1), ocross=(16, 0), hffn=(16, 1))
PAIR0, STAT0, XN0 = {}, {}, {}
_p = _s = _x = 0
for _n, (_k, _st) in NT.items():
    PAIR0[_n], STAT0[_n], XN0[_n] = _p, _s, _x
    _p += _k // 2
    _s += _st
    _x += _st * (_k // 2)
STAT0["final"] = _s

UNIT0, CHUNK0 = {}, {}
_u = _q = 0
for _n, _uu, _qq in (("xk_ada", 48, 4), ("xv", 16, 4), ("in_ada", 96, 8), ("glu", 4, 2), ("out1", 16, 4),
                     ("ffn1", 132, 34), ("in2", 32, 8), ("uq", 4, 4), ("ukv", 4, 4), ("out2", 16, 4),
                     ("xq", 16, 4), ("xo", 16, 4), ("ffn2", 132, 34)):
    UNIT0[_n], CHUNK0[_n] = _u, _q
    _u += _uu
    _q += _qq
UNITS, CHUNKS = _u, _q
HEAD0 = dict(dil=0, na=8, mla=16, cross=24)
ARENA = 207 * 1024 + 512
UNIT0["end"], CHUNK0["end"] = UNITS, CHUNKS
PAR = {n: i for i, n in enumerate(
    "dt ard mag th k r sin sh sh2 phl den rden cos nr ni t1 t2 zr zi".split())}


def build(nc, A, out):
    with ExitStack() as ctx:
        base = (nc.sbuf_base + 63) // 64 * 64
        size = ARENA
        ctx.enter_context(nc.sbuf_tensor("arena", [P, size // 4 + 16], F32))

        def sb(name, offset, shape, dt=F32):
            count = 1
            for n in shape[1:]:
                count *= n
            assert offset + count * (2 if dt == BF16 else 4) <= size, name
            return nc.alloc_sbuf_tensor_at(name, shape, dt, offset=base + offset)

        KB = 1024
        raw = [sb(f"raw{s}", 8 * KB * s, [P, UK, CW]) for s in range(RING)]
        whi = [sb(f"whi{s}", 8 * KB * (4 + s), [P, UK, CW], F32R) for s in range(RING)]
        wlo = [sb(f"wlo{s}", 8 * KB * (8 + s), [P, UK, CW], F32R) for s in range(RING)]
        x = sb("x", 96 * KB, [P, RT, D])
        sa_hi = sb("sa_hi", 112 * KB, [P, 8, S], F32R)
        sa_lo = sb("sa_lo", 120 * KB, [P, 8, S], F32R)
        s2_hi = sb("s2_hi", 128 * KB, [P, 8, S], F32R)
        s2_lo = sb("s2_lo", 136 * KB, [P, 8, S], F32R)
        qkT = [sb(f"qkT{b}", (128 + 2 * b) * KB, [P, 2, S]) for b in range(2)]
        xqT = sb("xqT", 128 * KB, [P, XKT, S])
        sp = [sb(f"sp{b}", (132 + 2 * b) * KB, [P, RT, S]) for b in range(2)]
        pT = [sb(f"pT{b}", (136 + 2 * b) * KB, [P, RT, S]) for b in range(2)]
        rT = [sb(f"rT{b}", (140 + b) * KB, [ROPE, S]) for b in range(2)]
        sqs = sb("sqs", 148 * KB, [P, SSM_W])
        sqj = sb("sqj", 145 * KB + 512, [P, HEADS, HD], BF16)
        krT = sb("krT", 142 * KB, [ROPE, S])
        xn = [sb(f"xn{b}", (144 + 2 * b) * KB, [P, RT, 2 * P]) for b in range(2)]
        full = [sb(f"full{b}", (148 + 2 * b) * KB, [P, 2, S]) for b in range(2)]
        junk = sb("junk", 144 * KB, [P, RT, D], BF16)
        at = [152 * KB]

        def small(name, shape, dt=F32):
            count = 1
            for n in shape[1:]:
                count *= n
            t = sb(name, at[0], shape, dt)
            at[0] += (4 * count + 31) // 32 * 32
            return t

        ident = small("ident", [P, P])
        vcol = small("vcol", [P, P])
        modc = small("modc", [P, 96])
        scol = [small(f"scol{b}", [P, KD]) for b in range(2)]
        ccol = small("ccol", [P, 2 * KD + P], F32R)
        qscol = small("qscol", [P, 1])
        ss = small("ss", [P, RT])
        var = small("var", [P, RT])
        rstd = small("rstd", [P, RT])
        neghalf = small("neghalf", [P, 2 * RT * HEADS])
        mx = small("mx", [P, 2, RT])
        negm = small("negm", [P, 2, RT])
        rsum = small("rsum", [P, 2, RT])
        rden = small("rden", [P, 2, RT])
        qk_ss = small("qk_ss", [P, RT, 2 * HEADS])
        qk_rs = small("qk_rs", [P, RT, 2 * HEADS])
        parity = small("parity", [P, 2])
        PH = 155 * KB + 512
        assert at[0] <= PH, at[0]
        mem = sb("mem", PH, [P, RT, D])
        kvst = [sb(f"kvst{b}", PH + (16 + 4 * b) * KB, [P, RT, CW]) for b in range(2)]
        vrow = sb("vrow", PH + 24 * KB, [P, P])
        crow = sb("crow", PH + 25 * KB, [KD, P])
        csil = sb("csil", PH + 26 * KB, [KD, P])
        cT = sb("cT", PH + 27 * KB, [P, KD])
        adast = [sb(f"adast{b}", PH + (44 + 2 * b) * KB, [2, CW]) for b in range(2)]
        mrow = [sb(f"mrow{n}", PH + (48 + n) * KB, [64, 2, P]) for n in range(2)]
        mbias = [sb(f"mbias{n}", PH + 50 * KB + 512 * n, [64, P]) for n in range(2)]
        proj = sb("proj", PH, [P, RT, 4 * SSM_W])
        uT = sb("uT", PH + 32 * KB, [P, 8, S])
        dist = sb("dist", PH + 40 * KB, [P, RT, S])
        mult = sb("mult", PH + 42 * KB, [P, RT, S])
        bt = [sb(f"bt{c}", PH + 4 * KB * c, [P, 8, P]) for c in range(2)]
        ct = [sb(f"ct{c}", PH + (8 + 4 * c) * KB, [P, 8, P]) for c in range(2)]
        bb = [sb(f"bb{c}", PH + (16 + 4 * c) * KB, [P, STILES, 2 * GC]) for c in range(2)]
        bn = [sb(f"bn{c}", PH + (24 + 2 * c) * KB, [P, STILES, GC]) for c in range(2)]
        cn = [sb(f"cn{c}", PH + (28 + 2 * c) * KB, [P, 8, NST]) for c in range(2)]
        cc = [sb(f"cc{c}", PH + (40 + 4 * c) * KB, [P, 8, P]) for c in range(2)]
        btmp = sb("btmp", PH + 40 * KB, [P, 4, STILES, GC])
        turn = sb("turn", PH + 16 * KB, [P, 4, S])
        half = sb("half", PH + 20 * KB, [P, 4, S])
        co = [sb("co0", PH + 24 * KB, [P, 4, S]), sb("co1", 8 * KB * 7, [P, 4, S])]
        si = [sb("si0", PH + 28 * KB, [P, 4, S]), sb("si1", 8 * KB * 7 + 4 * KB, [P, 4, S])]
        prod = [sb(f"prod{b}", 8 * KB * 11 + 4 * KB * b, [P, 4, S]) for b in range(2)]
        rot = [sb(f"rot{b}", PH + (40 + 4 * b) * KB, [P, 4, S]) for b in range(2)]
        iota = sb("iota", PH + 48 * KB, [P, S])
        cneg = [sb(f"cneg{b}", PH + 51 * KB + 512 * b, [P, P]) for b in range(2)]
        yt = sb("yt", PH + 49 * KB, [P, S])
        gt = sb("gt", PH + 50 * KB, [P, S])
        SP_ = 144 * KB
        srow = sb("srow", SP_, [96, P])
        dtr = sb("dtr", SP_ + 512, [96, 2])
        scolp = sb("scolp", SP_ + 1024, [P, 96])
        par = sb("par", SP_ + 3 * 512, [P, len(PAR), STILES])
        phh = sb("phh", SP_ + 4 * KB - 128, [P, STILES], F32R)
        phase = sb("phase", SP_ + 4 * KB, [P, 2, STILES, 16])
        y2_hi = sb("y2_hi", PH, [P, 8, S], F32R)
        y2_lo = sb("y2_lo", PH + 8 * KB, [P, 8, S], F32R)
        sig = sb("sig", PH + 16 * KB, [P, 8, S])
        gate1_b = sb("gate1_b", PH + 24 * KB, [P, D])
        act_hi = sb("act_hi", PH, [P, 16, S], F32R)
        act_lo = sb("act_lo", PH + 16 * KB, [P, 16, S], F32R)
        fg = sb("fg", PH + 32 * KB, [P, RT, CW])
        rtmp = sb("rtmp", PH + 40 * KB, [P, RT, CW])
        wide_b = sb("wide_b", PH + 44 * KB, [P, D])
        proj2 = sb("proj2", PH, [P, RT, IN2])
        q_mla = sb("q_mla", PH + 31 * KB, [P, RT, HEADS, QK])
        bias = [sb(f"bias{b}", PH + (43 + 2 * b) * KB, [P, RT, S]) for b in range(2)]
        colmask = sb("colmask", PH + 47 * KB, [P, S])
        ropec = sb("ropec", PH + 48 * KB, [P, RT, HROPE])
        ropes = sb("ropes", PH + 48 * KB + 256, [P, RT, HROPE])
        zrow = sb("zrow", PH + 48 * KB + 512, [HEADS * NA_DR, TOEP_W])
        kr = sb("kr", PH + 49 * KB, [P, RT, ROPE])
        xq = sb("xq", PH, [P, RT, D])
        xkT = sb("xkT", PH + 16 * KB, [P, KD, S])
        xkv = sb("xkv", PH + 32 * KB, [P, RT, D])

        bank = [ctx.enter_context(nc.psum_tensor(f"bank{i}", [P, CW], F32)) for i in range(8)]

        scr_k = nc.dram_tensor("scr_k", (S, D), F32).ap().rearrange("(t p) n -> p t n", p=P)
        scr_v = nc.dram_tensor("scr_v", (S, D), F32).ap().rearrange("(t p) n -> p t n", p=P)
        scr_ada = nc.dram_tensor("scr_ada", (2, 6 * D), F32).ap()
        scr_gate = nc.dram_tensor("scr_gate", (64, P), F32).ap()
        scr_toep = nc.dram_tensor("scr_toep", (HEADS * NA_DR, GRID_W * GRID_W), F32).ap()
        scr_rpb = nc.dram_tensor("scr_rpb", (HEADS * NA_DR, TOEP_W), F32).ap()

        def sem(name):
            return ctx.enter_context(nc.semaphore(name))

        landed = [sem(f"landed{s}") for s in range(RING)]
        hi_done = sem("hi_done")
        lo_done = sem("lo_done")
        used = sem("used")
        acc_free = [sem(f"acc_free{p}") for p in range(2)]
        x_upd = sem("x_upd")
        gated = sem("gated")
        ada_full = sem("ada_full")
        ada_free = [sem(f"ada_free{b}") for b in range(2)]
        adast_free = [sem(f"adast_free{b}") for b in range(2)]
        kvst_free = [sem(f"kvst_free{b}") for b in range(2)]
        nt_sq = [sem("nt_sq0"), sem("nt_sq1")]
        nt_var, nt_rstd, nt_xn, nt_tp, nt_full, nt_hi, nt_out = (
            sem(n) for n in ("nt_var", "nt_rstd", "nt_xn", "nt_tp", "nt_full", "nt_hi", "nt_out"))
        tp_done, tp_out = sem("tp_done"), sem("tp_out")
        (at_t, at_qk, at_rope, at_s, at_sb, at_mx, at_m, at_e, at_pm, at_r, at_pt, at_pc, at_o, at_y) = (
            sem(n) for n in ("at_t", "at_qk", "at_rope", "at_s", "at_sb", "at_mx", "at_m", "at_e", "at_pm", "at_r",
                             "at_pt", "at_pc", "at_o", "at_y"))
        ld = {n: sem("ld_" + n) for n in (
            "x", "mem", "vec", "c", "mrow0", "mrow1", "masks", "spar", "sdt", "sb", "sc", "iota", "gate1", "gate2",
            "rpb0", "rpb1", "rpb2", "toep", "bias0", "bias1", "na_const", "xk", "xv", "final", "parity", "gstore")}
        (s_id, s_half, s_vec, s_vcol, s_csil, s_ct, s_cT, s_ccol, s_mod, s_modT, s_modc, s_qk, s_qkv, s_qkr, s_qkn,
         s_kr, s_zero, s_fin, s_out) = (
            sem(n) for n in ("s_id", "s_half", "s_vec", "s_vcol", "s_csil", "s_ct", "s_cT", "s_ccol", "s_mod", "s_modT",
                             "s_modc", "s_qk", "s_qkv", "s_qkr", "s_qkn", "s_kr", "s_zero", "s_fin", "s_out"))
        link_dve = sem("link_dve")
        (ss_par, ss_parT, ss_pc, ss_exp, ss_bb, ss_btp, ss_btc, ss_phase, ss_add, ss_ang, ss_sin, ss_tab, ss_bu,
         ss_pp, ss_cneg, ss_y, ss_yt, ss_gt, ss_g, ss_trig) = (
            sem(n) for n in ("ss_par", "ss_parT", "ss_pc", "ss_exp", "ss_bb", "ss_btp", "ss_btc", "ss_phase",
                             "ss_add", "ss_ang", "ss_sin", "ss_tab", "ss_bu", "ss_pp", "ss_cneg", "ss_y", "ss_yt", "ss_gt", "ss_g",
                             "ss_trig"))
        ss_d, s_kb, s_krt, s_krT, gl_y2 = (sem(n) for n in ("ss_d", "s_kb", "s_krt", "s_krT", "gl_y2"))
        ff_tp, ff_hi, ff_lo = (sem(n) for n in ("ff_tp", "ff_hi", "ff_lo"))

        def sa(k):
            return (sa_hi[:, k, :], sa_lo[:, k, :]) if k < 8 else (s2_hi[:, k - 8, :], s2_lo[:, k - 8, :])

        def vec(name, k=0):
            return vcol[:, VAT[name] + k:VAT[name] + k + 1]

        def chunks_out(eng, q):
            eng.wait_ge(acc_free[0], 2 + 2 * ((q + 1) // 2))
            eng.wait_ge(acc_free[1], 2 + 2 * (q // 2))

        NTSRC = {
            "mem": lambda t, c, w: mem[:, t, c:c + w], "h1": lambda t, c, w: x[:, t, c:c + w],
            "yatt": lambda t, c, w: proj[:, t, SSM_W + c:SSM_W + c + w],
            "cq": lambda t, c, w: proj2[:, t, C_Q + c:C_Q + c + w],
            "ckv": lambda t, c, w: proj2[:, t, C_KV + c:C_KV + c + w],
            "yna": lambda t, c, w: proj2[:, t, c:c + w],
            "ymla": lambda t, c, w: q_mla[:, t, c // VD:(c + w) // VD, 0:VD],
            "ocross": lambda t, c, w: xq[:, t, c:c + w]}
        for n in ("h2", "hmix", "hmem", "hffn", "final"):
            NTSRC[n] = NTSRC["h1"]
        NTSCALE = {"mem": "mem_norm_2", "hmix": "ln_mix_2", "cq": "q_norm_2", "ckv": "kv_norm_2",
                   "yna": "na_out_norm_2", "ymla": "mla_out_norm_2", "hmem": "ln_mem_2", "hffn": "ln_ffn_2"}
        NTK0 = {"yatt": 8, "ckv": 4, "ymla": 8}

        QKSRC = {
            "dil": [lambda t, h, w=w: proj[:, t, SSM_W * w + h * HD:SSM_W * w + h * HD + HD] for w in (1, 2)],
            "na": [lambda t, h, w=w: proj2[:, t, NA_W * w + h * HD:NA_W * w + h * HD + HD] for w in (0, 1)],
            "mla": [lambda t, h: q_mla[:, t, h, 0:NOPE],
                    lambda t, h: proj2[:, t, NA_W + h * (NOPE + VD):NA_W + h * (NOPE + VD) + NOPE]]}
        VSRC = {
            "dil": lambda t, h: proj[:, t, 3 * SSM_W + h * HD:3 * SSM_W + h * HD + HD],
            "na": lambda t, h: proj2[:, t, 2 * NA_W + h * HD:2 * NA_W + h * HD + HD],
            "mla": lambda t, h: proj2[:, t, NA_W + h * (NOPE + VD) + NOPE:NA_W + (h + 1) * (NOPE + VD)],
            "cross": lambda t, h: xkv[:, t, h * XHD:h * XHD + XHD]}
        YDST = {"dil": QKSRC["dil"][0], "na": QKSRC["na"][0], "mla": QKSRC["mla"][0],
                "cross": lambda t, h: xq[:, t, h * XHD:h * XHD + XHD]}

        block = ctx.enter_context(nc.Block())

        def bcast(ap, *dims):
            return bass.AP(ap.tensor, ap.offset, [list(ap.ap[0])] + [list(d) for d in dims])

        def src_ready(eng, name):
            if name == "mem":
                eng.wait_ge(ld["mem"], 16)
            elif name == "h1":
                eng.wait_ge(ld["x"], 16)
            elif name in ("yatt", "yna", "ymla", "ocross"):
                eng.wait_ge(at_y, {"yatt": 8, "yna": 16, "ymla": 24, "ocross": 28}[name])
            elif name == "h2":
                eng.wait_ge(x_upd, 2 + 2 * 4)
            elif name == "hmix":
                eng.wait_ge(x_upd, 2 + 2 * 4 + 2 * 12)
            else:
                chunks_out(eng, CHUNK0[{"cq": "uq", "ckv": "uq", "hmem": "xq", "hffn": "ffn2", "final": "end"}[name]])

        def heads(kind):
            return range(HEAD0[kind], HEAD0[kind] + (X_HEADS if kind == "cross" else HEADS))

        @block.sync
        def _(sp_):
            sp_.dma_start(mem[:, :, :], A["mem_2"].rearrange("b (t p) n -> p (b t) n", p=P)).then_inc(ld["mem"], 16)
            sp_.dma_start(crow[:, :], A["c"].rearrange("b (k p) -> (b k) p", p=P)).then_inc(ld["c"], 16)
            for name, k in VECS:
                w = A[name]
                flat = bass.AP(w.tensor, w.offset, [[P, k], [1, P]])
                sp_.dma_start(vrow[VAT[name]:VAT[name] + k, :], flat).then_inc(ld["vec"], 16)

            def kview(name):
                w = A[name]
                return w.rearrange("d (k p) n -> p (d k) n", p=P)

            def load(blk, j, w, k, kt, col, cols):
                u = 4 * blk + j
                src = w[:, k:k + kt, bass.ds(col, cols)]
                sp_.wait_ge(lo_done, u + 1)
                sp_.dma_start(raw[j % RING][:, 0:kt, 0:cols], src).then_inc(landed[j % RING], 16)

            def load_chunk(blk, j, w, col, units=4, cols=CW, kt=UK, k0=0):
                for n in range(units):
                    load(blk, j + n, w, k0 + n * kt, kt, col, cols)

            def load_with_ada(blk, j, w, col, col_a):
                for n in range(4):
                    load(blk, j + 3 * n, w, n * UK, UK, col, CW)
                    for a in range(2):
                        load(blk, j + 3 * n + 1 + a, ada, n * UK, UK, col_a + a * CW, CW)

            ada, wk, wv = kview("w_ada"), kview("w_xk_2"), kview("w_xv_2")
            with sp_.Fori(0, 2) as i:
                blk = UNIT0["xk_ada"] // 4 + i * 6
                for c in range(2):
                    load_with_ada(blk, 12 * c, wk, i * (2 * CW) + c * CW, i * (4 * CW) + 2 * c * CW)
            sp_.dma_start(x[:, :, :], A["x"].rearrange("b (t p) n -> p (b t) n", p=P)).then_inc(ld["x"], 16)
            with sp_.Fori(0, 2) as i:
                for c in range(2):
                    load_chunk(UNIT0["xv"] // 4 + i * 2, 4 * c, wv, i * (2 * CW) + c * CW)
            w = kview("w_in")
            with sp_.Fori(0, 4) as i:
                blk = UNIT0["in_ada"] // 4 + i * 6
                for c in range(2):
                    load_with_ada(blk, 12 * c, w, i * (2 * CW) + c * CW, i * (4 * CW) + (8 + 2 * c) * CW)
            w = kview("ssm_w_glu")
            for c in range(2):
                load_chunk(UNIT0["glu"] // 4, 2 * c, w, c * CW, units=2)

            def square(stage, name, order=(0, 1, 2, 3)):
                w = kview(name)
                for c in range(4):
                    for n, m in enumerate(order):
                        load(UNIT0[stage] // 4, 4 * c + n, w, m * UK, UK, c * CW, CW)

            def ffn(stage, gate, up, down):
                g, u, dn = kview(gate), kview(up), kview(down)
                blk = UNIT0[stage] // 4
                for c0, n in THIRDS:
                    with sp_.Fori(0, n) as i:
                        load_chunk(blk + i * 2, 0, g, i * CW + c0 * CW)
                        load_chunk(blk + i * 2, 4, u, i * CW + c0 * CW)
                    blk += 2 * n
                    if n == 4:
                        with sp_.Fori(0, 2) as i:
                            for c in range(2):
                                load_chunk(blk + i * 2, 4 * c, dn, i * (2 * CW) + c * CW, k0=4 * c0)
                    else:
                        for c in range(4):
                            load_chunk(blk, n * c, dn, c * CW, units=n, k0=4 * c0)
                    blk += n

            square("out1", "w_out", (2, 3, 0, 1))
            ffn("ffn1", "w_ffn_gate", "w_ffn_up", "w_ffn_down")
            w = kview("w_in_2")
            with sp_.Fori(0, 3) as i:
                for c in range(2):
                    load_chunk(UNIT0["in2"] // 4 + i * 2, 4 * c, w, i * (2 * CW) + c * CW)
            load_chunk(UNIT0["in2"] // 4 + 6, 0, w, 6 * CW)
            load_chunk(UNIT0["in2"] // 4 + 6, 4, w, 7 * CW, cols=IN2 - 7 * CW)
            w = kview("w_uq_2")
            for c in range(4):
                load_chunk(UNIT0["uq"] // 4, c, w, c * 2 * QK, units=1, cols=2 * QK)
            w = kview("w_ukv_2")
            for c in range(4):
                load_chunk(UNIT0["ukv"] // 4, c, w, c * CW, units=1, kt=2)
            square("out2", "w_out_2")
            square("xq", "w_xq_2")
            square("xo", "w_xo_2")
            ffn("ffn2", "w_gate_2", "w_up_2", "w_down_2")
            for t in range(RT):
                sp_.wait_ge(s_fin, t + 1)
                sp_.dma_start(out[0, t * P:t * P + P, :], x[:, t, :]).then_inc(s_out, 16)
            sp_.wait_ge(s_out, 16 * RT)
            for b in range(2):
                sp_.wait_ge(adast_free[b], 16 + 16 * 12)
                sp_.wait_ge(kvst_free[b], 16 + 16 * 4)
            sp_.wait_ge(ld["gstore"], 16)
            sp_.wait_ge(ld["toep"], 16)

        @block.gpsimd
        def _(pool):
            pool.memset(ident[:, :], 0.0).then_inc(s_id, 1)
            pool.memset(neghalf[:, :], -0.5).then_inc(s_half, 1)
            pool.wait_ge(s_id, 1)
            pool.affine_select(out=ident[:, :], in_=ident[:, :], compare_op=ALU.not_equal, fill=1.0, base=0,
                               pattern=[[-1, P]], channel_multiplier=1).then_inc(s_id, 1)
            pool.wait_ge(s_half, 1)
            pool.dma_start(parity[:, :], A["const_parity"]).then_inc(ld["parity"], 16)
            bias_rows = A["b_ada"].rearrange("d (r f) -> (d r) f", f=P)
            ada_rows = scr_ada.rearrange("c (r f) -> r c f", f=P)
            pool.dma_start(mbias[0][0:32, :], bias_rows[0:32, :]).then_inc(ld["mrow0"], 16)
            pool.dma_start(mbias[1][:, :], bias_rows[32:96, :]).then_inc(ld["mrow1"], 16)

            def power(n):
                pool.wait_ge(nt_var, n + 1)
                pool.tensor_tensor(rstd[:, :], var[:, :], neghalf[:, 0:RT], ALU.pow).then_inc(nt_rstd, 1)

            power(STAT0["mem"])
            for b in range(2):
                pool.wait_ge(adast_free[b], 16 + 16 * 4)
            pool.dma_start(mrow[0][0:32, :, :], ada_rows[0:32, :, :]).then_inc(ld["mrow0"], 16)
            power(STAT0["h1"])
            pool.wait_ge(nt_out, PAIR0["yatt"])
            pool.dma_start(dist[:, :, :], A["const_dist"].rearrange("(t p) n -> p t n", p=P)).then_inc(ld["masks"], 16)
            pool.dma_start(mult[:, :, :], A["const_mult"].rearrange("(t p) n -> p t n", p=P)).then_inc(ld["masks"], 16)
            for n, name in enumerate(("ssm_a_re", "ssm_a_im")):
                a = A[name]
                pool.dma_start(srow[32 * n:32 * n + 32, :], bass.AP(a.tensor, a.offset, [[P, 32], [1, P]]))\
                    .then_inc(ld["spar"], 16)
            pool.dma_start(dtr[64:96, :], A["ssm_log_dt"].rearrange("d (t g) -> (d t) g", g=2)).then_inc(ld["sdt"], 16)
            pool.wait_ge(s_qkv, 1)
            pool.tensor_tensor(qk_rs[:, :, :].rearrange("p t h -> p (t h)"), qk_ss[:, :, :].rearrange("p t h -> p (t h)"),
                               neghalf[:, :], ALU.pow).then_inc(s_qkr, 1)
            for b in range(2):
                pool.wait_ge(adast_free[b], 16 + 16 * 12)
            pool.dma_start(mrow[1][:, :, :], ada_rows[32:96, :, :]).then_inc(ld["mrow1"], 16)
            pool.wait_ge(at_y, 8)
            for n, name in enumerate(("ssm_b_re", "ssm_b_im")):
                a = A[name]
                pool.dma_start(bn[n][:, :, :], bass.AP(a.tensor, a.offset, [[GC, P], [P * GC, STILES], [1, GC]]))\
                    .then_inc(ld["sb"], 16)
            for n, name in enumerate(("ssm_c_re", "ssm_c_im")):
                a = A[name]
                pool.dma_start(cn[n][:, :, :], bass.AP(a.tensor, a.offset, [[NST, P], [P * NST, 8], [1, NST]]))\
                    .then_inc(ld["sc"], 16)
            pool.dma_start(iota[:, :], A["const_iota"]).then_inc(ld["iota"], 16)
            pool.wait_ge(s_mod, 2)
            pool.dma_start(scr_gate, mrow[1][:, 0, :]).then_inc(ld["gstore"], 16)

            def add_angles(k):
                if k:
                    pool.wait_ge(ss_sin, 2 * k)
                j = slice(4 * k, 4 * k + 4)
                pool.tensor_tensor(turn[:, :, :].rearrange("p q (a b) -> p q a b", b=16),
                                   bcast(phase[:, 0, j, :], [16, 4], [1, 16], [0, 16]),
                                   bcast(phase[:, 1, j, :], [16, 4], [0, 16], [1, 16]), ALU.add).then_inc(ss_add, 1)

            def turn_forward(j):
                k, q, b = j // 4, j % 4, j % 2
                c_, s_ = co[k % 2][:, q, :], si[k % 2][:, q, :]
                pool.wait_ge(ss_tab, k + 1)
                if j >= 2:
                    pool.wait_ge(ss_y, j - 1)
                pool.wait_ge(ss_d, 8 * j + 7)
                pool.tensor_tensor(prod[b][:, 0, :], rot[b][:, 1, :], c_, ALU.mult).then_inc(ss_pp, 1)
                pool.tensor_tensor(prod[b][:, 2, :], rot[b][:, 1, :], s_, ALU.mult).then_inc(ss_pp, 1)
                pool.wait_ge(ss_d, 8 * j + 8)
                pool.tensor_tensor(prod[b][:, 1, :], rot[b][:, 3, :], s_, ALU.mult).then_inc(ss_pp, 1)
                pool.tensor_tensor(prod[b][:, 3, :], rot[b][:, 3, :], c_, ALU.mult).then_inc(ss_pp, 1)

            pool.wait_ge(ss_phase, 1)
            add_angles(0)
            for j in range(STILES):
                if j % 4 == 0 and j + 4 < STILES:
                    add_angles(j // 4 + 1)
                turn_forward(j)
            pool.wait_ge(ld["gstore"], 16)
            pool.wait_ge(ss_g, 8)
            pool.dma_start(gate1_b[:, :], bass.AP(scr_gate.tensor, scr_gate.offset, [[0, P], [1, D]]))\
                .then_inc(ld["gate1"], 16)
            power(STAT0["h2"])
            pool.dma_start(wide_b[:, :], bass.AP(scr_gate.tensor, scr_gate.offset + 48 * P, [[0, P], [1, D]]))\
                .then_inc(ld["gate2"], 16)
            power(STAT0["hmix"])
            pool.wait_ge(x_upd, 2 + 2 * 16)
            pool.memset(zrow[:, :], 0.0).then_inc(s_zero, 1)
            pool.wait_ge(s_zero, 1)
            pool.dma_start(zrow[:, TOEP_AT:TOEP_AT + NA_DC], A["na_rpb_2"].rearrange("d h r c -> (d h r) c"))\
                .then_inc(ld["rpb1"], 16)
            pool.wait_ge(ld["rpb1"], 16)
            pool.dma_start(scr_rpb, zrow[:, :]).then_inc(ld["rpb2"], 16)
            pool.wait_ge(ld["rpb2"], 16)
            rows = HEADS * NA_DR
            pool.dma_start(bass.AP(scr_toep.tensor, scr_toep.offset, [[GRID_W * GRID_W, rows], [GRID_W, GRID_W], [1, GRID_W]]),
                           bass.AP(scr_rpb.tensor, scr_rpb.offset + GRID_W - 1,
                                   [[TOEP_W, rows], [-1, GRID_W], [1, GRID_W]])).then_inc(ld["toep"], 16)
            pool.dma_start(colmask[:, :], A["const_colmask"]).then_inc(ld["na_const"], 16)
            pool.dma_start(ropec[:, :, :], A["const_cos"].rearrange("(t p) n -> p t n", p=P)).then_inc(ld["na_const"], 16)
            pool.dma_start(ropes[:, :, :], A["const_sin"].rearrange("(t p) n -> p t n", p=P)).then_inc(ld["na_const"], 16)
            pool.wait_ge(ld["na_const"], 48)
            pool.wait_ge(ld["toep"], 16)

            def bias_load(h):
                n, b = HEAD0["na"] + h, h % 2
                if h >= 2:
                    pool.wait_ge(at_sb, n - 1)
                for t in range(RT):
                    for r in range(2):
                        first = (h * NA_DR + NA_RMAX - 1 - 2 * t - r) * GRID_W * GRID_W
                        pool.dma_start(bias[b][GRID_W * r:GRID_W * r + GRID_W, t, :].rearrange("p (a c) -> p a c", c=GRID_W),
                                       bass.AP(scr_toep.tensor, scr_toep.offset + first,
                                               [[GRID_W, GRID_W], [GRID_W * GRID_W, NA_ROWS], [1, GRID_W]]))\
                            .then_inc(ld[f"bias{b}"], 16)

            bias_load(0)
            power(STAT0["cq"])
            power(STAT0["ckv"])
            for h in range(HEADS):
                if h + 1 < HEADS:
                    bias_load(h + 1)
                b = h % 2
                pool.wait_ge(ld[f"bias{b}"], 64 * (h // 2 + 1))
                pool.tensor_tensor(bias[b][:, :, :], bias[b][:, :, :], bcast(colmask[:, :], [0, RT], [1, S]), ALU.add)\
                    .then_inc(s_kb, 1)
            power(STAT0["yna"])
            power(STAT0["ymla"])
            pool.wait_ge(nt_out, PAIR0["hmem"])
            pool.wait_ge(at_y, 24)
            for b in range(2):
                pool.wait_ge(kvst_free[b], 16 + 16 * 4)
            pool.dma_start(xkv[:, :, :], scr_k).then_inc(ld["xk"], 16)
            pool.wait_ge(tp_done, 4 + 8)
            pool.dma_start(xkv[:, :, :], scr_v).then_inc(ld["xv"], 16)
            power(STAT0["hmem"])
            power(STAT0["hffn"])
            pool.wait_ge(nt_out, PAIR0["hffn"])
            a = A["final_norm_2"]
            pool.dma_start(wide_b[:, :], bass.AP(a.tensor, a.offset, [[0, P], [1, D]])).then_inc(ld["final"], 16)
            power(STAT0["final"])

        @block.tensor
        def _(pe):
            pe.sem_inc(used, RING)
            pe.sem_inc(ff_tp, 2)

            def split_ready(u):
                pe.wait_ge(lo_done, u + RING + 1)

            def chunk(blk, j, half_q, c, units=4, cols=CW, kt=UK, stat=sa, k0=0, before=(),
                      stride=1, after=lambda n: None):
                pair = c % 2
                pe.wait_ge(acc_free[pair], 2 * (half_q + c // 2) + 2)
                for n in range(units):
                    s = (j + stride * n) % RING
                    split_ready(4 * blk + j + stride * n)
                    for kk in range(kt):
                        k = n * kt + kk
                        if k in before:
                            before[k]()
                        first, last = k == 0, k == units * kt - 1
                        shi, slo = stat(k0 + k)
                        for t in range(RT):
                            o = bank[2 * pair + t][:, 0:cols]
                            rows = slice(t * P, t * P + P)
                            pe.matmul(o, shi[:, rows], whi[s][:, kk, 0:cols], start=first, stop=False)
                            pe.matmul(o, shi[:, rows], wlo[s][:, kk, 0:cols], start=False, stop=False)
                            mm = pe.matmul(o, slo[:, rows], whi[s][:, kk, 0:cols], start=False, stop=last)
                    mm.then_inc(used, 1)
                    after(n)

            def chunk_with_ada(blk, j, half_q, c, turn):
                def ada_units(n):
                    for b in range(2):
                        if n == 0:
                            pe.wait_ge(ada_free[b], turn + 1)
                        s = (j + 3 * n + 1 + b) % RING
                        split_ready(4 * blk + j + 3 * n + 1 + b)
                        for kk in range(UK):
                            k = n * UK + kk
                            two = ccol[:, 2 * k:2 * k + P]
                            pe.matmul(bank[6 + b][:, :], two, whi[s][:, kk, :], start=(k == 0), stop=False)
                            mm = pe.matmul(bank[6 + b][:, :], two, wlo[s][:, kk, :], start=False, stop=(k == KD - 1))
                        mm.then_inc(used, 1)

                chunk(blk, j, half_q, c, stride=3, after=ada_units)

            def turn_pair(name, j):
                n, stat = PAIR0[name] + j, NT[name][1]
                if stat:
                    pe.wait_ge(nt_xn, XN0[name] + j + 1)
                elif j == 0:
                    src_ready(pe, name)
                if n >= 2:
                    pe.wait_ge(nt_full, n - 1)
                for kk in range(2):
                    for t in range(RT):
                        src = xn[n % 2][:, t, kk * P:kk * P + P] if stat else NTSRC[name](t, (2 * j + kk) * P, P)
                        mm = pe.transpose(bank[4 + n % 2][:, kk * S + t * P:kk * S + t * P + P], src, ident[:, :])
                mm.then_inc(nt_tp, 1)

            def norm_turn(name):
                for j in range(NT[name][0] // 2):
                    turn_pair(name, j)

            def turn_on_the_way(pairs, ahead):
                def step(p):
                    for q, (name, m) in enumerate(pairs):
                        if q - ahead[q] == p or (p == 0 and q - ahead[q] < 0):
                            turn_pair(name, m)
                    name, m = pairs[p]
                    pe.wait_ge(nt_out, PAIR0[name] + m + 1)
                return {2 * p: (lambda p=p: step(p)) for p in range(len(pairs))}

            def eight(name):
                return turn_on_the_way([(name, m) for m in range(8)], [2] * 8)

            def turn_plain(src, pairs, n0, b0=6):
                for j in range(pairs):
                    n = n0 + j
                    if n >= 2:
                        pe.wait_ge(tp_out, n - 1)
                    for kk in range(2):
                        for t in range(RT):
                            mm = pe.transpose(bank[b0 + n % 2][:, kk * S + t * P:kk * S + t * P + P],
                                              src(t, (2 * j + kk) * P), ident[:, :])
                    mm.then_inc(tp_done, 1)

            def stat_ready(name):
                pe.wait_ge(nt_out, PAIR0[name] + NT[name][0] // 2)

            pe.wait_ge(s_id, 2)
            pe.wait_ge(ld["vec"], 16 * len(VECS))
            pe.transpose(bank[6][:, 0:P], vrow[:, :], ident[:, :]).then_inc(s_vec, 1)
            pe.wait_ge(s_csil, 1)
            pe.transpose(bank[7][:, 0:KD], csil[:, :], ident[0:KD, 0:KD]).then_inc(s_ct, 1)
            norm_turn("mem")
            stat_ready("mem")
            pe.wait_ge(s_ccol, 2)
            pe.wait_ge(s_vcol, 1)
            with pe.Fori(0, 2) as i:
                blk, hq, ha = UNIT0["xk_ada"] // 4 + i * 6, CHUNK0["xk_ada"] // 2 + i, i * 2
                for c in range(2):
                    chunk_with_ada(blk, 12 * c, hq, c, ha + c)
            with pe.Fori(0, 2) as i:
                for c in range(2):
                    chunk(UNIT0["xv"] // 4 + i * 2, 4 * c, CHUNK0["xv"] // 2 + i, c)
            pe.wait_ge(s_mod, 1)
            for b in range(2):
                pe.wait_ge(ada_free[b], 1 + 4)
            pe.transpose(bank[6][:, 0:32], mrow[0][0:32, 0, :], ident[0:32, 0:32]).then_inc(s_modT, 1)
            norm_turn("h1")
            stat_ready("h1")
            pe.wait_ge(s_modc, 1)

            def in_ada(i, between=lambda c: None):
                blk, hq, ha = UNIT0["in_ada"] // 4 + i * 6, CHUNK0["in_ada"] // 2 + i, 4 + i * 2
                for c in range(2):
                    chunk_with_ada(blk, 12 * c, hq, c, ha + c)
                    between(c)

            def turn_u(c):
                if c == 0:
                    chunks_out(pe, CHUNK0["in_ada"] + 6)
                    turn_plain(lambda t, c: proj[:, t, c:c + P], 4, 0, b0=4)

            with pe.Fori(0, 3) as i:
                in_ada(i)
            in_ada(3, turn_u)
            chunks_out(pe, CHUNK0["glu"])
            for b in range(2):
                pe.wait_ge(ada_free[b], 1 + 12)
            pe.wait_ge(tp_out, 4)
            pe.wait_ge(ss_par, 1)
            pe.transpose(bank[6][:, 0:96], srow[:, :], ident[0:96, 0:96]).then_inc(ss_parT, 1)
            pe.wait_ge(ss_pc, 1)

            def head_turn(kind, n):
                b, h = n % 2, n - HEAD0[kind]
                if kind == "cross":
                    pe.wait_ge(at_qk, n)
                elif n >= 2:
                    pe.wait_ge(at_qk, n - 1)
                if kind == "mla":
                    if h >= 2:
                        pe.wait_ge(at_rope, h - 1)
                    pe.wait_ge(at_y, n - 3 if h >= 2 else HEAD0["mla"])
                if kind == "cross":
                    for kt in range(XKT):
                        for t in range(RT):
                            mm = pe.transpose(bank[kt // 2][:, kt % 2 * S + t * P:kt % 2 * S + t * P + P],
                                              xq[:, t, h * XHD + kt * P:h * XHD + kt * P + P], ident[:, :])
                    mm.then_inc(at_t, 1)
                    return
                for w, src in enumerate(QKSRC[kind]):
                    for t in range(RT):
                        mm = pe.transpose(bank[b][:, w * S + t * P:w * S + t * P + P], src(t, h), ident[:, :])
                if kind == "mla":
                    for t in range(RT):
                        mm = pe.transpose(bank[6 + b][0:ROPE, (2 + t) * P:(3 + t) * P],
                                          q_mla[:, t, h, NOPE:QK], ident[:, :])
                mm.then_inc(at_t, 1)

            def head_scores(kind, n):
                b, h = n % 2, n - HEAD0[kind]
                pe.wait_ge(at_qk, n + 1)
                if kind == "mla":
                    pe.wait_ge(at_rope, h + 1)
                if n >= 2:
                    pe.wait_ge(at_e, n - 1)
                for t in range(RT):
                    rows = slice(t * P, t * P + P)
                    o = bank[2 + b][:, t * S:t * S + S]
                    if kind == "cross":
                        for kt in range(XKT):
                            mm = pe.matmul(o, xqT[:, kt, rows], xkT[:, h * XKT + kt, :], start=(kt == 0),
                                           stop=(kt == XKT - 1))
                    else:
                        mm = pe.matmul(o, qkT[b][:, 0, rows], qkT[b][:, 1, :], start=True, stop=(kind != "mla"))
                        if kind == "mla":
                            mm = pe.matmul(o, rT[b][:, rows], krT[:, :], start=False, stop=True)
                mm.then_inc(at_s, 1)

            def head_turn_p(kind, n):
                b = n % 2
                if kind == "dil":
                    pe.wait_ge(at_pm, n + 1)
                else:
                    pe.wait_ge(at_e, n + 1)
                if n >= 2:
                    pe.wait_ge(at_pc, n - 1)
                for t in range(RT):
                    for kt in range(RT):
                        mm = pe.transpose(bank[4 + b][:, kt * S + t * P:kt * S + t * P + P],
                                          sp[b][:, t, kt * P:kt * P + P], ident[:, :])
                mm.then_inc(at_pt, 1)

            def head_values(kind, n):
                b, h = n % 2, n - HEAD0[kind]
                pe.wait_ge(at_pc, n + 1)
                if kind == "cross":
                    pe.wait_ge(at_y, n)
                elif n >= 2:
                    pe.wait_ge(at_y, n - 1)
                if kind == "mla":
                    pe.wait_ge(at_rope, min(h + 3, HEADS))
                for t in range(RT):
                    o = bank[6 + t][:, :] if kind == "cross" else bank[6 + b][:, t * P:t * P + P]
                    for kt in range(RT):
                        mm = pe.matmul(o, pT[b][:, kt, t * P:t * P + P], VSRC[kind](kt, h), start=(kt == 0),
                                       stop=(kt == RT - 1))
                mm.then_inc(at_o, 1)

            def attend(kind):
                ns = heads(kind)
                head_turn(kind, ns[0])
                head_scores(kind, ns[0])
                head_turn(kind, ns[1])
                for n in ns:
                    if n + 1 in ns:
                        head_scores(kind, n + 1)
                    if n + 2 in ns:
                        head_turn(kind, n + 2)
                    head_turn_p(kind, n)
                    if n > ns[0]:
                        head_values(kind, n - 1)
                head_values(kind, ns[-1])
                pe.wait_ge(at_y, ns[-1] + 1)

            pe.wait_ge(s_qkn, 2)
            attend("dil")
            pe.wait_ge(s_mod, 2)
            pe.transpose(bank[6][:, 0:64], mrow[1][:, 0, :], ident[0:64, 0:64]).then_inc(s_modT, 1)
            norm_turn("yatt")

            pe.wait_ge(nt_full, PAIR0["h2"])
            for m in range(8):
                src, n = (bb, m // 2) if m < 4 else (cc, (m - 4) // 2)
                pe.wait_ge(ss_bb, n + 1 if m < 4 else n + 3)
                if m >= 2:
                    pe.wait_ge(ss_btc, m - 1)
                for q in range(4):
                    k = 4 * (m % 2) + q
                    s = bb[n][:, 4 * k:4 * k + 4, :] if m < 4 else cc[n][:, k, :]
                    mm = pe.transpose(bank[4 + m % 2][:, q * P:q * P + P], s, ident[:, :])
                mm.then_inc(ss_btp, 1)
            pe.wait_ge(ss_btc, 8)

            def drive(j):
                k, q = j // 4, j % 4
                if j >= 4:
                    pe.wait_ge(ss_d, 8 * (j - 4) + 4)
                rows = slice(32 * q, 32 * q + 32)
                for c in range(2):
                    mm = pe.matmul(bank[q][:, c * S:c * S + S], bt[c][rows, k, :], uT[rows, k, :], start=True, stop=True)
                mm.then_inc(ss_bu, 1)

            def readout(j):
                k, q = j // 4, j % 4
                pe.wait_ge(ss_pp, 4 * j + 4)
                if k >= 2 and q == 0:
                    pe.wait_ge(ss_yt, k - 1)
                o = bank[4 + k % 2][32 * q:32 * q + 32, 0:S]
                pe.wait_ge(ss_cneg, k + 1)
                cols = slice(32 * q, 32 * q + 32)
                for m, c in enumerate((ct[0][:, k, cols], cneg[k % 2][:, cols], ct[1][:, k, cols], ct[1][:, k, cols])):
                    mm = pe.matmul(o, c, prod[j % 2][:, m, :], start=(m == 0), stop=(m == 3))
                mm.then_inc(ss_y, 1)

            for j in range(3):
                drive(j)
            for j in range(STILES):
                if j + 3 < STILES:
                    drive(j + 3)
                readout(j)

            pe.wait_ge(ss_g, 8)
            for c in range(2):
                pe.wait_ge(acc_free[c], 2 * (CHUNK0["glu"] // 2) + 2)
                split_ready(UNIT0["glu"] + 2 * c + 1)
                for m in range(4):
                    o = bank[2 * c + m // 2][:, m % 2 * S:m % 2 * S + S]
                    cols = slice(m * P, m * P + P)
                    for k in range(8):
                        s, kk = 2 * c + k // UK, k % UK
                        pe.matmul(o, whi[s][:, kk, cols], sa_hi[:, k, :], start=(k == 0), stop=False)
                        pe.matmul(o, whi[s][:, kk, cols], sa_lo[:, k, :], start=False, stop=False)
                        mm = pe.matmul(o, wlo[s][:, kk, cols], sa_hi[:, k, :], start=False, stop=(k == 7))
                mm.then_inc(used, 2)

            def square(stage, stat=sa, before=()):
                for c in range(4):
                    chunk(UNIT0[stage] // 4, 4 * c, CHUNK0[stage] // 2, c, stat=stat, before=() if c else before)

            def ffn(stage, f0, norm):
                blk, hq = UNIT0[stage] // 4, CHUNK0[stage] // 2

                def turn_hidden(f, free):
                    pe.wait_ge(acc_free[1], free)
                    for hf in range(2):
                        pe.wait_ge(ff_lo, 2 * f + hf + 1)
                        for kk in range(2):
                            for t in range(RT):
                                mm = pe.transpose(bank[4 + hf][:, kk * S + t * P:kk * S + t * P + P],
                                                  fg[:, t, (2 * hf + kk) * P:(2 * hf + kk) * P + P], ident[:, :])
                        mm.then_inc(ff_tp, 1)

                for c0, n in THIRDS:
                    chunk(blk, 0, hq, 0, before=() if c0 else eight(norm))
                    chunk(blk, 4, hq, 1)
                    with pe.Fori(1, n) as i:
                        chunk(blk + i * 2, 0, hq + i, 0)
                        turn_hidden(i + (f0 + c0 - 1), 2 * (hq + i) + 2)
                        chunk(blk + i * 2, 4, hq + i, 1)
                    blk, hq, f_end = blk + 2 * n, hq + n, f0 + c0 + n
                    def acts(k):
                        return act_hi[:, k, :], act_lo[:, k, :]
                    on_the_way = {UK: lambda: turn_hidden(f_end - 1, 2 * hq + 2),
                                  UK * (n - 1): lambda: pe.wait_ge(ff_lo, 2 * f_end + 2)}
                    pe.wait_ge(ff_lo, 2 * f_end)
                    for c in range(4):
                        chunk(blk, n * c, hq, c, units=n, stat=acts, before=() if c else on_the_way)
                    blk, hq = blk + n, hq + 2

            square("out1", lambda k: sa(k + 8) if k < 8 else (y2_hi[:, k - 8, :], y2_lo[:, k - 8, :]),
                   {8: lambda: pe.wait_ge(gl_y2, 2)})
            ffn("ffn1", 0, "h2")
            chunk(UNIT0["in2"] // 4, 0, CHUNK0["in2"] // 2, 0, before=eight("hmix"))
            chunk(UNIT0["in2"] // 4, 4, CHUNK0["in2"] // 2, 1)
            with pe.Fori(1, 3) as i:
                for c in range(2):
                    chunk(UNIT0["in2"] // 4 + i * 2, 4 * c, CHUNK0["in2"] // 2 + i, c)
            chunk(UNIT0["in2"] // 4 + 6, 0, CHUNK0["in2"] // 2 + 3, 0)
            chunk(UNIT0["in2"] // 4 + 6, 4, CHUNK0["in2"] // 2 + 3, 1, cols=IN2 - 7 * CW)
            norm_turn("cq")
            norm_turn("ckv")
            stat_ready("ckv")
            for c in range(4):
                chunk(UNIT0["uq"] // 4, c, CHUNK0["uq"] // 2, c, units=1, cols=2 * QK)
            chunks_out(pe, CHUNK0["ukv"])
            attend("na")
            for c in range(4):
                chunk(UNIT0["ukv"] // 4, c, CHUNK0["ukv"] // 2, c, units=1, kt=2, k0=4)
            chunks_out(pe, CHUNK0["out2"])
            pe.wait_ge(s_kr, 1)
            for t in range(RT):
                mm = pe.transpose(bank[7][0:ROPE, (2 + t) * P:(3 + t) * P], kr[:, t, :], ident[:, :])
            mm.then_inc(s_krt, 1)
            pe.wait_ge(s_krT, 1)
            attend("mla")
            square("out2", before=turn_on_the_way([(name, m) for name in ("yna", "ymla") for m in range(4)],
                                                  [2, 2, 2, 2, 1, 1, 2, 2]))
            pe.wait_ge(ld["xk"], 16)
            turn_plain(lambda t, c: xkv[:, t, c:c + P], 8, 4)
            square("xq", before=eight("hmem"))
            pe.wait_ge(tp_out, 12)
            chunks_out(pe, CHUNK0["xo"])
            pe.wait_ge(ld["xv"], 16)
            attend("cross")
            square("xo", before=eight("ocross"))
            ffn("ffn2", FCH, "hffn")

        @block.scalar
        def _(act):
            for b in range(2):
                act.sem_inc(ada_free[b], 1)
                act.sem_inc(adast_free[b], 16)
                act.sem_inc(kvst_free[b], 16)

            def pump(blk, j):
                j += LOOKAHEAD
                s, blk = j % RING, blk + j // RING
                if isinstance(blk, int) and RING * blk + s >= UNITS:
                    return
                act.wait_ge(landed[s], 16 * blk + 16)
                act.wait_ge(used, RING * blk + s + 1)
                act.activation(whi[s][:, :, :], raw[s][:, :, :], ACT.Copy).then_inc(hi_done, 1)

            def pumps(blk, j, n):
                for m in range(n):
                    pump(blk, j + m)

            def unit_used(blk, j):
                act.wait_ge(used, RING + 4 * blk + j + 1)

            def norm_turn(name):
                k_tiles, stat = NT[name]
                s, p0 = STAT0[name], PAIR0[name]
                width = k_tiles * P
                if stat:
                    norm_squares(name, s, p0, width)
                for j in range(k_tiles // 2):
                    n, b = p0 + j, (p0 + j) % 2
                    act.wait_ge(nt_tp, n + 1)
                    if n >= 2:
                        act.wait_ge(nt_out, n - 1)
                    if name in ("yatt", "ocross"):
                        act.activation(full[b][:, :, :], bank[4 + b][:, :].rearrange("p (k s) -> p k s", k=2), ACT.Copy)\
                            .then_inc(nt_full, 1)
                        continue
                    for kk in range(2):
                        k = 2 * j + kk
                        o, i = full[b][:, kk, :], bank[4 + b][:, kk * S:kk * S + S]
                        if name in ("h1", "h2"):
                            m, shift = (0, 0) if name == "h1" else (1, 48)
                            ins = act.activation(o, i, ACT.Identity, scale=scol[m][:, k:k + 1],
                                                 bias=modc[:, shift + k:shift + k + 1])
                        else:
                            ins = act.activation(o, i, ACT.Copy, scale=vec(NTSCALE[name], k))
                    ins.then_inc(nt_full, 1)

            def norm_squares(name, s, p0, width):
                src_ready(act, name)
                if p0:
                    act.wait_ge(nt_out, p0)
                    act.wait_ge(nt_tp, p0)
                if s:
                    act.wait_ge(nt_var, s)
                src, o = NTSRC[name](0, 0, width), junk[:, 0, 0:width]
                if name == "ymla":
                    o = o.rearrange("p (a b) -> p a b", b=VD)
                act.activation(o, src, ACT.Square, accum_out=ss[:, 0:1]).then_inc(nt_sq[0], 1)

            def copy_out(blk, j, c, dst, cols=CW):
                unit_used(blk, j)
                act.activation(dst, bank[2 * (c % 2)][:, 0:cols], ACT.Copy).then_inc(acc_free[c % 2], 1)

            act.wait_ge(ld["c"], 16)
            act.activation(csil[:, :], crow[:, :], ACT.Silu).then_inc(s_csil, 1)
            act.wait_ge(s_vcol, 1)
            pumps(0, -LOOKAHEAD, LOOKAHEAD)
            norm_turn("mem")

            def ada_out(blk, j, half_a, a, col):
                b = a % 2
                unit_used(blk, j)
                act.wait_ge(adast_free[b], 16 * (half_a + a // 2 + 1))
                act.activation(adast[b][:, :], bank[6 + b][0:2, :], ACT.Copy).then_inc(ada_free[b], 1)
                act.wait_ge(ada_free[b], half_a + a // 2 + 2)
                act.dma_start(scr_ada[:, bass.ds(col, CW)], adast[b][:, :]).then_inc(adast_free[b], 16)

            def kv_out(blk, j, hq, c, scr, col):
                act.wait_ge(kvst_free[c], 16 * hq + 16)
                copy_out(blk, j, c, kvst[c][:, 0, :])
                act.wait_ge(acc_free[c], 2 * hq + 4)
                act.dma_start(scr[:, :, bass.ds(col, CW)], kvst[c][:, :, :]).then_inc(kvst_free[c], 16)

            with act.Fori(0, 2) as i:
                blk, hq, ha = UNIT0["xk_ada"] // 4 + i * 6, CHUNK0["xk_ada"] // 2 + i, i * 2
                for c in range(2):
                    pumps(blk, 12 * c, 10)
                    kv_out(blk, 12 * c + 9, hq, c, scr_k, i * (2 * CW) + c * CW)
                    for a in range(2):
                        pump(blk, 12 * c + 10 + a)
                        ada_out(blk, 12 * c + 10 + a, ha, 2 * c + a, i * (4 * CW) + (2 * c + a) * CW)
            with act.Fori(0, 2) as i:
                blk, hq = UNIT0["xv"] // 4 + i * 2, CHUNK0["xv"] // 2 + i
                for c in range(2):
                    pumps(blk, 4 * c, 4)
                    kv_out(blk, 4 * c + 3, hq, c, scr_v, i * (2 * CW) + c * CW)
            act.wait_ge(s_modc, 1)
            norm_turn("h1")
            for b in range(2):
                act.wait_ge(kvst_free[b], 16 + 16 * 4)

            def turn_plain(pairs, n0, dst, b0=6):
                for j in range(pairs):
                    n = n0 + j
                    act.wait_ge(tp_done, n + 1)
                    act.activation(dst[:, 2 * j:2 * j + 2, :], bank[b0 + n % 2][:, :].rearrange("p (k s) -> p k s", k=2),
                                   ACT.Copy).then_inc(tp_out, 1)

            def in_ada(i, between=lambda step: None):
                blk, hq, ha = UNIT0["in_ada"] // 4 + i * 6, CHUNK0["in_ada"] // 2 + i, 4 + i * 2
                for c in range(2):
                    for g in range(2):
                        pumps(blk, 12 * c + 4 * g, 4)
                        between(3 * c + g)
                    pumps(blk, 12 * c + 8, 2)
                    copy_out(blk, 12 * c + 9, c, proj[:, 0, bass.ds(i * (2 * CW) + c * CW, CW)])
                    for a in range(2):
                        pump(blk, 12 * c + 10 + a)
                        ada_out(blk, 12 * c + 10 + a, ha, 2 * c + a, i * (4 * CW) + (8 + 2 * c + a) * CW)
                    between(3 * c + 2)

            def qk_of_tile0(step):
                if step == 2:
                    turn_plain(4, 0, uT, b0=4)
                elif step in (0, 1):
                    if step == 0:
                        act.wait_ge(nt_out, PAIR0["yatt"])
                        chunks_out(act, CHUNK0["in_ada"] + 6)
                    else:
                        act.wait_ge(s_qk, 8)
                    for h in range(8 * step, 8 * step + 8):
                        act.activation(sqj[:, h % 8, :], proj[:, 0, SSM_W + h * HD:SSM_W + h * HD + HD], ACT.Square,
                                       accum_out=qk_ss[:, 0, h:h + 1]).then_inc(s_qk, 1)
                elif step == 4:
                    act.wait_ge(s_qkr, 1)
                    for h in range(2 * HEADS):
                        qk = proj[:, 0, SSM_W + h * HD:SSM_W + h * HD + HD]
                        ins = act.activation(qk, qk, ACT.Copy, scale=qk_rs[:, 0, h:h + 1])
                    ins.then_inc(s_qkn, 1)

            with act.Fori(0, 3) as i:
                in_ada(i)
            in_ada(3, qk_of_tile0)
            def head_in(kind, n):
                b = n % 2
                act.wait_ge(at_t, n + 1)
                if kind == "cross":
                    act.wait_ge(at_s, n)
                    act.activation(xqT[:, 0:2, :], bank[0][:, :].rearrange("p (k s) -> p k s", k=2), ACT.Copy)
                    act.activation(xqT[:, 2:4, :], bank[1][:, :].rearrange("p (k s) -> p k s", k=2), ACT.Copy)\
                        .then_inc(at_qk, 1)
                    return
                if n >= 2:
                    act.wait_ge(at_s, n - 1)
                if kind == "dil":
                    act.activation(qkT[b][:, 0, :], bank[b][:, 0:S], ACT.Copy, scale=qscol[:, :])
                    act.activation(qkT[b][:, 1, :], bank[b][:, S:2 * S], ACT.Copy).then_inc(at_qk, 1)
                else:
                    act.activation(qkT[b][:, :, :], bank[b][:, :].rearrange("p (k s) -> p k s", k=2), ACT.Copy)\
                        .then_inc(at_qk, 1)

            def head_exp(kind, n):
                b = n % 2
                act.wait_ge(at_m, n + 1)
                if n >= 2:
                    act.wait_ge(at_pt, n - 1)
                    act.wait_ge(at_r, n - 1)
                for t in range(RT):
                    src = sp[b][:, t, :] if kind in ("dil", "na") else bank[2 + b][:, t * S:t * S + S]
                    scale = {"mla": QK ** -0.5, "cross": XHD ** -0.5}.get(kind, 1.0)
                    acc = {} if kind == "dil" else dict(accum_out=rsum[:, b, t:t + 1])
                    ins = act.activation(sp[b][:, t, :], src, ACT.Exp, bias=negm[:, b, t:t + 1], scale=scale, **acc)
                ins.then_inc(at_e, 1)

            def head_out(kind, n):
                b, h = n % 2, n - HEAD0[kind]
                act.wait_ge(at_r, n + 1)
                act.wait_ge(at_o, n + 1)
                for t in range(RT):
                    o = bank[6 + t][:, :] if kind == "cross" else bank[6 + b][:, t * P:t * P + P]
                    ins = act.activation(YDST[kind](t, h), o, ACT.Copy, scale=rden[:, b, t:t + 1])
                ins.then_inc(at_y, 1)

            def attend(kind):
                ns = heads(kind)
                head_in(kind, ns[0])
                head_in(kind, ns[1])
                head_exp(kind, ns[0])
                for n in ns:
                    if n + 2 in ns:
                        head_in(kind, n + 2)
                    if n + 1 in ns:
                        head_exp(kind, n + 1)
                    if n > ns[0]:
                        head_out(kind, n - 1)
                head_out(kind, ns[-1])

            def p_(name):
                return par[:, PAR[name], :]
            act.wait_ge(ss_pc, 1)
            act.activation(p_("dt"), scolp[:, 64:96], ACT.Exp).then_inc(ss_exp, 1)
            act.wait_ge(ss_trig, 1)
            act.activation(p_("mag"), p_("ard"), ACT.Exp).then_inc(ss_exp, 1)
            act.wait_ge(ss_trig, 2)
            act.activation(p_("sin"), p_("r"), ACT.Sin)
            act.activation(p_("sh"), p_("r"), ACT.Sin, scale=0.5).then_inc(ss_exp, 1)
            act.wait_ge(ss_exp, 3)
            act.activation(p_("sh2"), p_("sh"), ACT.Square).then_inc(ss_exp, 1)
            act.wait_ge(s_qkn, 2)
            attend("dil")
            norm_turn("yatt")
            for m in range(8):
                act.wait_ge(ss_btp, m + 1)
                dst = (bt if m < 4 else ct)[(m % 4) // 2]
                act.activation(dst[:, 4 * (m % 2):4 * (m % 2) + 4, :],
                               bank[4 + m % 2][:, :].rearrange("p (k s) -> p k s", k=4), ACT.Copy).then_inc(ss_btc, 1)

            def sines(k):
                act.wait_ge(ss_ang, k + 1)
                if k >= 2:
                    act.wait_ge(ss_pp, 16 * (k - 1))
                act.activation(si[k % 2][:, :, :], turn[:, :, :], ACT.Sin, scale=6.283185)
                if k:
                    act.wait_ge(ss_tab, k)
                act.activation(half[:, :, :], turn[:, :, :], ACT.Sin, scale=3.1415925).then_inc(ss_sin, 1)
                act.wait_ge(ss_sin, 2 * k + 1)
                act.activation(half[:, :, :], half[:, :, :], ACT.Square).then_inc(ss_sin, 1)

            def negate(k):
                act.wait_ge(ss_btc, 8)
                if k >= 2:
                    act.wait_ge(ss_y, 4 * (k - 1))
                act.activation(cneg[k % 2][:, :], ct[0][:, k, :], ACT.Copy, scale=-1.0).then_inc(ss_cneg, 1)

            negate(0)
            sines(0)
            for k in range(8):
                if k + 1 < 8:
                    sines(k + 1)
                    negate(k + 1)
                act.wait_ge(ss_yt, k + 1)
                if k:
                    act.wait_ge(ss_g, k)
                act.activation(gt[:, :], yt[:, :], ACT.Gelu_apprx_tanh).then_inc(ss_gt, 1)

            blk = UNIT0["glu"] // 4
            for c in range(2):
                pumps(blk, 2 * c, 2)
                act.wait_ge(used, RING + 4 * blk + 2 * c + 2)
                for m in range(2):
                    act.activation(sig[:, 4 * c + 2 * m:4 * c + 2 * m + 2, :],
                                   bank[2 * c + m][:, :].rearrange("p (k s) -> p k s", k=2), ACT.Sigmoid)\
                        .then_inc(acc_free[c], 1)

            def pump_square(stage):
                with act.Fori(0, 2) as i:
                    pumps(UNIT0[stage] // 4 + i * 2, 0, 8)

            def silu_gate(blk):
                unit_used(blk, 3)
                for t in range(RT):
                    act.activation(fg[:, t, :], bank[t][:, :], ACT.Silu).then_inc(acc_free[0], 1)

            def hidden_heads(f, k):
                for hf in range(2):
                    act.wait_ge(ff_tp, 2 * f + hf + 3)
                    act.activation(act_hi[:, bass.ds(k + 2 * hf, 2), :],
                                   bank[4 + hf][:, :].rearrange("p (k s) -> p k s", k=2), ACT.Copy).then_inc(ff_hi, 1)

            def ffn(stage, f0):
                blk, hq = UNIT0[stage] // 4, CHUNK0[stage] // 2
                for c0, n in THIRDS:
                    pumps(blk, 0, 4)
                    silu_gate(blk)
                    pumps(blk, 4, 4)
                    with act.Fori(1, n) as i:
                        pumps(blk + i * 2, 0, 4)
                        hidden_heads(i + (f0 + c0 - 1), i * 4 - 4)
                        silu_gate(blk + i * 2)
                        pumps(blk + i * 2, 4, 4)
                    blk, hq = blk + 2 * n, hq + n
                    pumps(blk, 0, 1)
                    hidden_heads(f0 + c0 + n - 1, 4 * n - 4)
                    pumps(blk, 1, 4 * n - 1)
                    blk += n

            pump_square("out1")
            norm_turn("h2")
            ffn("ffn1", 0)
            norm_turn("hmix")
            with act.Fori(0, 3) as i:
                for c in range(2):
                    blk = UNIT0["in2"] // 4 + i * 2
                    pumps(blk, 4 * c, 4)
                    copy_out(blk, 4 * c + 3, c, proj2[:, 0, bass.ds(i * (2 * CW) + c * CW, CW)])
            blk = UNIT0["in2"] // 4 + 6
            for c in range(2):
                cols = (CW, IN2 - 7 * CW)[c]
                pumps(blk, 4 * c, 4)
                copy_out(blk, 4 * c + 3, c, proj2[:, 0, (6 + c) * CW:(6 + c) * CW + cols], cols)
            norm_turn("cq")
            norm_turn("ckv")
            for c in range(4):
                pumps(UNIT0["uq"] // 4, c, 1)
                copy_out(UNIT0["uq"] // 4, c, c, q_mla[:, 0, 2 * c:2 * c + 2, :].rearrange("p a b -> p (a b)"), 2 * QK)
            attend("na")
            for c in range(4):
                pumps(UNIT0["ukv"] // 4, c, 1)
                copy_out(UNIT0["ukv"] // 4, c, c, proj2[:, 0, NA_W + c * CW:NA_W + c * CW + CW])
            act.wait_ge(s_krT, 1)
            attend("mla")
            norm_turn("yna")
            norm_turn("ymla")
            pump_square("out2")
            turn_plain(8, 4, xkT)
            norm_turn("hmem")
            with act.Fori(0, 2) as i:
                for c in range(2):
                    blk = UNIT0["xq"] // 4 + i * 2
                    pumps(blk, 4 * c, 4)
                    copy_out(blk, 4 * c + 3, c, xq[:, 0, bass.ds(i * (2 * CW) + c * CW, CW)])
            attend("cross")
            norm_turn("ocross")
            pump_square("xo")
            norm_turn("hffn")
            ffn("ffn2", FCH)
            norm_squares("final", STAT0["final"], PAIR0["hffn"] + 8, D)

        @block.vector
        def _(dve):
            dve.sem_inc(lo_done, RING)
            dve.sem_inc(x_upd, 2)
            dve.sem_inc(ff_lo, 2)
            for p in range(2):
                dve.sem_inc(acc_free[p], 2)
            linked = [0]

            def link(ins):
                linked[0] += 1
                ins.then_inc(link_dve, 1)
                dve.wait_ge(link_dve, linked[0])

            def pump(blk, j):
                j += LOOKAHEAD
                s, blk = j % RING, blk + j // RING
                if isinstance(blk, int) and RING * blk + s >= UNITS:
                    return
                dve.wait_ge(hi_done, RING * blk + s + 1)
                dve.wait_ge(used, RING * blk + s + 1)
                dve.tensor_tensor(wlo[s][:, :, :], raw[s][:, :, :], whi[s][:, :, :].bitcast(F32), ALU.subtract)\
                    .then_inc(lo_done, 1)

            def pumps(blk, j, n):
                for m in range(n):
                    pump(blk, j + m)

            def unit_used(blk, j):
                dve.wait_ge(used, RING + 4 * blk + j + 1)

            def stats(name, s, p0, width):
                src_ready(dve, name)
                if p0:
                    dve.wait_ge(nt_out, p0)
                    dve.wait_ge(nt_tp, p0)
                if s:
                    dve.wait_ge(nt_var, s)
                src, o = NTSRC[name](1, 0, width), junk[:, 1, 0:width]
                if name == "ymla":
                    o = o.rearrange("p (a b) -> p a b", b=VD)
                dve.tensor_tensor_reduce(o, src, src, 1.0, 0.0, ALU.mult, ALU.add, ss[:, 1:2]).then_inc(nt_sq[1], 1)
                for t in range(RT):
                    dve.wait_ge(nt_sq[t], s + 1)
                if s:
                    dve.wait_ge(nt_rstd, s)
                dve.tensor_scalar(var[:, :], ss[:, :], 1.0 / width, EPS, ALU.mult, ALU.add).then_inc(nt_var, 1)
                dve.wait_ge(nt_rstd, s + 1)

            def norm_turn(name, units_used):
                k_tiles, stat = NT[name]
                pairs, p0 = k_tiles // 2, PAIR0[name]
                if stat:
                    stats(name, STAT0[name], p0, k_tiles * P)

                def normed(j):
                    n = p0 + j
                    if n >= 2:
                        dve.wait_ge(nt_tp, n - 1)
                    for t in range(RT):
                        src, o = NTSRC[name](t, 2 * j * P, 2 * P), xn[n % 2][:, t, :]
                        if name == "ymla":
                            o = o.rearrange("p (a b) -> p a b", b=VD)
                        ins = dve.tensor_scalar(o, src, rstd[:, t:t + 1], None, ALU.mult)
                    ins.then_inc(nt_xn, 1)

                if stat:
                    normed(0)
                    if pairs > 1:
                        normed(1)
                if units_used:
                    dve.wait_ge(used, RING + units_used)
                k0 = NTK0.get(name, 0)
                for j in range(pairs):
                    n, b, k = p0 + j, (p0 + j) % 2, k0 + 2 * j
                    hi, lo = (sa_hi, sa_lo) if k < 8 else (s2_hi, s2_lo)
                    k %= 8
                    dve.wait_ge(nt_full, n + 1)
                    dve.tensor_copy(hi[:, k:k + 2, :], full[b][:, :, :]).then_inc(nt_hi, 1)
                    if stat and j + 2 < pairs:
                        normed(j + 2)
                    dve.wait_ge(nt_hi, n + 1)
                    dve.tensor_tensor(lo[:, k:k + 2, :], full[b][:, :, :], hi[:, k:k + 2, :].bitcast(F32), ALU.subtract)\
                        .then_inc(nt_out, 1)

            def copy_out(blk, j, c, dst, cols=CW):
                unit_used(blk, j)
                dve.tensor_copy(dst, bank[2 * (c % 2) + 1][:, 0:cols]).then_inc(acc_free[c % 2], 1)

            def add_out(blk, j, hq, c, col):
                unit_used(blk, j)
                dve.wait_ge(acc_free[c % 2], 2 * (hq + c // 2) + 2)
                for t in range(RT):
                    xs = x[:, t, bass.ds(col, CW)]
                    dve.tensor_tensor(xs, bank[2 * (c % 2) + t][:, :], xs, ALU.add).then_inc(acc_free[c % 2], 1)

            def gated_out(blk, j, hq, c, col, gate, g):
                unit_used(blk, j)
                for t in range(RT):
                    dve.wait_ge(x_upd, 2 * g + t + 1)
                    dve.tensor_tensor(rtmp[:, t, :], bank[2 * (c % 2) + t][:, :], gate[:, bass.ds(col, CW)], ALU.mult)\
                        .then_inc(acc_free[c % 2], 1)
                for t in range(RT):
                    dve.wait_ge(acc_free[c % 2], 2 * (hq + c // 2) + 3 + t)
                    xs = x[:, t, bass.ds(col, CW)]
                    dve.tensor_tensor(xs, rtmp[:, t, :], xs, ALU.add).then_inc(x_upd, 1)

            dve.wait_ge(s_vec, 1)
            dve.tensor_copy(vcol[:, :], bank[6][:, 0:P]).then_inc(s_vcol, 1)
            dve.wait_ge(s_ct, 1)
            dve.tensor_copy(cT[:, :], bank[7][:, 0:KD]).then_inc(s_cT, 1)
            dve.wait_ge(s_cT, 1)
            pairs_ = ccol[:, 0:2 * KD].rearrange("p (k c) -> p k c", c=2)
            dve.memset(ccol[:, 2 * KD:2 * KD + P].bitcast(F32), 0.0)
            dve.tensor_copy(pairs_[:, :, 0], cT[:, :]).then_inc(s_ccol, 1)
            dve.wait_ge(s_ccol, 1)
            dve.tensor_tensor(pairs_[:, :, 1], cT[:, :], pairs_[:, :, 0].bitcast(F32), ALU.subtract).then_inc(s_ccol, 1)
            dve.wait_ge(s_vcol, 1)
            link(dve.tensor_tensor(qscol[:, :], vec("q_norm_w"), vec("k_norm_w"), ALU.mult))
            link(dve.tensor_scalar(qscol[:, :], qscol[:, :], HD ** -0.5, None, ALU.mult))
            pumps(0, -LOOKAHEAD, LOOKAHEAD)
            norm_turn("mem", 0)
            with dve.Fori(0, 2) as i:
                blk, hq = UNIT0["xk_ada"] // 4 + i * 6, CHUNK0["xk_ada"] // 2 + i
                for c in range(2):
                    pumps(blk, 12 * c, 10)
                    dve.wait_ge(kvst_free[c], 16 * hq + 16)
                    copy_out(blk, 12 * c + 9, c, kvst[c][:, 1, :])
                    pumps(blk, 12 * c + 10, 2)
            with dve.Fori(0, 2) as i:
                blk, hq = UNIT0["xv"] // 4 + i * 2, CHUNK0["xv"] // 2 + i
                for c in range(2):
                    pumps(blk, 4 * c, 4)
                    dve.wait_ge(kvst_free[c], 16 * hq + 16)
                    copy_out(blk, 4 * c + 3, c, kvst[c][:, 1, :])

            def modulation(m, rows):
                dve.wait_ge(ld[f"mrow{m}"], 32)
                link(dve.tensor_tensor(mrow[m][0:rows, 0, :], mrow[m][0:rows, 0, :], mrow[m][0:rows, 1, :], ALU.add))
                dve.tensor_tensor(mrow[m][0:rows, 0, :], mrow[m][0:rows, 0, :], mbias[m][0:rows, :], ALU.add)\
                    .then_inc(s_mod, 1)
                dve.wait_ge(s_modT, m + 1)
                link(dve.tensor_copy(modc[:, 32 * m:32 * m + rows], bank[6][:, 0:rows]))
                at_ = (KD, 32 + 2 * KD)[m]
                link(dve.tensor_scalar(scol[m][:, :], modc[:, at_:at_ + KD], 1.0, None, ALU.add))
                name = ("norm1_w", "norm2_w")[m]
                dve.tensor_tensor(scol[m][:, :], scol[m][:, :], vcol[:, VAT[name]:VAT[name] + KD], ALU.mult)\
                    .then_inc(s_modc, 1)

            modulation(0, 32)
            norm_turn("h1", UNIT0["in_ada"])
            for b in range(2):
                dve.wait_ge(kvst_free[b], 16 + 16 * 4)

            def in_ada(i, between=lambda step: None):
                blk = UNIT0["in_ada"] // 4 + i * 6
                for c in range(2):
                    for g in range(2):
                        pumps(blk, 12 * c + 4 * g, 4)
                        between(3 * c + g)
                    pumps(blk, 12 * c + 8, 2)
                    copy_out(blk, 12 * c + 9, c, proj[:, 1, bass.ds(i * (2 * CW) + c * CW, CW)])
                    pumps(blk, 12 * c + 10, 2)
                    between(3 * c + 2)

            def squares_of(half_):
                cols = slice(SSM_W * (1 + half_), SSM_W * (2 + half_))
                link(dve.tensor_tensor(sqs[:, :], proj[:, 1, cols], proj[:, 1, cols], ALU.mult))
                link(dve.tensor_reduce(qk_ss[:, 1, 8 * half_:8 * half_ + 8],
                                       sqs[:, :].rearrange("p (h e) -> p h e", e=HD), AX.X, ALU.add))

            def normed_qk(half_):
                cols = slice(SSM_W * (1 + half_), SSM_W * (2 + half_))
                qk = proj[:, 1, cols].rearrange("p (h e) -> p h e", e=HD)
                return dve.tensor_tensor(qk, qk, bcast(qk_rs[:, 1, 8 * half_:8 * half_ + 8], [1, HEADS], [0, HD]), ALU.mult)

            def qk_of_tile1(step):
                if step == 0:
                    dve.wait_ge(nt_out, PAIR0["yatt"])
                    chunks_out(dve, CHUNK0["in_ada"] + 6)
                    squares_of(0)
                elif step == 1:
                    squares_of(1)
                elif step == 2:
                    dve.wait_ge(s_qk, 2 * HEADS)
                    dve.tensor_scalar(qk_ss[:, :, :], qk_ss[:, :, :], 1.0 / HD, EPS, ALU.mult, ALU.add).then_inc(s_qkv, 1)
                    dve.wait_ge(ld["sdt"], 16)
                    dve.wait_ge(ld["spar"], 32)
                    dve.tensor_copy(srow[64:96, :].rearrange("p (g n) -> p g n", n=NST), bcast(dtr[64:96, :], [1, 2], [0, NST]))\
                        .then_inc(ss_par, 1)
                elif step == 3:
                    dve.wait_ge(s_qkr, 1)
                    normed_qk(0)
                elif step == 4:
                    normed_qk(1).then_inc(s_qkn, 1)

            with dve.Fori(0, 3) as i:
                in_ada(i)
            in_ada(3, qk_of_tile1)
            def p_(name):
                return par[:, PAR[name], :]

            are, aim = scolp[:, 0:32], scolp[:, 32:64]
            dve.wait_ge(ss_parT, 1)
            dve.tensor_copy(scolp[:, :], bank[6][:, 0:96]).then_inc(ss_pc, 1)
            dve.wait_ge(ss_exp, 1)
            link(dve.tensor_tensor(p_("ard"), are, p_("dt"), ALU.mult))
            dve.tensor_tensor(p_("th"), aim, p_("dt"), ALU.mult).then_inc(ss_trig, 1)
            dve.wait_ge(ss_trig, 1)
            link(dve.tensor_scalar(p_("k"), p_("th"), 1.0 / TWO_PI, MAGIC, ALU.mult, ALU.add))
            link(dve.tensor_scalar(p_("k"), p_("k"), MAGIC, None, ALU.subtract))
            link(dve.scalar_tensor_tensor(out=p_("r"), in0=p_("k"), scalar=-PI_HEAD, in1=p_("th"), op0=ALU.mult, op1=ALU.add))
            link(dve.scalar_tensor_tensor(out=p_("r"), in0=p_("k"), scalar=-PI_REST, in1=p_("r"), op0=ALU.mult, op1=ALU.add))
            dve.tensor_scalar(p_("r"), p_("r"), 3.1415925, -3.1415925, ALU.min, ALU.max).then_inc(ss_trig, 1)
            dve.wait_ge(ss_trig, 2)
            link(dve.tensor_scalar(phh[:, :], p_("r"), 1.0 / TWO_PI, None, ALU.mult))
            head = phh[:, :].bitcast(F32)
            link(dve.scalar_tensor_tensor(out=p_("phl"), in0=head, scalar=-PI_HEAD, in1=p_("r"), op0=ALU.mult, op1=ALU.add))
            link(dve.scalar_tensor_tensor(out=p_("phl"), in0=head, scalar=-PI_REST, in1=p_("phl"), op0=ALU.mult, op1=ALU.add))
            link(dve.tensor_scalar(p_("phl"), p_("phl"), 1.0 / TWO_PI, None, ALU.mult))
            link(dve.tensor_tensor(p_("den"), are, are, ALU.mult))
            link(dve.tensor_tensor(p_("t1"), aim, aim, ALU.mult))
            link(dve.tensor_tensor(p_("den"), p_("den"), p_("t1"), ALU.add))
            link(dve.reciprocal(p_("rden"), p_("den")))
            dve.wait_ge(ss_exp, 4)
            link(dve.tensor_scalar(p_("cos"), p_("sh2"), -2.0, 1.0, ALU.mult, ALU.add))
            link(dve.tensor_tensor(p_("nr"), p_("mag"), p_("cos"), ALU.mult))
            link(dve.tensor_tensor(p_("ni"), p_("mag"), p_("sin"), ALU.mult))
            link(dve.tensor_scalar(p_("nr"), p_("nr"), 1.0, None, ALU.subtract))
            link(dve.tensor_tensor(p_("t1"), p_("nr"), are, ALU.mult))
            link(dve.tensor_tensor(p_("t2"), p_("ni"), aim, ALU.mult))
            link(dve.tensor_tensor(p_("t1"), p_("t1"), p_("t2"), ALU.add))
            link(dve.tensor_tensor(p_("zr"), p_("t1"), p_("rden"), ALU.mult))
            link(dve.tensor_tensor(p_("t1"), p_("ni"), are, ALU.mult))
            link(dve.tensor_tensor(p_("t2"), p_("nr"), aim, ALU.mult))
            link(dve.tensor_tensor(p_("t1"), p_("t1"), p_("t2"), ALU.subtract))
            link(dve.tensor_tensor(p_("zi"), p_("t1"), p_("rden"), ALU.mult))
            dve.wait_ge(ld["masks"], 32)

            def head_max(kind, n):
                b, h = n % 2, n - HEAD0[kind]
                dve.wait_ge(at_s, n + 1)
                scores = bank[2 + b][:, :]
                if n >= 2:
                    dve.wait_ge(at_pt, n - 1)
                    dve.wait_ge(at_e, n - 1)
                flat = sp[b][:, :, :].rearrange("p t s -> p (t s)")
                if kind == "dil":
                    dve.scalar_tensor_tensor(out=flat, in0=dist[:, :, :].rearrange("p t s -> p (t s)"),
                                             scalar=-(2.0 ** -(h + 1)), in1=scores, op0=ALU.mult, op1=ALU.add)\
                        .then_inc(at_sb, 1)
                    dve.wait_ge(at_sb, n + 1)
                    scores = flat
                elif kind == "na":
                    dve.wait_ge(s_kb, h + 1)
                    dve.scalar_tensor_tensor(out=flat, in0=scores, scalar=HD ** -0.5,
                                             in1=bias[b][:, :, :].rearrange("p t s -> p (t s)"), op0=ALU.mult, op1=ALU.add)\
                        .then_inc(at_sb, 1)
                    dve.wait_ge(at_sb, n + 1)
                    scores = flat
                dve.tensor_reduce(mx[:, b, :], scores.rearrange("p (t s) -> p t s", t=RT), AX.X, ALU.max)\
                    .then_inc(at_mx, 1)
                dve.wait_ge(at_mx, n + 1)
                scale = {"mla": QK ** -0.5, "cross": XHD ** -0.5}.get(kind, 1.0)
                dve.tensor_scalar(negm[:, b, :], mx[:, b, :], -scale, None, ALU.mult).then_inc(at_m, 1)

            def head_sum(kind, n):
                b = n % 2
                dve.wait_ge(at_e, n + 1)
                if kind == "dil":
                    for t in range(RT):
                        ins = dve.scalar_tensor_tensor(out=sp[b][:, t, :], in0=sp[b][:, t, :], scalar=1.0,
                                                       in1=mult[:, t, :], op0=ALU.mult, op1=ALU.mult,
                                                       accum_out=rsum[:, b, t:t + 1])
                    ins.then_inc(at_pm, 1)
                    dve.wait_ge(at_pm, n + 1)
                if n >= 2:
                    dve.wait_ge(at_y, n - 1)
                dve.reciprocal(rden[:, b, :], rsum[:, b, :]).then_inc(at_r, 1)

            def head_pt(n):
                b = n % 2
                dve.wait_ge(at_pt, n + 1)
                if n >= 2:
                    dve.wait_ge(at_o, n - 1)
                dve.tensor_copy(pT[b][:, :, :], bank[4 + b][:, :].rearrange("p (k s) -> p k s", k=2)).then_inc(at_pc, 1)

            def head_rope(kind, n):
                if kind == "mla":
                    dve.wait_ge(at_t, n + 1)
                    dve.wait_ge(at_s, n - 1)
                    dve.tensor_copy(rT[n % 2][:, :], bank[6 + n % 2][0:ROPE, 2 * P:4 * P]).then_inc(at_rope, 1)

            def attend(kind):
                ns = heads(kind)
                head_rope(kind, ns[0])
                head_rope(kind, ns[1])
                head_max(kind, ns[0])
                for n in ns:
                    head_sum(kind, n)
                    if n + 2 in ns:
                        head_rope(kind, n + 2)
                    if n + 1 in ns:
                        head_max(kind, n + 1)
                    head_pt(n)

            attend("dil")
            modulation(1, 64)
            norm_turn("yatt", UNIT0["glu"])

            for c in range(2):
                link(dve.memset(bb[c][:, :, :], 0.0))
            dve.wait_ge(ld["sb"], 32)
            z3 = {c: bcast(p_(c), [1, STILES], [0, GC]) for c in ("zr", "zi")}
            for m, (b_, z) in enumerate(((0, "zr"), (1, "zi"), (1, "zr"), (0, "zi"))):
                link(dve.tensor_tensor(btmp[:, m], bn[b_][:, :, :], z3[z], ALU.mult))
            for c in range(2):
                for g in range(2):
                    rows, cols = slice(64 * g, 64 * g + 64), slice(GC * g, GC * g + GC)
                    ins = dve.tensor_tensor(bb[c][rows, :, cols], btmp[rows, 2 * c], btmp[rows, 2 * c + 1],
                                            (ALU.subtract, ALU.add)[c])
                ins.then_inc(ss_bb, 1)
            dve.wait_ge(ss_bb, 2)
            dve.wait_ge(ld["parity"], 16)
            dve.wait_ge(ld["sc"], 32)
            for c in range(2):
                for g in range(2):
                    ins = dve.tensor_scalar(cc[c][:, :, NST * g:NST * g + NST], cn[c][:, :, :], parity[:, g:g + 1],
                                            (1.0, -1.0)[c], ALU.mult, ALU.mult)
                ins.then_inc(ss_bb, 1)
            dve.wait_ge(ld["iota"], 16)
            dve.wait_ge(ss_btp, 8)

            whole = half[:, :, :].rearrange("p q s -> p (q s)").rearrange("p (w j a) -> p w j a", w=2, a=16)
            flat = [[0, STILES], [16, 16]], [[0, STILES], [1, 16]]
            for w in range(2):
                ins = dve.tensor_tensor(phase[:, w], bcast(head, [1, STILES], [0, 16]), bcast(iota[:, :], *flat[w]), ALU.mult)
            link(ins)
            link(dve.tensor_scalar(whole, phase[:, :, :, :], MAGIC, MAGIC, ALU.add, ALU.subtract))
            link(dve.tensor_tensor(phase[:, :, :, :], phase[:, :, :, :], whole, ALU.subtract))
            for w in range(2):
                ins = dve.tensor_tensor(whole[:, w], bcast(p_("phl"), [1, STILES], [0, 16]), bcast(iota[:, :], *flat[w]),
                                        ALU.mult)
            link(ins)
            link(dve.tensor_tensor(phase[:, :, :, :], phase[:, :, :, :], whole, ALU.add))
            link(dve.tensor_scalar(whole, phase[:, :, :, :], MAGIC, MAGIC, ALU.add, ALU.subtract))
            link(dve.tensor_tensor(phase[:, :, :, :], phase[:, :, :, :], whole, ALU.subtract))
            dve.sem_inc(ss_phase, 1)

            def angles(k):
                dve.wait_ge(ss_add, k + 1)
                link(dve.tensor_scalar(half[:, :, :], turn[:, :, :], MAGIC, MAGIC, ALU.add, ALU.subtract))
                dve.tensor_tensor(turn[:, :, :], turn[:, :, :], half[:, :, :], ALU.subtract).then_inc(ss_ang, 1)

            def cosines(k):
                dve.wait_ge(ss_sin, 2 * k + 2)
                if k >= 2:
                    dve.wait_ge(ss_pp, 16 * (k - 1))
                dve.tensor_scalar(co[k % 2][:, :, :], half[:, :, :], -2.0, 1.0, ALU.mult, ALU.add).then_inc(ss_tab, 1)

            def scan_tile(j):
                q, b, n = j % 4, j % 2, 8 * j
                c_, s_ = co[j // 4 % 2][:, q, :], si[j // 4 % 2][:, q, :]
                br, bi = bank[q][:, 0:S], bank[q][:, S:2 * S]
                mag = par[:, PAR["mag"], j:j + 1].broadcast_to([P, S])

                def step(ins):
                    ins.then_inc(ss_d, 1)

                dve.wait_ge(ss_tab, j // 4 + 1)
                dve.wait_ge(ss_bu, j + 1)
                if j >= 2:
                    dve.wait_ge(ss_pp, 4 * (j - 1))
                step(dve.tensor_tensor(rot[b][:, 0, :], br, c_, ALU.mult))
                step(dve.tensor_tensor(rot[b][:, 1, :], bi, s_, ALU.mult))
                step(dve.tensor_tensor(rot[b][:, 2, :], bi, c_, ALU.mult))
                step(dve.tensor_tensor(rot[b][:, 3, :], br, s_, ALU.mult))
                dve.wait_ge(ss_d, n + 2)
                step(dve.tensor_tensor(rot[b][:, 0, :], rot[b][:, 0, :], rot[b][:, 1, :], ALU.add))
                dve.wait_ge(ss_d, n + 4)
                step(dve.tensor_tensor(rot[b][:, 2, :], rot[b][:, 2, :], rot[b][:, 3, :], ALU.subtract))
                dve.wait_ge(ss_d, n + 5)
                step(dve.tensor_tensor_scan(rot[b][:, 1, :], mag, rot[b][:, 0, :], 0.0, ALU.mult, ALU.add))
                dve.wait_ge(ss_d, n + 6)
                step(dve.tensor_tensor_scan(rot[b][:, 3, :], mag, rot[b][:, 2, :], 0.0, ALU.mult, ALU.add))

            def output(k):
                dve.wait_ge(ss_y, 4 * k + 4)
                if k:
                    dve.wait_ge(ss_gt, k)
                else:
                    dve.wait_ge(ld["gstore"], 16)
                dve.scalar_tensor_tensor(out=yt[:, :], in0=uT[:, k, :], scalar=vec("ssm_d", k), in1=bank[4 + k % 2][:, 0:S],
                                         op0=ALU.mult, op1=ALU.add).then_inc(ss_yt, 1)

            def split_output(k):
                dve.wait_ge(ss_gt, k + 1)
                link(dve.tensor_copy(sa_hi[:, k, :], gt[:, :]))
                dve.tensor_tensor(sa_lo[:, k, :], gt[:, :], sa_hi[:, k, :].bitcast(F32), ALU.subtract).then_inc(ss_g, 1)

            angles(0)
            cosines(0)
            for k in range(8):
                scan_tile(4 * k)
                if k + 1 < 8:
                    angles(k + 1)
                scan_tile(4 * k + 1)
                if k:
                    output(k - 1)
                scan_tile(4 * k + 2)
                if k:
                    split_output(k - 1)
                scan_tile(4 * k + 3)
                if k + 1 < 8:
                    cosines(k + 1)
            output(7)
            split_output(7)

            blk = UNIT0["glu"] // 4
            dve.wait_ge(ss_g, 8)
            for c in range(2):
                pumps(blk, 2 * c, 2)
            for c in range(2):
                kt = slice(4 * c, 4 * c + 4)
                g4 = rtmp[:, :, :].rearrange("p t (k s) -> p (t k) s", s=S)
                link(dve.tensor_tensor(g4, sa_hi[:, kt, :].bitcast(F32), sa_lo[:, kt, :].bitcast(F32), ALU.add))
                dve.wait_ge(acc_free[c], 2 * (CHUNK0["glu"] // 2) + 4)
                link(dve.tensor_tensor(sig[:, kt, :], sig[:, kt, :], g4, ALU.mult))
                link(dve.tensor_copy(y2_hi[:, kt, :], sig[:, kt, :]))
                dve.tensor_tensor(y2_lo[:, kt, :], sig[:, kt, :], y2_hi[:, kt, :].bitcast(F32), ALU.subtract)\
                    .then_inc(gl_y2, 1)
            dve.wait_ge(gl_y2, 2)
            dve.wait_ge(ld["gate1"], 16)
            with dve.Fori(0, 2) as i:
                for c in range(2):
                    blk = UNIT0["out1"] // 4 + i * 2
                    pumps(blk, 4 * c, 4)
                    gated_out(blk, 4 * c + 3, CHUNK0["out1"] // 2 + i, c, i * (2 * CW) + c * CW, gate1_b, i * 2 + c)

            def times_up(blk, hq):
                unit_used(blk, 7)
                dve.wait_ge(acc_free[0], 2 * hq + 4)
                for t in range(RT):
                    dve.tensor_tensor(fg[:, t, :], fg[:, t, :], bank[2 + t][:, :], ALU.mult).then_inc(acc_free[1], 1)

            def hidden_rests(f, k):
                for hf in range(2):
                    dve.wait_ge(ff_hi, 2 * f + hf + 1)
                    ks = bass.ds(k + 2 * hf, 2)
                    dve.tensor_tensor(act_lo[:, ks, :], bank[4 + hf][:, :].rearrange("p (k s) -> p k s", k=2),
                                      act_hi[:, ks, :].bitcast(F32), ALU.subtract).then_inc(ff_lo, 1)

            def ffn(stage, f0, residual):
                blk, hq = UNIT0[stage] // 4, CHUNK0[stage] // 2
                for third, (c0, n) in enumerate(THIRDS):
                    pumps(blk, 0, 8)
                    times_up(blk, hq)
                    with dve.Fori(1, n) as i:
                        pumps(blk + i * 2, 0, 4)
                        hidden_rests(i + (f0 + c0 - 1), i * 4 - 4)
                        pumps(blk + i * 2, 4, 4)
                        times_up(blk + i * 2, hq + i)
                    blk, hq = blk + 2 * n, hq + n
                    for c in range(4):
                        if c == 0:
                            pumps(blk, 0, 1)
                            hidden_rests(f0 + c0 + n - 1, 4 * n - 4)
                            pumps(blk, 1, n - 1)
                        else:
                            pumps(blk, n * c, n)
                        residual(blk, n * c + n - 1, hq, c, c * CW, third, c)
                    blk, hq = blk + n, hq + 2

            norm_turn("h2", UNIT0["ffn1"])
            dve.wait_ge(ld["gate2"], 16)
            ffn("ffn1", 0, lambda blk, j, hq, c, col, third, n:
                gated_out(blk, j, hq, c, col, wide_b, n + (4 + 4 * third)))
            norm_turn("hmix", UNIT0["in2"])
            with dve.Fori(0, 3) as i:
                for c in range(2):
                    blk = UNIT0["in2"] // 4 + i * 2
                    pumps(blk, 4 * c, 4)
                    copy_out(blk, 4 * c + 3, c, proj2[:, 1, bass.ds(i * (2 * CW) + c * CW, CW)])
            blk = UNIT0["in2"] // 4 + 6
            for c in range(2):
                cols = (CW, IN2 - 7 * CW)[c]
                pumps(blk, 4 * c, 4)
                copy_out(blk, 4 * c + 3, c, proj2[:, 1, (6 + c) * CW:(6 + c) * CW + cols], cols)
            norm_turn("cq", UNIT0["uq"])
            norm_turn("ckv", UNIT0["uq"])
            for c in range(4):
                pumps(UNIT0["uq"] // 4, c, 1)
                copy_out(UNIT0["uq"] // 4, c, c, q_mla[:, 1, 2 * c:2 * c + 2, :].rearrange("p a b -> p (a b)"), 2 * QK)
            attend("na")
            for c in range(4):
                pumps(UNIT0["ukv"] // 4, c, 1)
                copy_out(UNIT0["ukv"] // 4, c, c, proj2[:, 1, NA_W + c * CW:NA_W + c * CW + CW])

            def rope(rows, o1, o2, x1, x2, dims):
                cs, sn = (bcast(a[:, :, :], *dims) for a in (ropec, ropes))
                a, b_, c_, d_ = rows
                dve.tensor_tensor(a, x1, cs, ALU.mult)
                dve.tensor_tensor(b_, x2, sn, ALU.mult)
                dve.tensor_tensor(c_, x1, sn, ALU.mult)
                link(dve.tensor_tensor(d_, x2, cs, ALU.mult))
                dve.tensor_tensor(o1, a, b_, ALU.subtract)
                link(dve.tensor_tensor(o2, c_, d_, ALU.add))

            chunks_out(dve, CHUNK0["out2"])
            dve.wait_ge(ld["na_const"], 48)
            dve.wait_ge(at_y, 16)
            q1, q2 = q_mla[:, :, :, NOPE:NOPE + HROPE], q_mla[:, :, :, NOPE + HROPE:QK]
            tq = [a[:, :, :].rearrange("p t (h e) -> p t h e", e=HROPE) for a in (sp[0], sp[1], pT[0], pT[1])]
            rope(tq, q1, q2, q1, q2, ([HROPE, RT], [0, HEADS], [1, HROPE]))
            k1, k2 = proj2[:, :, C_KR:C_KR + HROPE], proj2[:, :, C_KR + HROPE:IN2]
            tk = [a[:, :, 0:HROPE] for a in (sp[0], sp[1], pT[0], pT[1])]
            rope(tk, kr[:, :, 0:HROPE], kr[:, :, HROPE:ROPE], k1, k2, ([HROPE, RT], [1, HROPE]))
            dve.sem_inc(s_kr, 1)
            dve.wait_ge(s_krt, 1)
            dve.tensor_copy(krT[:, :], bank[7][0:ROPE, 2 * P:4 * P]).then_inc(s_krT, 1)
            attend("mla")
            norm_turn("yna", UNIT0["out2"])
            norm_turn("ymla", UNIT0["out2"])

            def add_square(stage):
                with dve.Fori(0, 2) as i:
                    for c in range(2):
                        blk = UNIT0[stage] // 4 + i * 2
                        pumps(blk, 4 * c, 4)
                        add_out(blk, 4 * c + 3, CHUNK0[stage] // 2 + i, c, i * (2 * CW) + c * CW)

            add_square("out2")
            norm_turn("hmem", UNIT0["xq"])
            with dve.Fori(0, 2) as i:
                for c in range(2):
                    blk = UNIT0["xq"] // 4 + i * 2
                    pumps(blk, 4 * c, 4)
                    copy_out(blk, 4 * c + 3, c, xq[:, 1, bass.ds(i * (2 * CW) + c * CW, CW)])
            attend("cross")
            norm_turn("ocross", UNIT0["xo"])
            add_square("xo")
            norm_turn("hffn", UNIT0["ffn2"])
            ffn("ffn2", FCH, lambda blk, j, hq, c, col, third, n: add_out(blk, j, hq, c, col))
            stats("final", STAT0["final"], PAIR0["hffn"] + 8, D)
            dve.wait_ge(ld["final"], 16)
            for t in range(RT):
                dve.scalar_tensor_tensor(out=x[:, t, :], in0=x[:, t, :], scalar=rstd[:, t:t + 1], in1=wide_b[:, :],
                                         op0=ALU.mult, op1=ALU.mult).then_inc(s_fin, 1)


_INS = ["x", "c", "w_ada", "b_ada", "norm1_w", "w_in", "ssm_a_re", "ssm_a_im", "ssm_log_dt", "ssm_b_re", "ssm_b_im",
        "ssm_c_re", "ssm_c_im", "ssm_d", "ssm_w_glu", "q_norm_w", "k_norm_w", "w_out", "norm2_w", "w_ffn_gate",
        "w_ffn_up", "w_ffn_down", "mem_2", "ln_mix_2", "w_in_2", "q_norm_2", "kv_norm_2", "w_uq_2", "w_ukv_2",
        "na_rpb_2", "na_out_norm_2", "mla_out_norm_2", "w_out_2", "ln_mem_2", "mem_norm_2", "w_xq_2", "w_xk_2",
        "w_xv_2", "w_xo_2", "ln_ffn_2", "w_gate_2", "w_up_2", "w_down_2", "final_norm_2"]


def shape_constants():
    import numpy as np

    t, s = np.arange(S)[:, None], np.arange(S)[None, :]
    d = t - s
    count = ((d >= 0) & (d <= 128)).astype(np.float32) + ((d >= 0) & (d % 4 == 0)) + ((d >= 0) & (d % 16 == 0))
    dist = np.where(count > 0, d, 1e33)
    col = np.arange(GRID_W)
    start = np.clip(col - NA_COLS // 2, 0, GRID_W - NA_COLS)[:, None]
    window = (col[None, :] >= start) & (col[None, :] < start + NA_COLS)
    inv = 1.0 / (np.float32(10000.0) ** (np.arange(0, ROPE, 2, dtype=np.float32) / ROPE))
    ang = np.arange(S, dtype=np.float32)[:, None] * inv[None, :].astype(np.float32)
    tables = {"dist": dist, "mult": count, "colmask": np.tile(np.where(window, 0.0, -1e30), (2, NA_ROWS)),
              "cos": np.cos(ang), "sin": np.sin(ang), "iota": np.tile(np.arange(S), (P, 1)),
              "parity": np.stack([np.arange(P) // GC % 2 == 0, np.arange(P) // GC % 2 == 1], 1)}
    return {"const_" + n: np.ascontiguousarray(a, dtype=np.float32) for n, a in tables.items()}


def kernel(**inputs):
    import numpy as np
    import concourse.bacc as bacc
    from concourse.bass_utils import run_bass_kernel_spmd

    nc = bacc.Bacc("TRN2", target_bir_lowering=False, num_devices=1)
    arrays = {"in_" + n: np.ascontiguousarray(inputs[n]) for n in _INS}
    arrays.update(shape_constants())
    aps = {n: nc.dram_tensor(n, a.shape, mybir.dt.from_np(a.dtype), kind="ExternalInput").ap() for n, a in arrays.items()}
    out = nc.dram_tensor("out", (1, S, D), F32, kind="ExternalOutput").ap()
    build(nc, {n.removeprefix("in_"): a for n, a in aps.items()}, out)
    r = run_bass_kernel_spmd(nc, [arrays], core_ids=[0])
    return r.results[0]["out"]
```

```python
from contextlib import ExitStack

import concourse.bass as bass
from concourse import mybir
from concourse.alu_op_type import AluOpType as ALU

F32 = mybir.dt.float32
F32R = mybir.dt.float32r
BF16 = mybir.dt.bfloat16
ACT = mybir.ActivationFunctionType
AX = mybir.AxisListType

P = 128
D = 2048
S = 256
RT = S // P
KD = D // P
CW = 512
UK = 4
RING = 4
LOOKAHEAD = 3
EPS = 1e-6

SSM_W = 1024
GROUPS, GC, NST = 64, 16, 64
STILES = GROUPS * NST // P
HEADS, HD = 8, 128
X_HEADS, XHD = 4, 512
XKT = XHD // P
FF = 5632
FCH = FF // CW
THIRDS = ((0, 4), (4, 4), (8, 3))
GRID_W, NA_ROWS, NA_COLS, NA_RMAX = 64, 4, 16, 8
NA_DR, NA_DC = 2 * NA_RMAX - 1, 2 * NA_COLS - 1
TOEP_W = 128
TOEP_AT = (GRID_W - 1) - (NA_COLS - 1)
NOPE, ROPE, VD = 128, 64, 128
HROPE = ROPE // 2
QK = NOPE + ROPE
Q_RANK, KV_RANK = 512, 256
NA_W = 1024
IN2 = 3 * NA_W + Q_RANK + KV_RANK + ROPE
C_Q = 3 * NA_W
C_KV = C_Q + Q_RANK
C_KR = C_KV + KV_RANK
TWO_PI = 6.283185307179586
PI_HEAD = 6.28125
PI_REST = TWO_PI - PI_HEAD
MAGIC = 12582912.0

VECS = (("norm1_w", 16), ("norm2_w", 16), ("ln_mix_2", 16), ("ln_mem_2", 16), ("mem_norm_2", 16), ("ln_ffn_2", 16),
        ("na_out_norm_2", 8), ("mla_out_norm_2", 8), ("ssm_d", 8), ("q_norm_2", 4), ("kv_norm_2", 2),
        ("q_norm_w", 1), ("k_norm_w", 1))
VAT = {}
_at = 0
for _n, _k in VECS:
    VAT[_n] = _at
    _at += _k

NT = dict(mem=(16, 2), h1=(16, 1), yatt=(8, 0), h2=(16, 1), hmix=(16, 2), cq=(4, 1), ckv=(2, 1), yna=(8, 1),
          ymla=(8, 1), hmem=(16, 2), ocross=(16, 0), hffn=(16, 2))
PAIR0, STAT0, XN0, HEADS0 = {}, {}, {}, {}
_p = _s = _x = _h = 0
for _n, (_k, _how) in NT.items():
    PAIR0[_n], STAT0[_n], XN0[_n], HEADS0[_n] = _p, _s, _x, _h
    _p += _k // 2
    _s += _how > 0
    _x += (_how == 1) * (_k // 2)
    _h += (_how > 0) * (_k // 2)
STAT0["final"] = _s
PLAIN_PAIRS = [PAIR0[n] + j for n, (k, st) in NT.items() if not st for j in range(k // 2)]

UNIT0, CHUNK0 = {}, {}
_u = _q = 0
for _n, _uu, _qq in (("xk_ada", 48, 4), ("xv", 16, 4), ("in_ada", 96, 8), ("glu", 4, 2), ("out1", 16, 4),
                     ("ffn1", 132, 34), ("in2", 32, 8), ("uq", 4, 4), ("ukv", 4, 4), ("out2", 16, 4),
                     ("xq", 16, 4), ("xo", 16, 4), ("ffn2", 132, 34)):
    UNIT0[_n], CHUNK0[_n] = _u, _q
    _u += _uu
    _q += _qq
UNITS, CHUNKS = _u, _q
HEAD0 = dict(dil=0, na=8, mla=16, cross=24)
ARENA = 207 * 1024 + 512
UNIT0["end"], CHUNK0["end"] = UNITS, CHUNKS
PAR = {n: i for i, n in enumerate(
    "dt ard mag th k r sin sh sh2 phl den rden cos nr ni t1 t2 zr zi".split())}


def build(nc, A, out):
    with ExitStack() as ctx:
        base = (nc.sbuf_base + 63) // 64 * 64
        size = ARENA
        ctx.enter_context(nc.sbuf_tensor("arena", [P, size // 4 + 16], F32))

        def sb(name, offset, shape, dt=F32):
            count = 1
            for n in shape[1:]:
                count *= n
            assert offset + count * (2 if dt == BF16 else 4) <= size, name
            return nc.alloc_sbuf_tensor_at(name, shape, dt, offset=base + offset)

        KB = 1024
        raw = [sb(f"raw{s}", 8 * KB * s, [P, UK, CW]) for s in range(RING)]
        whi = [sb(f"whi{s}", 8 * KB * (4 + s), [P, UK, CW], F32R) for s in range(RING)]
        wlo = [sb(f"wlo{s}", 8 * KB * (8 + s), [P, UK, CW], F32R) for s in range(RING)]
        x = sb("x", 96 * KB, [P, RT, D])
        sa_hi = sb("sa_hi", 112 * KB, [P, 8, S], F32R)
        sa_lo = sb("sa_lo", 120 * KB, [P, 8, S], F32R)
        s2_hi = sb("s2_hi", 128 * KB, [P, 8, S], F32R)
        s2_lo = sb("s2_lo", 136 * KB, [P, 8, S], F32R)
        qkT = [sb(f"qkT{b}", (128 + 2 * b) * KB, [P, 2, S]) for b in range(2)]
        xqT = sb("xqT", 128 * KB, [P, XKT, S])
        sp = [sb(f"sp{b}", (132 + 2 * b) * KB, [P, RT, S]) for b in range(2)]
        pT = [sb(f"pT{b}", (136 + 2 * b) * KB, [P, RT, S]) for b in range(2)]
        rT = [sb(f"rT{b}", (140 + b) * KB, [ROPE, S]) for b in range(2)]
        sqs = sb("sqs", 148 * KB, [P, SSM_W])
        sqj = sb("sqj", 145 * KB + 512, [P, HEADS, HD], BF16)
        krT = sb("krT", 142 * KB, [ROPE, S])
        xn = [sb(f"xn{b}", (144 + 2 * b) * KB, [P, RT, 2 * P]) for b in range(2)]
        full = [sb(f"full{b}", (148 + 2 * b) * KB, [P, 2, S]) for b in range(2)]
        junk = sb("junk", 144 * KB, [P, RT, D], BF16)
        at = [152 * KB]

        def small(name, shape, dt=F32):
            count = 1
            for n in shape[1:]:
                count *= n
            t = sb(name, at[0], shape, dt)
            at[0] += (4 * count + 31) // 32 * 32
            return t

        ident = small("ident", [P, P])
        vcol = small("vcol", [P, P])
        modc = small("modc", [P, 96])
        scol = [small(f"scol{b}", [P, KD]) for b in range(2)]
        ccol = small("ccol", [P, 2 * KD + P], F32R)
        qscol = small("qscol", [P, 1])
        ss = small("ss", [P, RT])
        var = small("var", [P, RT])
        rstd = small("rstd", [P, RT])
        neghalf = small("neghalf", [P, 2 * RT * HEADS])
        mx = small("mx", [P, 2, RT])
        negm = small("negm", [P, 2, RT])
        rsum = small("rsum", [P, 2, RT])
        rden = small("rden", [P, 2, RT])
        qk_ss = small("qk_ss", [P, RT, 2 * HEADS])
        qk_rs = small("qk_rs", [P, RT, 2 * HEADS])
        parity = small("parity", [P, 2])
        PH = 155 * KB + 512
        assert at[0] <= PH, at[0]
        mem = sb("mem", PH, [P, RT, D])
        kvst = [sb(f"kvst{b}", PH + (16 + 4 * b) * KB, [P, RT, CW]) for b in range(2)]
        vrow = sb("vrow", PH + 24 * KB, [P, P])
        crow = sb("crow", PH + 25 * KB, [KD, P])
        csil = sb("csil", PH + 26 * KB, [KD, P])
        cT = sb("cT", PH + 27 * KB, [P, KD])
        adast = [sb(f"adast{b}", PH + (44 + 2 * b) * KB, [2, CW]) for b in range(2)]
        mrow = [sb(f"mrow{n}", PH + (48 + n) * KB, [64, 2, P]) for n in range(2)]
        mbias = [sb(f"mbias{n}", PH + 50 * KB + 512 * n, [64, P]) for n in range(2)]
        proj = sb("proj", PH, [P, RT, 4 * SSM_W])
        uT = sb("uT", PH + 32 * KB, [P, 8, S])
        dist = sb("dist", PH + 40 * KB, [P, RT, S])
        mult = sb("mult", PH + 42 * KB, [P, RT, S])
        bt = [sb(f"bt{c}", PH + 4 * KB * c, [P, 8, P]) for c in range(2)]
        ct = [sb(f"ct{c}", PH + (8 + 4 * c) * KB, [P, 8, P]) for c in range(2)]
        bb = [sb(f"bb{c}", 8 * KB * 7 + 4 * KB * c, [P, STILES, 2 * GC]) for c in range(2)]
        bn = [sb(f"bn{c}", (8 * 11 + 2 * c) * KB, [P, STILES, GC]) for c in range(2)]
        cn = [sb(f"cn{c}", (8 * 11 + 4 + 2 * c) * KB, [P, 8, NST]) for c in range(2)]
        cc = [sb(f"cc{c}", PH + (40 + 4 * c) * KB, [P, 8, P]) for c in range(2)]
        btmp = sb("btmp", PH + 40 * KB, [P, 4, STILES, GC])
        turn = sb("turn", PH + 16 * KB, [P, 4, S])
        half = sb("half", PH + 20 * KB, [P, 4, S])
        co = [sb("co0", PH + 24 * KB, [P, 4, S]), sb("co1", 8 * KB * 7, [P, 4, S])]
        si = [sb("si0", PH + 28 * KB, [P, 4, S]), sb("si1", 8 * KB * 7 + 4 * KB, [P, 4, S])]
        prod = [sb(f"prod{b}", 8 * KB * 11 + 4 * KB * b, [P, 4, S]) for b in range(2)]
        rot = [sb(f"rot{b}", PH + (40 + 4 * b) * KB, [P, 4, S]) for b in range(2)]
        iota = sb("iota", PH + 48 * KB, [P, S])
        cneg = [sb(f"cneg{b}", PH + 51 * KB + 512 * b, [P, P]) for b in range(2)]
        yt = sb("yt", PH + 49 * KB, [P, S])
        gt = sb("gt", PH + 50 * KB, [P, S])
        SP_ = 144 * KB
        srow = sb("srow", SP_, [96, P])
        dtr = sb("dtr", SP_ + 512, [96, 2])
        scolp = sb("scolp", SP_ + 1024, [P, 96])
        par = sb("par", SP_ + 3 * 512, [P, len(PAR), STILES])
        phh = sb("phh", SP_ + 4 * KB - 128, [P, STILES], F32R)
        phase = sb("phase", SP_ + 4 * KB, [P, 2, STILES, 16])
        y2_hi = sb("y2_hi", PH, [P, 8, S], F32R)
        y2_lo = sb("y2_lo", PH + 8 * KB, [P, 8, S], F32R)
        sig = sb("sig", PH + 16 * KB, [P, 8, S])
        gate1_b = sb("gate1_b", PH + 24 * KB, [P, D])
        act_hi = sb("act_hi", PH, [P, 16, S], F32R)
        act_lo = sb("act_lo", PH + 16 * KB, [P, 16, S], F32R)
        fg = sb("fg", PH + 32 * KB, [P, RT, CW])
        rtmp = sb("rtmp", PH + 40 * KB, [P, RT, CW])
        wide_b = sb("wide_b", PH + 44 * KB, [P, D])
        proj2 = sb("proj2", PH, [P, RT, IN2])
        q_mla = sb("q_mla", PH + 31 * KB, [P, RT, HEADS, QK])
        bias = [sb(f"bias{b}", PH + (43 + 2 * b) * KB, [P, RT, S]) for b in range(2)]
        colmask = sb("colmask", PH + 47 * KB, [P, S])
        ropec = sb("ropec", PH + 48 * KB, [P, RT, HROPE])
        ropes = sb("ropes", PH + 48 * KB + 256, [P, RT, HROPE])
        zrow = sb("zrow", PH + 48 * KB + 512, [HEADS * NA_DR, TOEP_W])
        kr = sb("kr", PH + 49 * KB, [P, RT, ROPE])
        xq = sb("xq", PH, [P, RT, D])
        xkT = sb("xkT", PH + 16 * KB, [P, KD, S])
        xkv = sb("xkv", PH + 32 * KB, [P, RT, D])

        bank = [ctx.enter_context(nc.psum_tensor(f"bank{i}", [P, CW], F32)) for i in range(8)]

        scr_k = nc.dram_tensor("scr_k", (S, D), F32).ap().rearrange("(t p) n -> p t n", p=P)
        scr_v = nc.dram_tensor("scr_v", (S, D), F32).ap().rearrange("(t p) n -> p t n", p=P)
        scr_ada = nc.dram_tensor("scr_ada", (2, 6 * D), F32).ap()
        scr_gate = nc.dram_tensor("scr_gate", (64, P), F32).ap()
        scr_toep = nc.dram_tensor("scr_toep", (HEADS * GRID_W, NA_DR * GRID_W), F32).ap()
        scr_rpb = nc.dram_tensor("scr_rpb", (HEADS * NA_DR, TOEP_W), F32).ap()

        def sem(name):
            return ctx.enter_context(nc.semaphore(name))

        landed = [sem(f"landed{s}") for s in range(RING)]
        hi_done = sem("hi_done")
        lo_done = sem("lo_done")
        used = sem("used")
        acc_free = [sem(f"acc_free{p}") for p in range(2)]
        x_updated = sem("x_updated")
        ada_free = [sem(f"ada_free{b}") for b in range(2)]
        adast_free = [sem(f"adast_free{b}") for b in range(2)]
        kvst_free = [sem(f"kvst_free{b}") for b in range(2)]
        squares_summed = [sem(f"squares_summed{b}") for b in range(2)]
        variance_ready = sem("variance_ready")
        rstd_ready = sem("rstd_ready")
        rows_normed = sem("rows_normed")
        norm_turned = sem("norm_turned")
        norm_scaled = sem("norm_scaled")
        norm_heads = sem("norm_heads")
        norm_split = sem("norm_split")
        plain_turned = sem("plain_turned")
        plain_copied = sem("plain_copied")
        qk_turned = sem("qk_turned")
        qk_copied = sem("qk_copied")
        rope_copied = sem("rope_copied")
        scores_ready = sem("scores_ready")
        biased_scores = sem("biased_scores")
        maxima_ready = sem("maxima_ready")
        negmax_ready = sem("negmax_ready")
        exp_ready = sem("exp_ready")
        probs_counted = sem("probs_counted")
        recip_ready = sem("recip_ready")
        probs_turned = sem("probs_turned")
        probs_copied = sem("probs_copied")
        values_ready = sem("values_ready")
        head_written = sem("head_written")
        ident_ready = sem("ident_ready")
        neghalf_ready = sem("neghalf_ready")
        vec_turned = sem("vec_turned")
        vcol_ready = sem("vcol_ready")
        silu_c_ready = sem("silu_c_ready")
        c_turned = sem("c_turned")
        c_column = sem("c_column")
        c_split = sem("c_split")
        mod_rows = sem("mod_rows")
        mod_turned = sem("mod_turned")
        mod_columns = sem("mod_columns")
        tile0_squares = sem("tile0_squares")
        qk_variance = sem("qk_variance")
        qk_rstd = sem("qk_rstd")
        qk_normed = sem("qk_normed")
        key_rotated = sem("key_rotated")
        key_turned = sem("key_turned")
        key_copied = sem("key_copied")
        bias_masked = sem("bias_masked")
        zeros_ready = sem("zeros_ready")
        out_rows_ready = sem("out_rows_ready")
        out_stored = sem("out_stored")
        link_done = sem("link_done")
        ssm_rows = sem("ssm_rows")
        ssm_rows_turned = sem("ssm_rows_turned")
        ssm_columns = sem("ssm_columns")
        ssm_exps = sem("ssm_exps")
        ssm_angles = sem("ssm_angles")
        bc_ready = sem("bc_ready")
        bc_turned = sem("bc_turned")
        bc_copied = sem("bc_copied")
        phase_ready = sem("phase_ready")
        angles_added = sem("angles_added")
        angles_reduced = sem("angles_reduced")
        sines_ready = sem("sines_ready")
        cosines_ready = sem("cosines_ready")
        drive_ready = sem("drive_ready")
        scan_steps = sem("scan_steps")
        products_ready = sem("products_ready")
        cneg_ready = sem("cneg_ready")
        readout_ready = sem("readout_ready")
        y_ready = sem("y_ready")
        gelu_ready = sem("gelu_ready")
        y_split = sem("y_split")
        gated_y_split = sem("gated_y_split")
        hidden_turned = sem("hidden_turned")
        hidden_hi_done = sem("hidden_hi_done")
        hidden_lo_done = sem("hidden_lo_done")
        ld = {n: sem("ld_" + n) for n in (
            "x", "mem", "vec", "c", "mrow0", "mrow1", "masks", "spar", "sdt", "sb", "sc", "iota", "gate1", "gate2",
            "rpb1", "rpb2", "toep", "bias0", "bias1", "na_const", "xk", "xv", "final", "parity", "gstore")}

        def sa(k):
            return (sa_hi[:, k, :], sa_lo[:, k, :]) if k < 8 else (s2_hi[:, k - 8, :], s2_lo[:, k - 8, :])

        def vec(name, k=0):
            return vcol[:, VAT[name] + k:VAT[name] + k + 1]

        def chunks_out(eng, q):
            eng.wait_ge(acc_free[0], 2 + 2 * ((q + 1) // 2))
            eng.wait_ge(acc_free[1], 2 + 2 * (q // 2))

        NTSRC = {
            "mem": lambda t, c, w: mem[:, t, c:c + w], "h1": lambda t, c, w: x[:, t, c:c + w],
            "yatt": lambda t, c, w: proj[:, t, SSM_W + c:SSM_W + c + w],
            "cq": lambda t, c, w: proj2[:, t, C_Q + c:C_Q + c + w],
            "ckv": lambda t, c, w: proj2[:, t, C_KV + c:C_KV + c + w],
            "yna": lambda t, c, w: proj2[:, t, c:c + w],
            "ymla": lambda t, c, w: q_mla[:, t, c // VD:(c + w) // VD, 0:VD],
            "ocross": lambda t, c, w: xq[:, t, c:c + w]}
        for n in ("h2", "hmix", "hmem", "hffn", "final"):
            NTSRC[n] = NTSRC["h1"]
        NTSCALE = {"mem": "mem_norm_2", "hmix": "ln_mix_2", "cq": "q_norm_2", "ckv": "kv_norm_2",
                   "yna": "na_out_norm_2", "ymla": "mla_out_norm_2", "hmem": "ln_mem_2", "hffn": "ln_ffn_2"}
        NTK0 = {"yatt": 8, "ckv": 4, "ymla": 8}

        QKSRC = {
            "dil": [lambda t, h, w=w: proj[:, t, SSM_W * w + h * HD:SSM_W * w + h * HD + HD] for w in (1, 2)],
            "na": [lambda t, h, w=w: proj2[:, t, NA_W * w + h * HD:NA_W * w + h * HD + HD] for w in (0, 1)],
            "mla": [lambda t, h: q_mla[:, t, h, 0:NOPE],
                    lambda t, h: proj2[:, t, NA_W + h * (NOPE + VD):NA_W + h * (NOPE + VD) + NOPE]]}
        VSRC = {
            "dil": lambda t, h: proj[:, t, 3 * SSM_W + h * HD:3 * SSM_W + h * HD + HD],
            "na": lambda t, h: proj2[:, t, 2 * NA_W + h * HD:2 * NA_W + h * HD + HD],
            "mla": lambda t, h: proj2[:, t, NA_W + h * (NOPE + VD) + NOPE:NA_W + (h + 1) * (NOPE + VD)],
            "cross": lambda t, h: xkv[:, t, h * XHD:h * XHD + XHD]}
        YDST = {"dil": QKSRC["dil"][0], "na": QKSRC["na"][0], "mla": QKSRC["mla"][0],
                "cross": lambda t, h: xq[:, t, h * XHD:h * XHD + XHD]}

        block = ctx.enter_context(nc.Block())

        def bcast(ap, *dims):
            return bass.AP(ap.tensor, ap.offset, [list(ap.ap[0])] + [list(d) for d in dims])

        def src_ready(eng, name):
            if name == "mem":
                eng.wait_ge(ld["mem"], 16)
            elif name == "h1":
                eng.wait_ge(ld["x"], 16)
            elif name in ("yatt", "yna", "ymla", "ocross"):
                eng.wait_ge(head_written, {"yatt": 8, "yna": 16, "ymla": 24, "ocross": 28}[name])
            elif name == "h2":
                eng.wait_ge(x_updated, 2 + 2 * 4)
            elif name == "hmix":
                eng.wait_ge(x_updated, 2 + 2 * 4 + 2 * 12)
            else:
                chunks_out(eng, CHUNK0[{"cq": "uq", "ckv": "uq", "hmem": "xq", "hffn": "ffn2", "final": "end"}[name]])

        def heads(kind):
            return range(HEAD0[kind], HEAD0[kind] + (X_HEADS if kind == "cross" else HEADS))

        @block.sync
        def _(sp_):
            sp_.dma_start(mem[:, :, :], A["mem_2"].rearrange("b (t p) n -> p (b t) n", p=P)).then_inc(ld["mem"], 16)
            sp_.dma_start(crow[:, :], A["c"].rearrange("b (k p) -> (b k) p", p=P)).then_inc(ld["c"], 16)
            for name, k in VECS:
                w = A[name]
                flat = bass.AP(w.tensor, w.offset, [[P, k], [1, P]])
                sp_.dma_start(vrow[VAT[name]:VAT[name] + k, :], flat).then_inc(ld["vec"], 16)

            def kview(name):
                w = A[name]
                return w.rearrange("d (k p) n -> p (d k) n", p=P)

            def load(blk, j, w, k, kt, col, cols):
                u = 4 * blk + j
                src = w[:, k:k + kt, bass.ds(col, cols)]
                sp_.wait_ge(lo_done, u + 1)
                sp_.dma_start(raw[j % RING][:, 0:kt, 0:cols], src).then_inc(landed[j % RING], 16)

            def load_chunk(blk, j, w, col, units=4, cols=CW, kt=UK, k0=0):
                for n in range(units):
                    load(blk, j + n, w, k0 + n * kt, kt, col, cols)

            def load_with_ada(blk, j, w, col, col_a):
                for n in range(4):
                    load(blk, j + 3 * n, w, n * UK, UK, col, CW)
                    for a in range(2):
                        load(blk, j + 3 * n + 1 + a, ada, n * UK, UK, col_a + a * CW, CW)

            ada, wk, wv = kview("w_ada"), kview("w_xk_2"), kview("w_xv_2")
            with sp_.Fori(0, 2) as i:
                blk = UNIT0["xk_ada"] // 4 + i * 6
                for c in range(2):
                    load_with_ada(blk, 12 * c, wk, i * (2 * CW) + c * CW, i * (4 * CW) + 2 * c * CW)
            sp_.dma_start(x[:, :, :], A["x"].rearrange("b (t p) n -> p (b t) n", p=P)).then_inc(ld["x"], 16)
            with sp_.Fori(0, 2) as i:
                for c in range(2):
                    load_chunk(UNIT0["xv"] // 4 + i * 2, 4 * c, wv, i * (2 * CW) + c * CW)
            w = kview("w_in")
            with sp_.Fori(0, 4) as i:
                blk = UNIT0["in_ada"] // 4 + i * 6
                for c in range(2):
                    load_with_ada(blk, 12 * c, w, i * (2 * CW) + c * CW, i * (4 * CW) + (8 + 2 * c) * CW)
            w = kview("ssm_w_glu")
            for c in range(2):
                load_chunk(UNIT0["glu"] // 4, 2 * c, w, c * CW, units=2)

            def square(stage, name, order=(0, 1, 2, 3)):
                w = kview(name)
                for c in range(4):
                    for n, m in enumerate(order):
                        load(UNIT0[stage] // 4, 4 * c + n, w, m * UK, UK, c * CW, CW)

            def ffn(stage, gate, up, down):
                g, u, dn = kview(gate), kview(up), kview(down)
                blk = UNIT0[stage] // 4
                for c0, n in THIRDS:
                    with sp_.Fori(0, n) as i:
                        load_chunk(blk + i * 2, 0, g, i * CW + c0 * CW)
                        load_chunk(blk + i * 2, 4, u, i * CW + c0 * CW)
                    blk += 2 * n
                    if n == 4:
                        with sp_.Fori(0, 2) as i:
                            for c in range(2):
                                load_chunk(blk + i * 2, 4 * c, dn, i * (2 * CW) + c * CW, k0=4 * c0)
                    else:
                        for c in range(4):
                            load_chunk(blk, n * c, dn, c * CW, units=n, k0=4 * c0)
                    blk += n

            square("out1", "w_out", (2, 3, 0, 1))
            ffn("ffn1", "w_ffn_gate", "w_ffn_up", "w_ffn_down")
            w = kview("w_in_2")
            with sp_.Fori(0, 3) as i:
                for c in range(2):
                    load_chunk(UNIT0["in2"] // 4 + i * 2, 4 * c, w, i * (2 * CW) + c * CW)
            load_chunk(UNIT0["in2"] // 4 + 6, 0, w, 6 * CW)
            load_chunk(UNIT0["in2"] // 4 + 6, 4, w, 7 * CW, cols=IN2 - 7 * CW)
            w = kview("w_uq_2")
            for c in range(4):
                load_chunk(UNIT0["uq"] // 4, c, w, c * 2 * QK, units=1, cols=2 * QK)
            w = kview("w_ukv_2")
            for c in range(4):
                load_chunk(UNIT0["ukv"] // 4, c, w, c * CW, units=1, kt=2)
            square("out2", "w_out_2")
            square("xq", "w_xq_2")
            square("xo", "w_xo_2")
            ffn("ffn2", "w_gate_2", "w_up_2", "w_down_2")
            for t in range(RT):
                sp_.wait_ge(out_rows_ready, t + 1)
                sp_.dma_start(out[0, t * P:t * P + P, :], x[:, t, :]).then_inc(out_stored, 16)
            sp_.wait_ge(out_stored, 16 * RT)
            for b in range(2):
                sp_.wait_ge(adast_free[b], 16 + 16 * 12)
                sp_.wait_ge(kvst_free[b], 16 + 16 * 4)
            sp_.wait_ge(ld["gstore"], 16)
            sp_.wait_ge(ld["toep"], 16 * HEADS)

        @block.gpsimd
        def _(pool):
            pool.memset(ident[:, :], 0.0).then_inc(ident_ready, 1)
            pool.memset(neghalf[:, :], -0.5).then_inc(neghalf_ready, 1)
            pool.wait_ge(ident_ready, 1)
            pool.affine_select(out=ident[:, :], in_=ident[:, :], compare_op=ALU.not_equal, fill=1.0, base=0,
                               pattern=[[-1, P]], channel_multiplier=1).then_inc(ident_ready, 1)
            pool.wait_ge(neghalf_ready, 1)
            pool.dma_start(parity[:, :], A["const_parity"]).then_inc(ld["parity"], 16)
            bias_rows = A["b_ada"].rearrange("d (r f) -> (d r) f", f=P)
            ada_rows = scr_ada.rearrange("c (r f) -> r c f", f=P)
            pool.dma_start(mbias[0][0:32, :], bias_rows[0:32, :]).then_inc(ld["mrow0"], 16)
            pool.dma_start(mbias[1][:, :], bias_rows[32:96, :]).then_inc(ld["mrow1"], 16)

            def power(n):
                pool.wait_ge(variance_ready, n + 1)
                pool.tensor_tensor(rstd[:, :], var[:, :], neghalf[:, 0:RT], ALU.pow).then_inc(rstd_ready, 1)

            power(STAT0["mem"])
            for b in range(2):
                pool.wait_ge(adast_free[b], 16 + 16 * 4)
            pool.dma_start(mrow[0][0:32, :, :], ada_rows[0:32, :, :]).then_inc(ld["mrow0"], 16)
            power(STAT0["h1"])
            pool.wait_ge(norm_split, PAIR0["yatt"])
            pool.dma_start(dist[:, :, :], A["const_dist"].rearrange("(t p) n -> p t n", p=P)).then_inc(ld["masks"], 16)
            pool.dma_start(mult[:, :, :], A["const_mult"].rearrange("(t p) n -> p t n", p=P)).then_inc(ld["masks"], 16)
            for n, name in enumerate(("ssm_a_re", "ssm_a_im")):
                a = A[name]
                pool.dma_start(srow[32 * n:32 * n + 32, :], bass.AP(a.tensor, a.offset, [[P, 32], [1, P]]))\
                    .then_inc(ld["spar"], 16)
            pool.dma_start(dtr[64:96, :], A["ssm_log_dt"].rearrange("d (t g) -> (d t) g", g=2)).then_inc(ld["sdt"], 16)
            pool.dma_start(iota[:, :], A["const_iota"]).then_inc(ld["iota"], 16)
            pool.wait_ge(qk_variance, 1)
            pool.tensor_tensor(qk_rs[:, :, :].rearrange("p t h -> p (t h)"), qk_ss[:, :, :].rearrange("p t h -> p (t h)"),
                               neghalf[:, :], ALU.pow).then_inc(qk_rstd, 1)
            for b in range(2):
                pool.wait_ge(adast_free[b], 16 + 16 * 12)
            pool.dma_start(mrow[1][:, :, :], ada_rows[32:96, :, :]).then_inc(ld["mrow1"], 16)

            def add_angles(k):
                if k:
                    pool.wait_ge(sines_ready, 2 * k)
                j = slice(4 * k, 4 * k + 4)
                pool.tensor_tensor(turn[:, :, :].rearrange("p q (a b) -> p q a b", b=16),
                                   bcast(phase[:, 0, j, :], [16, 4], [1, 16], [0, 16]),
                                   bcast(phase[:, 1, j, :], [16, 4], [0, 16], [1, 16]), ALU.add).then_inc(angles_added, 1)

            pool.wait_ge(used, RING + UNIT0["glu"])
            for n, name in enumerate(("ssm_b_re", "ssm_b_im")):
                a = A[name]
                pool.dma_start(bn[n][:, :, :], bass.AP(a.tensor, a.offset, [[GC, P], [P * GC, STILES], [1, GC]]))\
                    .then_inc(ld["sb"], 16)
            for n, name in enumerate(("ssm_c_re", "ssm_c_im")):
                a = A[name]
                pool.dma_start(cn[n][:, :, :], bass.AP(a.tensor, a.offset, [[NST, P], [P * NST, 8], [1, NST]]))\
                    .then_inc(ld["sc"], 16)
            pool.wait_ge(phase_ready, 1)
            add_angles(0)
            pool.wait_ge(mod_rows, 2)
            pool.dma_start(scr_gate, mrow[1][:, 0, :]).then_inc(ld["gstore"], 16)

            def turn_forward(j):
                k, q, b = j // 4, j % 4, j % 2
                c_, s_ = co[k % 2][:, q, :], si[k % 2][:, q, :]
                pool.wait_ge(cosines_ready, k + 1)
                if j >= 2:
                    pool.wait_ge(readout_ready, j - 1)
                pool.wait_ge(scan_steps, 8 * j + 7)
                pool.tensor_tensor(prod[b][:, 0, :], rot[b][:, 1, :], c_, ALU.mult).then_inc(products_ready, 1)
                pool.tensor_tensor(prod[b][:, 2, :], rot[b][:, 1, :], s_, ALU.mult).then_inc(products_ready, 1)
                pool.wait_ge(scan_steps, 8 * j + 8)
                pool.tensor_tensor(prod[b][:, 1, :], rot[b][:, 3, :], s_, ALU.mult).then_inc(products_ready, 1)
                pool.tensor_tensor(prod[b][:, 3, :], rot[b][:, 3, :], c_, ALU.mult).then_inc(products_ready, 1)

            for j in range(STILES):
                if j % 4 == 0 and j + 4 < STILES:
                    add_angles(j // 4 + 1)
                turn_forward(j)
            pool.wait_ge(ld["gstore"], 16)
            pool.wait_ge(y_split, 8)
            pool.dma_start(gate1_b[:, :], bass.AP(scr_gate.tensor, scr_gate.offset, [[0, P], [1, D]]))\
                .then_inc(ld["gate1"], 16)
            power(STAT0["h2"])
            pool.dma_start(wide_b[:, :], bass.AP(scr_gate.tensor, scr_gate.offset + 48 * P, [[0, P], [1, D]]))\
                .then_inc(ld["gate2"], 16)
            power(STAT0["hmix"])
            pool.wait_ge(x_updated, 2 + 2 * 16)
            pool.memset(zrow[:, :], 0.0).then_inc(zeros_ready, 1)
            pool.wait_ge(zeros_ready, 1)
            pool.dma_start(zrow[:, TOEP_AT:TOEP_AT + NA_DC], A["na_rpb_2"].rearrange("d h r c -> (d h r) c"))\
                .then_inc(ld["rpb1"], 16)
            pool.wait_ge(ld["rpb1"], 16)
            pool.dma_start(scr_rpb, zrow[:, :]).then_inc(ld["rpb2"], 16)
            pool.wait_ge(ld["rpb2"], 16)
            for h in range(HEADS):
                pool.dma_start(bass.AP(scr_toep.tensor, scr_toep.offset + h * GRID_W * NA_DR * GRID_W,
                                       [[GRID_W, NA_DR], [NA_DR * GRID_W, GRID_W], [1, GRID_W]]),
                               bass.AP(scr_rpb.tensor, scr_rpb.offset + h * NA_DR * TOEP_W + GRID_W - 1,
                                       [[TOEP_W, NA_DR], [-1, GRID_W], [1, GRID_W]])).then_inc(ld["toep"], 16)
            pool.dma_start(colmask[:, :], A["const_colmask"]).then_inc(ld["na_const"], 16)
            pool.dma_start(ropec[:, :, :], A["const_cos"].rearrange("(t p) n -> p t n", p=P)).then_inc(ld["na_const"], 16)
            pool.dma_start(ropes[:, :, :], A["const_sin"].rearrange("(t p) n -> p t n", p=P)).then_inc(ld["na_const"], 16)
            pool.wait_ge(ld["na_const"], 48)
            pool.wait_ge(ld["toep"], 16 * HEADS)

            def bias_load(h):
                n, b = HEAD0["na"] + h, h % 2
                if h >= 2:
                    pool.wait_ge(biased_scores, n - 1)
                for r in range(2):
                    first = (h * GRID_W * NA_DR + NA_RMAX - 1 - r) * GRID_W
                    pool.dma_start(bias[b][GRID_W * r:GRID_W * r + GRID_W, :, :],
                                   bass.AP(scr_toep.tensor, scr_toep.offset + first,
                                           [[NA_DR * GRID_W, GRID_W], [-2 * GRID_W, RT], [1, S]]))\
                        .then_inc(ld[f"bias{b}"], 16)

            bias_load(0)
            power(STAT0["cq"])
            power(STAT0["ckv"])
            for h in range(HEADS):
                if h + 1 < HEADS:
                    bias_load(h + 1)
                b = h % 2
                pool.wait_ge(ld[f"bias{b}"], 32 * (h // 2 + 1))
                pool.tensor_tensor(bias[b][:, :, :], bias[b][:, :, :], bcast(colmask[:, :], [0, RT], [1, S]), ALU.add)\
                    .then_inc(bias_masked, 1)
            power(STAT0["yna"])
            power(STAT0["ymla"])
            pool.wait_ge(norm_split, PAIR0["hmem"])
            pool.wait_ge(head_written, 24)
            for b in range(2):
                pool.wait_ge(kvst_free[b], 16 + 16 * 4)
            pool.dma_start(xkv[:, :, :], scr_k).then_inc(ld["xk"], 16)
            pool.wait_ge(plain_turned, 4 + 8)
            pool.dma_start(xkv[:, :, :], scr_v).then_inc(ld["xv"], 16)
            power(STAT0["hmem"])
            power(STAT0["hffn"])
            pool.wait_ge(norm_split, PAIR0["hffn"])
            a = A["final_norm_2"]
            pool.dma_start(wide_b[:, :], bass.AP(a.tensor, a.offset, [[0, P], [1, D]])).then_inc(ld["final"], 16)
            power(STAT0["final"])

        @block.tensor
        def _(pe):
            pe.sem_inc(used, RING)
            pe.sem_inc(hidden_turned, 2)

            def split_ready(u):
                pe.wait_ge(lo_done, u + RING + 1)

            def chunk(blk, j, half_q, c, units=4, cols=CW, kt=UK, stat=sa, k0=0, before=(),
                      stride=1, after=lambda n: None):
                pair = c % 2
                pe.wait_ge(acc_free[pair], 2 * (half_q + c // 2) + 2)
                for n in range(units):
                    s = (j + stride * n) % RING
                    split_ready(4 * blk + j + stride * n)
                    for kk in range(kt):
                        k = n * kt + kk
                        if k in before:
                            before[k]()
                        first, last = k == 0, k == units * kt - 1
                        shi, slo = stat(k0 + k)
                        for t in range(RT):
                            o = bank[2 * pair + t][:, 0:cols]
                            rows = slice(t * P, t * P + P)
                            pe.matmul(o, shi[:, rows], whi[s][:, kk, 0:cols], start=first, stop=False)
                            pe.matmul(o, shi[:, rows], wlo[s][:, kk, 0:cols], start=False, stop=False)
                            mm = pe.matmul(o, slo[:, rows], whi[s][:, kk, 0:cols], start=False, stop=last)
                    mm.then_inc(used, 1)
                    after(n)

            def chunk_with_ada(blk, j, half_q, c, turn, before=(), between=lambda: None):
                def ada_units(n):
                    if n == 0:
                        between()
                    for b in range(2):
                        if n == 0:
                            pe.wait_ge(ada_free[b], turn + 1)
                        s = (j + 3 * n + 1 + b) % RING
                        split_ready(4 * blk + j + 3 * n + 1 + b)
                        for kk in range(UK):
                            k = n * UK + kk
                            two = ccol[:, 2 * k:2 * k + P]
                            pe.matmul(bank[6 + b][:, :], two, whi[s][:, kk, :], start=(k == 0), stop=False)
                            mm = pe.matmul(bank[6 + b][:, :], two, wlo[s][:, kk, :], start=False, stop=(k == KD - 1))
                        mm.then_inc(used, 1)

                chunk(blk, j, half_q, c, stride=3, after=ada_units, before=before)

            def turn_pair(name, j):
                n, normed = PAIR0[name] + j, NT[name][1] == 1
                if normed:
                    pe.wait_ge(rows_normed, XN0[name] + j + 1)
                elif j == 0:
                    src_ready(pe, name)
                if n >= 2:
                    pe.wait_ge(norm_split if n - 2 in PLAIN_PAIRS else norm_scaled, n - 1)
                for kk in range(2):
                    for t in range(RT):
                        src = xn[n % 2][:, t, kk * P:kk * P + P] if normed else NTSRC[name](t, (2 * j + kk) * P, P)
                        mm = pe.transpose(bank[4 + n % 2][:, kk * S + t * P:kk * S + t * P + P], src, ident[:, :])
                mm.then_inc(norm_turned, 1)

            def norm_turn(name):
                for j in range(NT[name][0] // 2):
                    turn_pair(name, j)

            def turn_on_the_way(pairs, ahead):
                def step(p):
                    for q, (name, m) in enumerate(pairs):
                        if q - ahead[q] == p or (p == 0 and q - ahead[q] < 0):
                            turn_pair(name, m)
                    name, m = pairs[p]
                    pe.wait_ge(norm_split, PAIR0[name] + m + 1)
                return {2 * p: (lambda p=p: step(p)) for p in range(len(pairs))}

            def eight(name):
                return turn_on_the_way([(name, m) for m in range(8)], [2] * 8)

            def turn_plain(src, pairs, n0, b0=6):
                for j in range(pairs):
                    n = n0 + j
                    if n >= 2:
                        pe.wait_ge(plain_copied, n - 1)
                    for kk in range(2):
                        for t in range(RT):
                            mm = pe.transpose(bank[b0 + n % 2][:, kk * S + t * P:kk * S + t * P + P],
                                              src(t, (2 * j + kk) * P), ident[:, :])
                    mm.then_inc(plain_turned, 1)

            def stat_ready(name):
                pe.wait_ge(norm_split, PAIR0[name] + NT[name][0] // 2)

            pe.wait_ge(ident_ready, 2)
            pe.wait_ge(ld["vec"], 16 * len(VECS))
            pe.transpose(bank[6][:, 0:P], vrow[:, :], ident[:, :]).then_inc(vec_turned, 1)
            pe.wait_ge(silu_c_ready, 1)
            pe.transpose(bank[7][:, 0:KD], csil[:, :], ident[0:KD, 0:KD]).then_inc(c_turned, 1)
            norm_turn("mem")
            stat_ready("mem")
            pe.wait_ge(c_split, 2)
            pe.wait_ge(vcol_ready, 1)
            with pe.Fori(0, 2) as i:
                blk, hq, ha = UNIT0["xk_ada"] // 4 + i * 6, CHUNK0["xk_ada"] // 2 + i, i * 2
                for c in range(2):
                    chunk_with_ada(blk, 12 * c, hq, c, ha + c)
            for c in range(4):
                if c == 3:
                    pe.wait_ge(mod_rows, 1)
                    for b in range(2):
                        pe.wait_ge(ada_free[b], 1 + 4)
                    pe.transpose(bank[6][:, 0:32], mrow[0][0:32, 0, :], ident[0:32, 0:32]).then_inc(mod_turned, 1)
                chunk(UNIT0["xv"] // 4, 4 * c, CHUNK0["xv"] // 2, c)
            pe.wait_ge(mod_columns, 1)

            def in_ada(i, between=lambda c: None, first={}):
                blk, hq, ha = UNIT0["in_ada"] // 4 + i * 6, CHUNK0["in_ada"] // 2 + i, 4 + i * 2
                for c in range(2):
                    chunk_with_ada(blk, 12 * c, hq, c, ha + c, **({} if c else first))
                    between(c)

            def turn_u(c):
                if c == 0:
                    chunks_out(pe, CHUNK0["in_ada"] + 6)
                    turn_plain(lambda t, c: proj[:, t, c:c + P], 4, 0, b0=4)
                    pe.wait_ge(plain_copied, 4)
                    pe.wait_ge(ssm_rows, 1)
                    pe.transpose(bank[4][:, 0:96], srow[:, :], ident[0:96, 0:96]).then_inc(ssm_rows_turned, 1)

            def turn_rest():
                for m in range(4, 8):
                    turn_pair("h1", m)

            def ready(p):
                if p < 2:
                    turn_pair("h1", 2 + p)
                pe.wait_ge(norm_split, PAIR0["h1"] + p + 1)

            turn_pair("h1", 0)
            turn_pair("h1", 1)
            in_ada(0, first=dict(before={2 * p: (lambda p=p: ready(p)) for p in range(8)}, between=turn_rest))
            with pe.Fori(1, 3) as i:
                in_ada(i)
            in_ada(3, turn_u)
            chunks_out(pe, CHUNK0["glu"])
            for b in range(2):
                pe.wait_ge(ada_free[b], 1 + 12)
            pe.wait_ge(plain_copied, 4)

            def head_turn(kind, n):
                b, h = n % 2, n - HEAD0[kind]
                if kind == "cross":
                    pe.wait_ge(qk_copied, n)
                elif n >= 2:
                    pe.wait_ge(qk_copied, n - 1)
                if kind == "mla":
                    if h >= 2:
                        pe.wait_ge(rope_copied, h - 1)
                    pe.wait_ge(head_written, n - 3 if h >= 2 else HEAD0["mla"])
                if kind == "cross":
                    for kt in range(XKT):
                        for t in range(RT):
                            mm = pe.transpose(bank[kt // 2][:, kt % 2 * S + t * P:kt % 2 * S + t * P + P],
                                              xq[:, t, h * XHD + kt * P:h * XHD + kt * P + P], ident[:, :])
                    mm.then_inc(qk_turned, 1)
                    return
                for w, src in enumerate(QKSRC[kind]):
                    for t in range(RT):
                        mm = pe.transpose(bank[b][:, w * S + t * P:w * S + t * P + P], src(t, h), ident[:, :])
                if kind == "mla":
                    for t in range(RT):
                        mm = pe.transpose(bank[6 + b][0:ROPE, (2 + t) * P:(3 + t) * P],
                                          q_mla[:, t, h, NOPE:QK], ident[:, :])
                mm.then_inc(qk_turned, 1)

            def head_scores(kind, n):
                b, h = n % 2, n - HEAD0[kind]
                pe.wait_ge(qk_copied, n + 1)
                if kind == "mla":
                    pe.wait_ge(rope_copied, h + 1)
                if n >= 2:
                    pe.wait_ge(exp_ready, n - 1)
                for t in range(RT):
                    rows = slice(t * P, t * P + P)
                    o = bank[2 + b][:, t * S:t * S + S]
                    if kind == "cross":
                        for kt in range(XKT):
                            mm = pe.matmul(o, xqT[:, kt, rows], xkT[:, h * XKT + kt, :], start=(kt == 0),
                                           stop=(kt == XKT - 1))
                    else:
                        mm = pe.matmul(o, qkT[b][:, 0, rows], qkT[b][:, 1, :], start=True, stop=(kind != "mla"))
                        if kind == "mla":
                            mm = pe.matmul(o, rT[b][:, rows], krT[:, :], start=False, stop=True)
                mm.then_inc(scores_ready, 1)

            def head_turn_p(kind, n):
                b = n % 2
                if kind == "dil":
                    pe.wait_ge(probs_counted, n + 1)
                else:
                    pe.wait_ge(exp_ready, n + 1)
                if n >= 2:
                    pe.wait_ge(probs_copied, n - 1)
                for t in range(RT):
                    for kt in range(RT):
                        mm = pe.transpose(bank[4 + b][:, kt * S + t * P:kt * S + t * P + P],
                                          sp[b][:, t, kt * P:kt * P + P], ident[:, :])
                mm.then_inc(probs_turned, 1)

            def head_values(kind, n):
                b, h = n % 2, n - HEAD0[kind]
                pe.wait_ge(probs_copied, n + 1)
                if kind == "cross":
                    pe.wait_ge(head_written, n)
                elif n >= 2:
                    pe.wait_ge(head_written, n - 1)
                if kind == "mla":
                    pe.wait_ge(rope_copied, min(h + 3, HEADS))
                for t in range(RT):
                    o = bank[6 + t][:, :] if kind == "cross" else bank[6 + b][:, t * P:t * P + P]
                    for kt in range(RT):
                        mm = pe.matmul(o, pT[b][:, kt, t * P:t * P + P], VSRC[kind](kt, h), start=(kt == 0),
                                       stop=(kt == RT - 1))
                mm.then_inc(values_ready, 1)

            def attend(kind):
                ns = heads(kind)
                head_turn(kind, ns[0])
                head_scores(kind, ns[0])
                head_turn(kind, ns[1])
                for n in ns:
                    if n + 1 in ns:
                        head_scores(kind, n + 1)
                    if n + 2 in ns:
                        head_turn(kind, n + 2)
                    head_turn_p(kind, n)
                    if n > ns[0]:
                        head_values(kind, n - 1)
                head_values(kind, ns[-1])
                pe.wait_ge(head_written, ns[-1] + 1)

            pe.wait_ge(qk_normed, 2)
            attend("dil")
            norm_turn("yatt")

            pe.wait_ge(norm_split, PAIR0["h2"])
            for m in range(8):
                src, n = (bb, m // 2) if m < 4 else (cc, (m - 4) // 2)
                pe.wait_ge(bc_ready, n + 1 if m < 4 else n + 3)
                if m >= 2:
                    pe.wait_ge(bc_copied, m - 1)
                for q in range(4):
                    k = 4 * (m % 2) + q
                    s = bb[n][:, 4 * k:4 * k + 4, :] if m < 4 else cc[n][:, k, :]
                    mm = pe.transpose(bank[4 + m % 2][:, q * P:q * P + P], s, ident[:, :])
                mm.then_inc(bc_turned, 1)
            pe.wait_ge(mod_rows, 2)
            pe.transpose(bank[6][:, 0:64], mrow[1][:, 0, :], ident[0:64, 0:64]).then_inc(mod_turned, 1)
            pe.wait_ge(bc_copied, 8)

            def drive(j):
                k, q = j // 4, j % 4
                if j >= 4:
                    pe.wait_ge(scan_steps, 8 * (j - 4) + 4)
                rows = slice(32 * q, 32 * q + 32)
                for c in range(2):
                    mm = pe.matmul(bank[q][:, c * S:c * S + S], bt[c][rows, k, :], uT[rows, k, :], start=True, stop=True)
                mm.then_inc(drive_ready, 1)

            def readout(j):
                k, q = j // 4, j % 4
                pe.wait_ge(products_ready, 4 * j + 4)
                if k >= 2 and q == 0:
                    pe.wait_ge(y_ready, k - 1)
                o = bank[4 + k % 2][32 * q:32 * q + 32, 0:S]
                pe.wait_ge(cneg_ready, k + 1)
                cols = slice(32 * q, 32 * q + 32)
                for m, c in enumerate((ct[0][:, k, cols], cneg[k % 2][:, cols], ct[1][:, k, cols], ct[1][:, k, cols])):
                    mm = pe.matmul(o, c, prod[j % 2][:, m, :], start=(m == 0), stop=(m == 3))
                mm.then_inc(readout_ready, 1)

            for j in range(3):
                drive(j)
            for j in range(STILES):
                if j + 3 < STILES:
                    drive(j + 3)
                readout(j)

            pe.wait_ge(y_split, 8)
            for c in range(2):
                pe.wait_ge(acc_free[c], 2 * (CHUNK0["glu"] // 2) + 2)
                split_ready(UNIT0["glu"] + 2 * c + 1)
                for m in range(4):
                    o = bank[2 * c + m // 2][:, m % 2 * S:m % 2 * S + S]
                    cols = slice(m * P, m * P + P)
                    for k in range(8):
                        s, kk = 2 * c + k // UK, k % UK
                        pe.matmul(o, whi[s][:, kk, cols], sa_hi[:, k, :], start=(k == 0), stop=False)
                        pe.matmul(o, whi[s][:, kk, cols], sa_lo[:, k, :], start=False, stop=False)
                        mm = pe.matmul(o, wlo[s][:, kk, cols], sa_hi[:, k, :], start=False, stop=(k == 7))
                mm.then_inc(used, 2)

            def square(stage, stat=sa, before=()):
                for c in range(4):
                    chunk(UNIT0[stage] // 4, 4 * c, CHUNK0[stage] // 2, c, stat=stat, before=() if c else before)

            def ffn(stage, f0, norm):
                blk, hq = UNIT0[stage] // 4, CHUNK0[stage] // 2

                def turn_hidden(f, free):
                    pe.wait_ge(acc_free[1], free)
                    for hf in range(2):
                        pe.wait_ge(hidden_lo_done, 2 * f + hf + 1)
                        for kk in range(2):
                            for t in range(RT):
                                mm = pe.transpose(bank[4 + hf][:, kk * S + t * P:kk * S + t * P + P],
                                                  fg[:, t, (2 * hf + kk) * P:(2 * hf + kk) * P + P], ident[:, :])
                        mm.then_inc(hidden_turned, 1)

                for c0, n in THIRDS:
                    chunk(blk, 0, hq, 0, before=() if c0 else eight(norm))
                    chunk(blk, 4, hq, 1)
                    with pe.Fori(1, n) as i:
                        chunk(blk + i * 2, 0, hq + i, 0)
                        turn_hidden(i + (f0 + c0 - 1), 2 * (hq + i) + 2)
                        chunk(blk + i * 2, 4, hq + i, 1)
                    blk, hq, f_end = blk + 2 * n, hq + n, f0 + c0 + n
                    def acts(k):
                        return act_hi[:, k, :], act_lo[:, k, :]
                    on_the_way = {UK: lambda: turn_hidden(f_end - 1, 2 * hq + 2),
                                  UK * (n - 1): lambda: pe.wait_ge(hidden_lo_done, 2 * f_end + 2)}
                    pe.wait_ge(hidden_lo_done, 2 * f_end)
                    for c in range(4):
                        chunk(blk, n * c, hq, c, units=n, stat=acts, before=() if c else on_the_way)
                    blk, hq = blk + n, hq + 2

            square("out1", lambda k: sa(k + 8) if k < 8 else (y2_hi[:, k - 8, :], y2_lo[:, k - 8, :]),
                   {8: lambda: pe.wait_ge(gated_y_split, 2)})
            ffn("ffn1", 0, "h2")
            chunk(UNIT0["in2"] // 4, 0, CHUNK0["in2"] // 2, 0, before=eight("hmix"))
            chunk(UNIT0["in2"] // 4, 4, CHUNK0["in2"] // 2, 1)
            with pe.Fori(1, 3) as i:
                for c in range(2):
                    chunk(UNIT0["in2"] // 4 + i * 2, 4 * c, CHUNK0["in2"] // 2 + i, c)
            chunk(UNIT0["in2"] // 4 + 6, 0, CHUNK0["in2"] // 2 + 3, 0)
            chunk(UNIT0["in2"] // 4 + 6, 4, CHUNK0["in2"] // 2 + 3, 1, cols=IN2 - 7 * CW)
            norm_turn("cq")
            norm_turn("ckv")
            stat_ready("ckv")
            for c in range(4):
                chunk(UNIT0["uq"] // 4, c, CHUNK0["uq"] // 2, c, units=1, cols=2 * QK)
            chunks_out(pe, CHUNK0["ukv"])
            attend("na")
            for c in range(4):
                chunk(UNIT0["ukv"] // 4, c, CHUNK0["ukv"] // 2, c, units=1, kt=2, k0=4)
            chunks_out(pe, CHUNK0["out2"])
            pe.wait_ge(key_rotated, 1)
            for t in range(RT):
                mm = pe.transpose(bank[7][0:ROPE, (2 + t) * P:(3 + t) * P], kr[:, t, :], ident[:, :])
            mm.then_inc(key_turned, 1)
            pe.wait_ge(key_copied, 1)
            attend("mla")
            square("out2", before=turn_on_the_way([(name, m) for name in ("yna", "ymla") for m in range(4)],
                                                  [2, 2, 2, 2, 1, 1, 2, 2]))
            pe.wait_ge(ld["xk"], 16)
            turn_plain(lambda t, c: xkv[:, t, c:c + P], 8, 4)
            square("xq", before=eight("hmem"))
            pe.wait_ge(plain_copied, 12)
            chunks_out(pe, CHUNK0["xo"])
            pe.wait_ge(ld["xv"], 16)
            attend("cross")
            square("xo", before=eight("ocross"))
            ffn("ffn2", FCH, "hffn")

        @block.scalar
        def _(act):
            for b in range(2):
                act.sem_inc(ada_free[b], 1)
                act.sem_inc(adast_free[b], 16)
                act.sem_inc(kvst_free[b], 16)

            def pump(blk, j):
                j += LOOKAHEAD
                s, blk = j % RING, blk + j // RING
                if isinstance(blk, int) and RING * blk + s >= UNITS:
                    return
                act.wait_ge(landed[s], 16 * blk + 16)
                act.wait_ge(used, RING * blk + s + 1)
                act.activation(whi[s][:, :, :], raw[s][:, :, :], ACT.Copy).then_inc(hi_done, 1)

            def pumps(blk, j, n):
                for m in range(n):
                    pump(blk, j + m)

            def unit_used(blk, j):
                act.wait_ge(used, RING + 4 * blk + j + 1)

            def norm_turn(name, between=lambda: None):
                k_tiles, stat = NT[name]
                s, p0 = STAT0[name], PAIR0[name]
                width = k_tiles * P
                if stat == 1:
                    norm_squares(name, s, p0, width)
                if name == "yatt":
                    act.wait_ge(used, RING + UNIT0["glu"])
                elif name == "ocross":
                    act.wait_ge(used, RING + UNIT0["xo"])
                for j in range(k_tiles // 2):
                    n, b = p0 + j, (p0 + j) % 2
                    act.wait_ge(norm_turned, n + 1)
                    if not stat:
                        k = NTK0.get(name, 0) + 2 * j
                        hi = (sa_hi, s2_hi)[k // 8]
                        act.activation(hi[:, k % 8:k % 8 + 2, :], bank[4 + b][:, :].rearrange("p (k s) -> p k s", k=2),
                                       ACT.Copy).then_inc(norm_scaled, 1)
                        continue
                    if n >= 2:
                        act.wait_ge(norm_split, n - 1)
                    for kk in range(2):
                        k = 2 * j + kk
                        o, i = full[b][:, kk, :], bank[4 + b][:, kk * S:kk * S + S]
                        if name in ("h1", "h2"):
                            m, shift = (0, 0) if name == "h1" else (1, 48)
                            ins = act.activation(o, i, ACT.Identity, scale=scol[m][:, k:k + 1],
                                                 bias=modc[:, shift + k:shift + k + 1])
                        else:
                            ins = act.activation(o, i, ACT.Copy, scale=vec(NTSCALE[name], k))
                    ins.then_inc(norm_scaled, 1)
                between()
                if stat == 2:
                    norm_squares(name, s, p0 + k_tiles // 2, width)

            def norm_squares(name, s, p0, width):
                src_ready(act, name)
                if p0:
                    act.wait_ge(norm_split, p0)
                    act.wait_ge(norm_turned, p0)
                if s:
                    act.wait_ge(variance_ready, s)
                src, o = NTSRC[name](0, 0, width), junk[:, 0, 0:width]
                if name == "ymla":
                    o = o.rearrange("p (a b) -> p a b", b=VD)
                act.activation(o, src, ACT.Square, accum_out=ss[:, 0:1]).then_inc(squares_summed[0], 1)

            def copy_out(blk, j, c, dst, cols=CW, norm=None):
                unit_used(blk, j)
                factor = {}
                if norm:
                    act.wait_ge(rstd_ready, STAT0[norm] + 1)
                    factor = dict(scale=rstd[:, 0:1])
                act.activation(dst, bank[2 * (c % 2)][:, 0:cols], ACT.Copy, **factor).then_inc(acc_free[c % 2], 1)

            act.wait_ge(ld["c"], 16)
            act.activation(csil[:, :], crow[:, :], ACT.Silu).then_inc(silu_c_ready, 1)
            act.wait_ge(vcol_ready, 1)
            norm_turn("mem", between=lambda: pumps(0, -LOOKAHEAD, LOOKAHEAD))

            def ada_out(blk, j, half_a, a, col):
                b = a % 2
                unit_used(blk, j)
                act.wait_ge(adast_free[b], 16 * (half_a + a // 2 + 1))
                act.activation(adast[b][:, :], bank[6 + b][0:2, :], ACT.Copy).then_inc(ada_free[b], 1)
                act.wait_ge(ada_free[b], half_a + a // 2 + 2)
                act.dma_start(scr_ada[:, bass.ds(col, CW)], adast[b][:, :]).then_inc(adast_free[b], 16)

            def kv_out(blk, j, hq, c, scr, col):
                act.wait_ge(kvst_free[c], 16 * hq + 16)
                copy_out(blk, j, c, kvst[c][:, 0, :], norm="mem")
                act.wait_ge(acc_free[c], 2 * hq + 4)
                act.dma_start(scr[:, :, bass.ds(col, CW)], kvst[c][:, :, :]).then_inc(kvst_free[c], 16)

            with act.Fori(0, 2) as i:
                blk, hq, ha = UNIT0["xk_ada"] // 4 + i * 6, CHUNK0["xk_ada"] // 2 + i, i * 2
                for c in range(2):
                    pumps(blk, 12 * c, 10)
                    kv_out(blk, 12 * c + 9, hq, c, scr_k, i * (2 * CW) + c * CW)
                    for a in range(2):
                        pump(blk, 12 * c + 10 + a)
                        ada_out(blk, 12 * c + 10 + a, ha, 2 * c + a, i * (4 * CW) + (2 * c + a) * CW)
            with act.Fori(0, 2) as i:
                blk, hq = UNIT0["xv"] // 4 + i * 2, CHUNK0["xv"] // 2 + i
                for c in range(2):
                    pumps(blk, 4 * c, 4)
                    kv_out(blk, 4 * c + 3, hq, c, scr_v, i * (2 * CW) + c * CW)
            act.wait_ge(mod_columns, 1)
            norm_turn("h1")
            for b in range(2):
                act.wait_ge(kvst_free[b], 16 + 16 * 4)

            def turn_plain(pairs, n0, dst, b0=6):
                for j in range(pairs):
                    n = n0 + j
                    act.wait_ge(plain_turned, n + 1)
                    act.activation(dst[:, 2 * j:2 * j + 2, :], bank[b0 + n % 2][:, :].rearrange("p (k s) -> p k s", k=2),
                                   ACT.Copy).then_inc(plain_copied, 1)

            def in_ada(i, between=lambda step: None):
                blk, hq, ha = UNIT0["in_ada"] // 4 + i * 6, CHUNK0["in_ada"] // 2 + i, 4 + i * 2
                for c in range(2):
                    for g in range(2):
                        pumps(blk, 12 * c + 4 * g, 4)
                        between(3 * c + g)
                    pumps(blk, 12 * c + 8, 2)
                    copy_out(blk, 12 * c + 9, c, proj[:, 0, bass.ds(i * (2 * CW) + c * CW, CW)])
                    for a in range(2):
                        pump(blk, 12 * c + 10 + a)
                        ada_out(blk, 12 * c + 10 + a, ha, 2 * c + a, i * (4 * CW) + (8 + 2 * c + a) * CW)
                    between(3 * c + 2)

            def p_(name):
                return par[:, PAR[name], :]

            def qk_of_tile0(step):
                if step == 2:
                    turn_plain(4, 0, uT, b0=4)
                elif step in (0, 1):
                    if step == 0:
                        act.wait_ge(norm_split, PAIR0["yatt"])
                        chunks_out(act, CHUNK0["in_ada"] + 6)
                    else:
                        act.wait_ge(tile0_squares, 8)
                    for h in range(8 * step, 8 * step + 8):
                        act.activation(sqj[:, h % 8, :], proj[:, 0, SSM_W + h * HD:SSM_W + h * HD + HD], ACT.Square,
                                       accum_out=qk_ss[:, 0, h:h + 1]).then_inc(tile0_squares, 1)
                elif step == 3:
                    act.wait_ge(ssm_columns, 1)
                    act.activation(p_("dt"), scolp[:, 64:96], ACT.Exp).then_inc(ssm_exps, 1)
                elif step == 4:
                    act.wait_ge(ssm_angles, 1)
                    act.activation(p_("mag"), p_("ard"), ACT.Exp).then_inc(ssm_exps, 1)
                    act.wait_ge(ssm_angles, 2)
                    act.activation(p_("sin"), p_("r"), ACT.Sin)
                    act.activation(p_("sh"), p_("r"), ACT.Sin, scale=0.5).then_inc(ssm_exps, 1)
                    act.wait_ge(ssm_exps, 3)
                    act.activation(p_("sh2"), p_("sh"), ACT.Square).then_inc(ssm_exps, 1)
                    act.wait_ge(qk_rstd, 1)
                    for h in range(2 * HEADS):
                        qk = proj[:, 0, SSM_W + h * HD:SSM_W + h * HD + HD]
                        ins = act.activation(qk, qk, ACT.Copy, scale=qk_rs[:, 0, h:h + 1])
                    ins.then_inc(qk_normed, 1)

            with act.Fori(0, 3) as i:
                in_ada(i)
            in_ada(3, qk_of_tile0)
            def head_in(kind, n):
                b = n % 2
                act.wait_ge(qk_turned, n + 1)
                if kind == "cross":
                    act.wait_ge(scores_ready, n)
                    act.activation(xqT[:, 0:2, :], bank[0][:, :].rearrange("p (k s) -> p k s", k=2), ACT.Copy)
                    act.activation(xqT[:, 2:4, :], bank[1][:, :].rearrange("p (k s) -> p k s", k=2), ACT.Copy)\
                        .then_inc(qk_copied, 1)
                    return
                if n >= 2:
                    act.wait_ge(scores_ready, n - 1)
                if kind == "dil":
                    act.activation(qkT[b][:, 0, :], bank[b][:, 0:S], ACT.Copy, scale=qscol[:, :])
                    act.activation(qkT[b][:, 1, :], bank[b][:, S:2 * S], ACT.Copy).then_inc(qk_copied, 1)
                else:
                    act.activation(qkT[b][:, :, :], bank[b][:, :].rearrange("p (k s) -> p k s", k=2), ACT.Copy)\
                        .then_inc(qk_copied, 1)

            def head_exp(kind, n):
                b = n % 2
                act.wait_ge(negmax_ready, n + 1)
                if n >= 2:
                    act.wait_ge(probs_turned, n - 1)
                    act.wait_ge(recip_ready, n - 1)
                for t in range(RT):
                    src = sp[b][:, t, :] if kind in ("dil", "na") else bank[2 + b][:, t * S:t * S + S]
                    scale = {"mla": QK ** -0.5, "cross": XHD ** -0.5}.get(kind, 1.0)
                    acc = {} if kind == "dil" else dict(accum_out=rsum[:, b, t:t + 1])
                    ins = act.activation(sp[b][:, t, :], src, ACT.Exp, bias=negm[:, b, t:t + 1], scale=scale, **acc)
                ins.then_inc(exp_ready, 1)

            def head_out(kind, n):
                b, h = n % 2, n - HEAD0[kind]
                act.wait_ge(recip_ready, n + 1)
                act.wait_ge(values_ready, n + 1)
                for t in range(RT):
                    o = bank[6 + t][:, :] if kind == "cross" else bank[6 + b][:, t * P:t * P + P]
                    ins = act.activation(YDST[kind](t, h), o, ACT.Copy, scale=rden[:, b, t:t + 1])
                ins.then_inc(head_written, 1)

            def attend(kind):
                ns = heads(kind)
                head_in(kind, ns[0])
                head_in(kind, ns[1])
                head_exp(kind, ns[0])
                for n in ns:
                    if n + 2 in ns:
                        head_in(kind, n + 2)
                    if n + 1 in ns:
                        head_exp(kind, n + 1)
                    if n > ns[0]:
                        head_out(kind, n - 1)
                head_out(kind, ns[-1])

            act.wait_ge(qk_normed, 2)
            attend("dil")
            norm_turn("yatt")
            def sines(k):
                act.wait_ge(angles_reduced, k + 1)
                if k >= 2:
                    act.wait_ge(products_ready, 16 * (k - 1))
                act.activation(si[k % 2][:, :, :], turn[:, :, :], ACT.Sin, scale=6.283185)
                if k:
                    act.wait_ge(cosines_ready, k)
                act.activation(half[:, :, :], turn[:, :, :], ACT.Sin, scale=3.1415925).then_inc(sines_ready, 1)
                act.wait_ge(sines_ready, 2 * k + 1)
                act.activation(half[:, :, :], half[:, :, :], ACT.Square).then_inc(sines_ready, 1)

            def negate(k):
                act.wait_ge(bc_copied, 8)
                if k >= 2:
                    act.wait_ge(readout_ready, 4 * (k - 1))
                act.activation(cneg[k % 2][:, :], ct[0][:, k, :], ACT.Copy, scale=-1.0).then_inc(cneg_ready, 1)

            sines(0)
            for m in range(8):
                act.wait_ge(bc_turned, m + 1)
                dst = (bt if m < 4 else ct)[(m % 4) // 2]
                act.activation(dst[:, 4 * (m % 2):4 * (m % 2) + 4, :],
                               bank[4 + m % 2][:, :].rearrange("p (k s) -> p k s", k=4), ACT.Copy).then_inc(bc_copied, 1)
            negate(0)
            for k in range(8):
                if k + 1 < 8:
                    sines(k + 1)
                    negate(k + 1)
                act.wait_ge(y_ready, k + 1)
                if k:
                    act.wait_ge(y_split, k)
                act.activation(gt[:, :], yt[:, :], ACT.Gelu_apprx_tanh).then_inc(gelu_ready, 1)

            blk = UNIT0["glu"] // 4
            for c in range(2):
                pumps(blk, 2 * c, 2)
                act.wait_ge(used, RING + 4 * blk + 2 * c + 2)
                for m in range(2):
                    act.activation(sig[:, 4 * c + 2 * m:4 * c + 2 * m + 2, :],
                                   bank[2 * c + m][:, :].rearrange("p (k s) -> p k s", k=2), ACT.Sigmoid)\
                        .then_inc(acc_free[c], 1)

            def pump_square(stage):
                with act.Fori(0, 2) as i:
                    pumps(UNIT0[stage] // 4 + i * 2, 0, 8)

            def silu_gate(stage, blk):
                unit_used(blk, 3)
                late = stage == "ffn2"
                if late:
                    act.wait_ge(rstd_ready, STAT0["hffn"] + 1)
                for t in range(RT):
                    factor = dict(scale=rstd[:, t:t + 1]) if late else {}
                    act.activation(fg[:, t, :], bank[t][:, :], ACT.Silu, **factor).then_inc(acc_free[0], 1)

            def hidden_heads(f, k):
                for hf in range(2):
                    act.wait_ge(hidden_turned, 2 * f + hf + 3)
                    act.activation(act_hi[:, bass.ds(k + 2 * hf, 2), :],
                                   bank[4 + hf][:, :].rearrange("p (k s) -> p k s", k=2), ACT.Copy).then_inc(hidden_hi_done, 1)

            def ffn(stage, f0):
                blk, hq = UNIT0[stage] // 4, CHUNK0[stage] // 2
                for c0, n in THIRDS:
                    pumps(blk, 0, 4)
                    silu_gate(stage, blk)
                    pumps(blk, 4, 4)
                    with act.Fori(1, n) as i:
                        pumps(blk + i * 2, 0, 4)
                        hidden_heads(i + (f0 + c0 - 1), i * 4 - 4)
                        silu_gate(stage, blk + i * 2)
                        pumps(blk + i * 2, 4, 4)
                    blk, hq = blk + 2 * n, hq + n
                    pumps(blk, 0, 1)
                    hidden_heads(f0 + c0 + n - 1, 4 * n - 4)
                    pumps(blk, 1, 4 * n - 1)
                    blk += n

            pump_square("out1")
            norm_turn("h2")
            ffn("ffn1", 0)
            norm_turn("hmix")
            with act.Fori(0, 3) as i:
                for c in range(2):
                    blk = UNIT0["in2"] // 4 + i * 2
                    pumps(blk, 4 * c, 4)
                    copy_out(blk, 4 * c + 3, c, proj2[:, 0, bass.ds(i * (2 * CW) + c * CW, CW)], norm="hmix")
            blk = UNIT0["in2"] // 4 + 6
            for c in range(2):
                cols = (CW, IN2 - 7 * CW)[c]
                pumps(blk, 4 * c, 4)
                copy_out(blk, 4 * c + 3, c, proj2[:, 0, (6 + c) * CW:(6 + c) * CW + cols], cols, "hmix")
            norm_turn("cq")
            norm_turn("ckv")
            for c in range(4):
                pumps(UNIT0["uq"] // 4, c, 1)
                copy_out(UNIT0["uq"] // 4, c, c, q_mla[:, 0, 2 * c:2 * c + 2, :].rearrange("p a b -> p (a b)"), 2 * QK)
            attend("na")
            for c in range(4):
                pumps(UNIT0["ukv"] // 4, c, 1)
                copy_out(UNIT0["ukv"] // 4, c, c, proj2[:, 0, NA_W + c * CW:NA_W + c * CW + CW])
            act.wait_ge(key_copied, 1)
            attend("mla")
            norm_turn("yna")
            norm_turn("ymla")
            pump_square("out2")
            turn_plain(8, 4, xkT)
            norm_turn("hmem")
            with act.Fori(0, 2) as i:
                for c in range(2):
                    blk = UNIT0["xq"] // 4 + i * 2
                    pumps(blk, 4 * c, 4)
                    copy_out(blk, 4 * c + 3, c, xq[:, 0, bass.ds(i * (2 * CW) + c * CW, CW)], norm="hmem")
            attend("cross")
            norm_turn("ocross")
            pump_square("xo")
            norm_turn("hffn")
            ffn("ffn2", FCH)
            norm_squares("final", STAT0["final"], PAIR0["hffn"] + 8, D)

        @block.vector
        def _(dve):
            dve.sem_inc(lo_done, RING)
            dve.sem_inc(x_updated, 2)
            dve.sem_inc(hidden_lo_done, 2)
            for p in range(2):
                dve.sem_inc(acc_free[p], 2)
            linked = [0]

            def link(ins):
                linked[0] += 1
                ins.then_inc(link_done, 1)
                dve.wait_ge(link_done, linked[0])

            def pump(blk, j):
                j += LOOKAHEAD
                s, blk = j % RING, blk + j // RING
                if isinstance(blk, int) and RING * blk + s >= UNITS:
                    return
                dve.wait_ge(hi_done, RING * blk + s + 1)
                dve.wait_ge(used, RING * blk + s + 1)
                dve.tensor_tensor(wlo[s][:, :, :], raw[s][:, :, :], whi[s][:, :, :].bitcast(F32), ALU.subtract)\
                    .then_inc(lo_done, 1)

            def pumps(blk, j, n):
                for m in range(n):
                    pump(blk, j + m)

            def unit_used(blk, j):
                dve.wait_ge(used, RING + 4 * blk + j + 1)

            def stats(name, s, p0, width):
                src_ready(dve, name)
                if p0:
                    dve.wait_ge(norm_split, p0)
                    dve.wait_ge(norm_turned, p0)
                if s:
                    dve.wait_ge(variance_ready, s)
                src, o = NTSRC[name](1, 0, width), junk[:, 1, 0:width]
                if name == "ymla":
                    o = o.rearrange("p (a b) -> p a b", b=VD)
                dve.tensor_tensor_reduce(o, src, src, 1.0, 0.0, ALU.mult, ALU.add, ss[:, 1:2]).then_inc(squares_summed[1], 1)
                for t in range(RT):
                    dve.wait_ge(squares_summed[t], s + 1)
                if s:
                    dve.wait_ge(rstd_ready, s)
                dve.tensor_scalar(var[:, :], ss[:, :], 1.0 / width, EPS, ALU.mult, ALU.add).then_inc(variance_ready, 1)
                dve.wait_ge(rstd_ready, s + 1)

            def norm_turn(name, units_used, between=lambda: None):
                k_tiles, stat = NT[name]
                pairs, p0 = k_tiles // 2, PAIR0[name]
                if stat == 1:
                    stats(name, STAT0[name], p0, k_tiles * P)

                def normed(j):
                    n = p0 + j
                    if n >= 2:
                        dve.wait_ge(norm_turned, n - 1)
                    for t in range(RT):
                        src, o = NTSRC[name](t, 2 * j * P, 2 * P), xn[n % 2][:, t, :]
                        if name == "ymla":
                            o = o.rearrange("p (a b) -> p a b", b=VD)
                        ins = dve.tensor_scalar(o, src, rstd[:, t:t + 1], None, ALU.mult)
                    ins.then_inc(rows_normed, 1)

                if stat == 1:
                    normed(0)
                    if pairs > 1:
                        normed(1)
                if units_used:
                    dve.wait_ge(used, RING + units_used)
                k0 = NTK0.get(name, 0)
                for j in range(pairs):
                    n, b, k = p0 + j, (p0 + j) % 2, k0 + 2 * j
                    hi, lo = (sa_hi, sa_lo) if k < 8 else (s2_hi, s2_lo)
                    k %= 8
                    dve.wait_ge(norm_scaled, n + 1)
                    if not stat:
                        dve.tensor_tensor(lo[:, k:k + 2, :], bank[4 + b][:, :].rearrange("p (k s) -> p k s", k=2),
                                          hi[:, k:k + 2, :].bitcast(F32), ALU.subtract).then_inc(norm_split, 1)
                        continue
                    dve.tensor_copy(hi[:, k:k + 2, :], full[b][:, :, :]).then_inc(norm_heads, 1)
                    if stat == 1 and j + 2 < pairs:
                        normed(j + 2)
                    dve.wait_ge(norm_heads, HEADS0[name] + j + 1)
                    dve.tensor_tensor(lo[:, k:k + 2, :], full[b][:, :, :], hi[:, k:k + 2, :].bitcast(F32), ALU.subtract)\
                        .then_inc(norm_split, 1)
                between()
                if stat == 2:
                    stats(name, STAT0[name], p0 + pairs, k_tiles * P)

            def copy_out(blk, j, c, dst, cols=CW, norm=None):
                unit_used(blk, j)
                o = bank[2 * (c % 2) + 1][:, 0:cols]
                if norm:
                    ins = dve.tensor_scalar(dst, o, rstd[:, 1:2], None, ALU.mult)
                else:
                    ins = dve.tensor_copy(dst, o)
                ins.then_inc(acc_free[c % 2], 1)

            def add_out(blk, j, hq, c, col):
                unit_used(blk, j)
                dve.wait_ge(acc_free[c % 2], 2 * (hq + c // 2) + 2)
                for t in range(RT):
                    xs = x[:, t, bass.ds(col, CW)]
                    dve.tensor_tensor(xs, bank[2 * (c % 2) + t][:, :], xs, ALU.add).then_inc(acc_free[c % 2], 1)

            def gated_out(blk, j, hq, c, col, gate, g):
                unit_used(blk, j)
                for t in range(RT):
                    dve.wait_ge(x_updated, 2 * g + t + 1)
                    dve.tensor_tensor(rtmp[:, t, :], bank[2 * (c % 2) + t][:, :], gate[:, bass.ds(col, CW)], ALU.mult)\
                        .then_inc(acc_free[c % 2], 1)
                for t in range(RT):
                    dve.wait_ge(acc_free[c % 2], 2 * (hq + c // 2) + 3 + t)
                    xs = x[:, t, bass.ds(col, CW)]
                    dve.tensor_tensor(xs, rtmp[:, t, :], xs, ALU.add).then_inc(x_updated, 1)

            dve.wait_ge(vec_turned, 1)
            dve.tensor_copy(vcol[:, :], bank[6][:, 0:P]).then_inc(vcol_ready, 1)
            dve.wait_ge(c_turned, 1)
            dve.tensor_copy(cT[:, :], bank[7][:, 0:KD]).then_inc(c_column, 1)
            dve.wait_ge(c_column, 1)
            pairs_ = ccol[:, 0:2 * KD].rearrange("p (k c) -> p k c", c=2)
            dve.memset(ccol[:, 2 * KD:2 * KD + P].bitcast(F32), 0.0)
            dve.tensor_copy(pairs_[:, :, 0], cT[:, :]).then_inc(c_split, 1)
            dve.wait_ge(c_split, 1)
            dve.tensor_tensor(pairs_[:, :, 1], cT[:, :], pairs_[:, :, 0].bitcast(F32), ALU.subtract).then_inc(c_split, 1)
            dve.wait_ge(vcol_ready, 1)
            link(dve.tensor_tensor(qscol[:, :], vec("q_norm_w"), vec("k_norm_w"), ALU.mult))
            link(dve.tensor_scalar(qscol[:, :], qscol[:, :], HD ** -0.5, None, ALU.mult))
            norm_turn("mem", 0, lambda: pumps(0, -LOOKAHEAD, LOOKAHEAD))
            with dve.Fori(0, 2) as i:
                blk, hq = UNIT0["xk_ada"] // 4 + i * 6, CHUNK0["xk_ada"] // 2 + i
                for c in range(2):
                    pumps(blk, 12 * c, 10)
                    dve.wait_ge(kvst_free[c], 16 * hq + 16)
                    copy_out(blk, 12 * c + 9, c, kvst[c][:, 1, :], norm="mem")
                    pumps(blk, 12 * c + 10, 2)
            def modulation(m, rows):
                dve.wait_ge(ld[f"mrow{m}"], 32)
                link(dve.tensor_tensor(mrow[m][0:rows, 0, :], mrow[m][0:rows, 0, :], mrow[m][0:rows, 1, :], ALU.add))
                dve.tensor_tensor(mrow[m][0:rows, 0, :], mrow[m][0:rows, 0, :], mbias[m][0:rows, :], ALU.add)\
                    .then_inc(mod_rows, 1)
                dve.wait_ge(mod_turned, m + 1)
                link(dve.tensor_copy(modc[:, 32 * m:32 * m + rows], bank[6][:, 0:rows]))
                at_ = (KD, 32 + 2 * KD)[m]
                link(dve.tensor_scalar(scol[m][:, :], modc[:, at_:at_ + KD], 1.0, None, ALU.add))
                name = ("norm1_w", "norm2_w")[m]
                dve.tensor_tensor(scol[m][:, :], scol[m][:, :], vcol[:, VAT[name]:VAT[name] + KD], ALU.mult)\
                    .then_inc(mod_columns, 1)

            for c in range(4):
                pumps(UNIT0["xv"] // 4, 4 * c, 4)
                dve.wait_ge(kvst_free[c % 2], 16 * (CHUNK0["xv"] // 2 + c // 2) + 16)
                copy_out(UNIT0["xv"] // 4, 4 * c + 3, c, kvst[c % 2][:, 1, :], norm="mem")
                if c == 2:
                    modulation(0, 32)
            norm_turn("h1", UNIT0["in_ada"])
            for b in range(2):
                dve.wait_ge(kvst_free[b], 16 + 16 * 4)

            def in_ada(i, between=lambda step: None):
                blk = UNIT0["in_ada"] // 4 + i * 6
                for c in range(2):
                    for g in range(2):
                        pumps(blk, 12 * c + 4 * g, 4)
                        between(3 * c + g)
                    pumps(blk, 12 * c + 8, 2)
                    copy_out(blk, 12 * c + 9, c, proj[:, 1, bass.ds(i * (2 * CW) + c * CW, CW)])
                    pumps(blk, 12 * c + 10, 2)
                    between(3 * c + 2)

            def squares_of(half_):
                cols = slice(SSM_W * (1 + half_), SSM_W * (2 + half_))
                link(dve.tensor_tensor(sqs[:, :], proj[:, 1, cols], proj[:, 1, cols], ALU.mult))
                link(dve.tensor_reduce(qk_ss[:, 1, 8 * half_:8 * half_ + 8],
                                       sqs[:, :].rearrange("p (h e) -> p h e", e=HD), AX.X, ALU.add))

            def normed_qk(half_):
                cols = slice(SSM_W * (1 + half_), SSM_W * (2 + half_))
                qk = proj[:, 1, cols].rearrange("p (h e) -> p h e", e=HD)
                return dve.tensor_tensor(qk, qk, bcast(qk_rs[:, 1, 8 * half_:8 * half_ + 8], [1, HEADS], [0, HD]), ALU.mult)

            def p_(name):
                return par[:, PAR[name], :]

            are, aim = scolp[:, 0:32], scolp[:, 32:64]

            def qk_of_tile1(step):
                if step == 0:
                    dve.wait_ge(norm_split, PAIR0["yatt"])
                    chunks_out(dve, CHUNK0["in_ada"] + 6)
                    squares_of(0)
                elif step == 1:
                    squares_of(1)
                elif step == 2:
                    dve.wait_ge(tile0_squares, 2 * HEADS)
                    dve.tensor_scalar(qk_ss[:, :, :], qk_ss[:, :, :], 1.0 / HD, EPS, ALU.mult, ALU.add).then_inc(qk_variance, 1)
                    dve.wait_ge(ld["sdt"], 16)
                    dve.wait_ge(ld["spar"], 32)
                    dve.tensor_copy(srow[64:96, :].rearrange("p (g n) -> p g n", n=NST), bcast(dtr[64:96, :], [1, 2], [0, NST]))\
                        .then_inc(ssm_rows, 1)
                elif step == 3:
                    dve.wait_ge(ssm_rows_turned, 1)
                    dve.tensor_copy(scolp[:, :], bank[4][:, 0:96]).then_inc(ssm_columns, 1)
                    dve.wait_ge(qk_rstd, 1)
                    normed_qk(0)
                elif step == 4:
                    dve.wait_ge(ssm_exps, 1)
                    link(dve.tensor_tensor(p_("ard"), are, p_("dt"), ALU.mult))
                    dve.tensor_tensor(p_("th"), aim, p_("dt"), ALU.mult).then_inc(ssm_angles, 1)
                    dve.wait_ge(ssm_angles, 1)
                    link(dve.tensor_scalar(p_("k"), p_("th"), 1.0 / TWO_PI, MAGIC, ALU.mult, ALU.add))
                    link(dve.tensor_scalar(p_("k"), p_("k"), MAGIC, None, ALU.subtract))
                    link(dve.scalar_tensor_tensor(out=p_("r"), in0=p_("k"), scalar=-PI_HEAD, in1=p_("th"), op0=ALU.mult, op1=ALU.add))
                    link(dve.scalar_tensor_tensor(out=p_("r"), in0=p_("k"), scalar=-PI_REST, in1=p_("r"), op0=ALU.mult, op1=ALU.add))
                    dve.tensor_scalar(p_("r"), p_("r"), 3.1415925, -3.1415925, ALU.min, ALU.max).then_inc(ssm_angles, 1)
                    dve.wait_ge(ssm_angles, 2)
                    normed_qk(1).then_inc(qk_normed, 1)

            with dve.Fori(0, 3) as i:
                in_ada(i)
            in_ada(3, qk_of_tile1)
            dve.wait_ge(ld["masks"], 32)

            def step_parameters():
                link(dve.tensor_scalar(phh[:, :], p_("r"), 1.0 / TWO_PI, None, ALU.mult))
                link(dve.scalar_tensor_tensor(out=p_("phl"), in0=head, scalar=-PI_HEAD, in1=p_("r"), op0=ALU.mult, op1=ALU.add))
                link(dve.scalar_tensor_tensor(out=p_("phl"), in0=head, scalar=-PI_REST, in1=p_("phl"), op0=ALU.mult, op1=ALU.add))
                link(dve.tensor_scalar(p_("phl"), p_("phl"), 1.0 / TWO_PI, None, ALU.mult))
                link(dve.tensor_tensor(p_("den"), are, are, ALU.mult))
                link(dve.tensor_tensor(p_("t1"), aim, aim, ALU.mult))
                link(dve.tensor_tensor(p_("den"), p_("den"), p_("t1"), ALU.add))
                link(dve.reciprocal(p_("rden"), p_("den")))
                dve.wait_ge(ssm_exps, 4)
                link(dve.tensor_scalar(p_("cos"), p_("sh2"), -2.0, 1.0, ALU.mult, ALU.add))
                link(dve.tensor_tensor(p_("nr"), p_("mag"), p_("cos"), ALU.mult))
                link(dve.tensor_tensor(p_("ni"), p_("mag"), p_("sin"), ALU.mult))
                link(dve.tensor_scalar(p_("nr"), p_("nr"), 1.0, None, ALU.subtract))
                link(dve.tensor_tensor(p_("t1"), p_("nr"), are, ALU.mult))
                link(dve.tensor_tensor(p_("t2"), p_("ni"), aim, ALU.mult))
                link(dve.tensor_tensor(p_("t1"), p_("t1"), p_("t2"), ALU.add))
                link(dve.tensor_tensor(p_("zr"), p_("t1"), p_("rden"), ALU.mult))
                link(dve.tensor_tensor(p_("t1"), p_("ni"), are, ALU.mult))
                link(dve.tensor_tensor(p_("t2"), p_("nr"), aim, ALU.mult))
                link(dve.tensor_tensor(p_("t1"), p_("t1"), p_("t2"), ALU.subtract))
                link(dve.tensor_tensor(p_("zi"), p_("t1"), p_("rden"), ALU.mult))

            whole = turn[:, :, :].rearrange("p q s -> p (q s)").rearrange("p (w j a) -> p w j a", w=2, a=16)
            head = phh[:, :].bitcast(F32)

            def times_steps(o, turns):
                for w in range(2):
                    ins = dve.tensor_tensor(o[:, w], bcast(turns, [1, STILES], [0, 16]),
                                            bcast(iota[:, :], [0, STILES], [(16, 1)[w], 16]), ALU.mult)
                link(ins)

            def whole_turns():
                link(dve.tensor_scalar(whole, phase[:, :, :, :], MAGIC, MAGIC, ALU.add, ALU.subtract))

            def phase_changed(op):
                link(dve.tensor_tensor(phase[:, :, :, :], phase[:, :, :, :], whole, op))

            def phase_table(n):
                if n == 1:
                    dve.wait_ge(ld["iota"], 16)
                    dve.wait_ge(plain_turned, 4)
                    times_steps(phase, head)
                elif n in (2, 6):
                    whole_turns()
                elif n == 3:
                    phase_changed(ALU.subtract)
                elif n == 4:
                    times_steps(whole, p_("phl"))
                elif n == 5:
                    phase_changed(ALU.add)
                elif n == 7:
                    phase_changed(ALU.subtract)
                    dve.sem_inc(phase_ready, 1)
                else:
                    step_parameters()
                    dve.wait_ge(used, RING + UNIT0["glu"])
                    for c in range(2):
                        link(dve.memset(bb[c][:, :, :], 0.0))

            def head_max(kind, n):
                b, h = n % 2, n - HEAD0[kind]
                dve.wait_ge(scores_ready, n + 1)
                scores = bank[2 + b][:, :]
                if n >= 2:
                    dve.wait_ge(probs_turned, n - 1)
                    dve.wait_ge(exp_ready, n - 1)
                flat = sp[b][:, :, :].rearrange("p t s -> p (t s)")
                if kind == "dil":
                    dve.scalar_tensor_tensor(out=flat, in0=dist[:, :, :].rearrange("p t s -> p (t s)"),
                                             scalar=-(2.0 ** -(h + 1)), in1=scores, op0=ALU.mult, op1=ALU.add)\
                        .then_inc(biased_scores, 1)
                    dve.wait_ge(biased_scores, n + 1)
                    scores = flat
                elif kind == "na":
                    dve.wait_ge(bias_masked, h + 1)
                    dve.scalar_tensor_tensor(out=flat, in0=scores, scalar=HD ** -0.5,
                                             in1=bias[b][:, :, :].rearrange("p t s -> p (t s)"), op0=ALU.mult, op1=ALU.add)\
                        .then_inc(biased_scores, 1)
                    dve.wait_ge(biased_scores, n + 1)
                    scores = flat
                dve.tensor_reduce(mx[:, b, :], scores.rearrange("p (t s) -> p t s", t=RT), AX.X, ALU.max)\
                    .then_inc(maxima_ready, 1)
                dve.wait_ge(maxima_ready, n + 1)
                scale = {"mla": QK ** -0.5, "cross": XHD ** -0.5}.get(kind, 1.0)
                dve.tensor_scalar(negm[:, b, :], mx[:, b, :], -scale, None, ALU.mult).then_inc(negmax_ready, 1)

            def head_sum(kind, n):
                b = n % 2
                dve.wait_ge(exp_ready, n + 1)
                if kind == "dil":
                    for t in range(RT):
                        ins = dve.scalar_tensor_tensor(out=sp[b][:, t, :], in0=sp[b][:, t, :], scalar=1.0,
                                                       in1=mult[:, t, :], op0=ALU.mult, op1=ALU.mult,
                                                       accum_out=rsum[:, b, t:t + 1])
                    ins.then_inc(probs_counted, 1)
                    dve.wait_ge(probs_counted, n + 1)
                if n >= 2:
                    dve.wait_ge(head_written, n - 1)
                dve.reciprocal(rden[:, b, :], rsum[:, b, :]).then_inc(recip_ready, 1)

            def head_pt(n):
                b = n % 2
                dve.wait_ge(probs_turned, n + 1)
                if n >= 2:
                    dve.wait_ge(values_ready, n - 1)
                dve.tensor_copy(pT[b][:, :, :], bank[4 + b][:, :].rearrange("p (k s) -> p k s", k=2)).then_inc(probs_copied, 1)

            def head_rope(kind, n):
                if kind == "mla":
                    dve.wait_ge(qk_turned, n + 1)
                    dve.wait_ge(scores_ready, n - 1)
                    dve.tensor_copy(rT[n % 2][:, :], bank[6 + n % 2][0:ROPE, 2 * P:4 * P]).then_inc(rope_copied, 1)

            def attend(kind, between=lambda n: None):
                ns = heads(kind)
                head_rope(kind, ns[0])
                head_rope(kind, ns[1])
                head_max(kind, ns[0])
                for n in ns:
                    head_sum(kind, n)
                    if n + 2 in ns:
                        head_rope(kind, n + 2)
                    if n + 1 in ns:
                        head_max(kind, n + 1)
                    head_pt(n)
                    between(n - ns[0])

            attend("dil", phase_table)
            norm_turn("yatt", UNIT0["glu"])

            def angles(k):
                dve.wait_ge(angles_added, k + 1)
                link(dve.tensor_scalar(half[:, :, :], turn[:, :, :], MAGIC, MAGIC, ALU.add, ALU.subtract))
                dve.tensor_tensor(turn[:, :, :], turn[:, :, :], half[:, :, :], ALU.subtract).then_inc(angles_reduced, 1)

            angles(0)
            dve.wait_ge(ld["sb"], 32)
            z3 = {c: bcast(p_(c), [1, STILES], [0, GC]) for c in ("zr", "zi")}
            for m, (b_, z) in enumerate(((0, "zr"), (1, "zi"), (1, "zr"), (0, "zi"))):
                link(dve.tensor_tensor(btmp[:, m], bn[b_][:, :, :], z3[z], ALU.mult))
            for c in range(2):
                for g in range(2):
                    rows, cols = slice(64 * g, 64 * g + 64), slice(GC * g, GC * g + GC)
                    ins = dve.tensor_tensor(bb[c][rows, :, cols], btmp[rows, 2 * c], btmp[rows, 2 * c + 1],
                                            (ALU.subtract, ALU.add)[c])
                ins.then_inc(bc_ready, 1)
            dve.wait_ge(bc_ready, 2)
            dve.wait_ge(ld["parity"], 16)
            dve.wait_ge(ld["sc"], 32)
            for c in range(2):
                for g in range(2):
                    ins = dve.tensor_scalar(cc[c][:, :, NST * g:NST * g + NST], cn[c][:, :, :], parity[:, g:g + 1],
                                            (1.0, -1.0)[c], ALU.mult, ALU.mult)
                ins.then_inc(bc_ready, 1)
            modulation(1, 64)
            dve.wait_ge(bc_turned, 8)

            def cosines(k):
                dve.wait_ge(sines_ready, 2 * k + 2)
                if k >= 2:
                    dve.wait_ge(products_ready, 16 * (k - 1))
                dve.tensor_scalar(co[k % 2][:, :, :], half[:, :, :], -2.0, 1.0, ALU.mult, ALU.add).then_inc(cosines_ready, 1)

            def scan_tile(j):
                q, b, n = j % 4, j % 2, 8 * j
                c_, s_ = co[j // 4 % 2][:, q, :], si[j // 4 % 2][:, q, :]
                br, bi = bank[q][:, 0:S], bank[q][:, S:2 * S]
                mag = par[:, PAR["mag"], j:j + 1].broadcast_to([P, S])

                def step(ins):
                    ins.then_inc(scan_steps, 1)

                dve.wait_ge(cosines_ready, j // 4 + 1)
                dve.wait_ge(drive_ready, j + 1)
                if j >= 2:
                    dve.wait_ge(products_ready, 4 * (j - 1))
                step(dve.tensor_tensor(rot[b][:, 0, :], br, c_, ALU.mult))
                step(dve.tensor_tensor(rot[b][:, 1, :], bi, s_, ALU.mult))
                step(dve.tensor_tensor(rot[b][:, 2, :], bi, c_, ALU.mult))
                step(dve.tensor_tensor(rot[b][:, 3, :], br, s_, ALU.mult))
                dve.wait_ge(scan_steps, n + 2)
                step(dve.tensor_tensor(rot[b][:, 0, :], rot[b][:, 0, :], rot[b][:, 1, :], ALU.add))
                dve.wait_ge(scan_steps, n + 4)
                step(dve.tensor_tensor(rot[b][:, 2, :], rot[b][:, 2, :], rot[b][:, 3, :], ALU.subtract))
                dve.wait_ge(scan_steps, n + 5)
                step(dve.tensor_tensor_scan(rot[b][:, 1, :], mag, rot[b][:, 0, :], 0.0, ALU.mult, ALU.add))
                dve.wait_ge(scan_steps, n + 6)
                step(dve.tensor_tensor_scan(rot[b][:, 3, :], mag, rot[b][:, 2, :], 0.0, ALU.mult, ALU.add))

            def output(k):
                dve.wait_ge(readout_ready, 4 * k + 4)
                if k:
                    dve.wait_ge(gelu_ready, k)
                else:
                    dve.wait_ge(ld["gstore"], 16)
                dve.scalar_tensor_tensor(out=yt[:, :], in0=uT[:, k, :], scalar=vec("ssm_d", k), in1=bank[4 + k % 2][:, 0:S],
                                         op0=ALU.mult, op1=ALU.add).then_inc(y_ready, 1)

            def split_output(k):
                dve.wait_ge(gelu_ready, k + 1)
                link(dve.tensor_copy(sa_hi[:, k, :], gt[:, :]))
                dve.tensor_tensor(sa_lo[:, k, :], gt[:, :], sa_hi[:, k, :].bitcast(F32), ALU.subtract).then_inc(y_split, 1)

            cosines(0)
            for k in range(8):
                scan_tile(4 * k)
                if k + 1 < 8:
                    angles(k + 1)
                scan_tile(4 * k + 1)
                if k:
                    output(k - 1)
                scan_tile(4 * k + 2)
                if k:
                    split_output(k - 1)
                scan_tile(4 * k + 3)
                if k + 1 < 8:
                    cosines(k + 1)
            output(7)
            split_output(7)

            blk = UNIT0["glu"] // 4
            dve.wait_ge(y_split, 8)
            for c in range(2):
                pumps(blk, 2 * c, 2)
            for c in range(2):
                kt = slice(4 * c, 4 * c + 4)
                g4 = rtmp[:, :, :].rearrange("p t (k s) -> p (t k) s", s=S)
                link(dve.tensor_tensor(g4, sa_hi[:, kt, :].bitcast(F32), sa_lo[:, kt, :].bitcast(F32), ALU.add))
                dve.wait_ge(acc_free[c], 2 * (CHUNK0["glu"] // 2) + 4)
                link(dve.tensor_tensor(sig[:, kt, :], sig[:, kt, :], g4, ALU.mult))
                link(dve.tensor_copy(y2_hi[:, kt, :], sig[:, kt, :]))
                dve.tensor_tensor(y2_lo[:, kt, :], sig[:, kt, :], y2_hi[:, kt, :].bitcast(F32), ALU.subtract)\
                    .then_inc(gated_y_split, 1)
            dve.wait_ge(gated_y_split, 2)
            dve.wait_ge(ld["gate1"], 16)
            with dve.Fori(0, 2) as i:
                for c in range(2):
                    blk = UNIT0["out1"] // 4 + i * 2
                    pumps(blk, 4 * c, 4)
                    gated_out(blk, 4 * c + 3, CHUNK0["out1"] // 2 + i, c, i * (2 * CW) + c * CW, gate1_b, i * 2 + c)

            def times_up(stage, blk, hq):
                unit_used(blk, 7)
                dve.wait_ge(acc_free[0], 2 * hq + 4)
                for t in range(RT):
                    if stage == "ffn2":
                        ins = dve.scalar_tensor_tensor(out=fg[:, t, :], in0=bank[2 + t][:, :], scalar=rstd[:, t:t + 1],
                                                       in1=fg[:, t, :], op0=ALU.mult, op1=ALU.mult)
                    else:
                        ins = dve.tensor_tensor(fg[:, t, :], fg[:, t, :], bank[2 + t][:, :], ALU.mult)
                    ins.then_inc(acc_free[1], 1)

            def hidden_rests(f, k):
                for hf in range(2):
                    dve.wait_ge(hidden_hi_done, 2 * f + hf + 1)
                    ks = bass.ds(k + 2 * hf, 2)
                    dve.tensor_tensor(act_lo[:, ks, :], bank[4 + hf][:, :].rearrange("p (k s) -> p k s", k=2),
                                      act_hi[:, ks, :].bitcast(F32), ALU.subtract).then_inc(hidden_lo_done, 1)

            def ffn(stage, f0, residual):
                blk, hq = UNIT0[stage] // 4, CHUNK0[stage] // 2
                for third, (c0, n) in enumerate(THIRDS):
                    pumps(blk, 0, 8)
                    times_up(stage, blk, hq)
                    with dve.Fori(1, n) as i:
                        pumps(blk + i * 2, 0, 4)
                        hidden_rests(i + (f0 + c0 - 1), i * 4 - 4)
                        pumps(blk + i * 2, 4, 4)
                        times_up(stage, blk + i * 2, hq + i)
                    blk, hq = blk + 2 * n, hq + n
                    for c in range(4):
                        if c == 0:
                            pumps(blk, 0, 1)
                            hidden_rests(f0 + c0 + n - 1, 4 * n - 4)
                            pumps(blk, 1, n - 1)
                        else:
                            pumps(blk, n * c, n)
                        residual(blk, n * c + n - 1, hq, c, c * CW, third, c)
                    blk, hq = blk + n, hq + 2

            norm_turn("h2", UNIT0["ffn1"])
            dve.wait_ge(ld["gate2"], 16)
            ffn("ffn1", 0, lambda blk, j, hq, c, col, third, n:
                gated_out(blk, j, hq, c, col, wide_b, n + (4 + 4 * third)))
            norm_turn("hmix", UNIT0["in2"])
            with dve.Fori(0, 3) as i:
                for c in range(2):
                    blk = UNIT0["in2"] // 4 + i * 2
                    pumps(blk, 4 * c, 4)
                    copy_out(blk, 4 * c + 3, c, proj2[:, 1, bass.ds(i * (2 * CW) + c * CW, CW)], norm="hmix")
            blk = UNIT0["in2"] // 4 + 6
            for c in range(2):
                cols = (CW, IN2 - 7 * CW)[c]
                pumps(blk, 4 * c, 4)
                copy_out(blk, 4 * c + 3, c, proj2[:, 1, (6 + c) * CW:(6 + c) * CW + cols], cols, "hmix")
            norm_turn("cq", UNIT0["uq"])
            norm_turn("ckv", UNIT0["uq"])
            for c in range(4):
                pumps(UNIT0["uq"] // 4, c, 1)
                copy_out(UNIT0["uq"] // 4, c, c, q_mla[:, 1, 2 * c:2 * c + 2, :].rearrange("p a b -> p (a b)"), 2 * QK)
            def rope_piece(n):
                q1, q2 = q_mla[:, :, :, NOPE:NOPE + HROPE], q_mla[:, :, :, NOPE + HROPE:QK]
                tmp = [a[:, :, :] for a in xn + full]
                tq = [a.rearrange("p t (h e) -> p t h e", e=HROPE) for a in tmp]
                cq, sq = (bcast(a[:, :, :], [HROPE, RT], [0, HEADS], [1, HROPE]) for a in (ropec, ropes))
                if n == 0:
                    chunks_out(dve, CHUNK0["ukv"])
                    dve.wait_ge(norm_split, PAIR0["yna"])
                    dve.wait_ge(ld["na_const"], 48)
                    dve.tensor_tensor(tq[0], q1, cq, ALU.mult)
                elif n == 1:
                    dve.tensor_tensor(tq[1], q2, sq, ALU.mult)
                elif n == 2:
                    dve.tensor_tensor(tq[2], q1, sq, ALU.mult)
                elif n == 3:
                    link(dve.tensor_tensor(tq[3], q2, cq, ALU.mult))
                elif n == 4:
                    dve.tensor_tensor(q1, tq[0], tq[1], ALU.subtract)
                elif n == 5:
                    link(dve.tensor_tensor(q2, tq[2], tq[3], ALU.add))
                elif n == 6:
                    k1, k2 = proj2[:, :, C_KR:C_KR + HROPE], proj2[:, :, C_KR + HROPE:IN2]
                    tk = [a[:, :, 0:HROPE] for a in tmp]
                    for o, x_, table in zip(tk, (k1, k2, k1, k2), (ropec, ropes, ropes, ropec)):
                        ins = dve.tensor_tensor(o, x_, table[:, :, :], ALU.mult)
                    link(ins)
                    dve.tensor_tensor(kr[:, :, 0:HROPE], tk[0], tk[1], ALU.subtract)
                    link(dve.tensor_tensor(kr[:, :, HROPE:ROPE], tk[2], tk[3], ALU.add))
                    dve.sem_inc(key_rotated, 1)

            attend("na", rope_piece)
            for c in range(4):
                pumps(UNIT0["ukv"] // 4, c, 1)
                copy_out(UNIT0["ukv"] // 4, c, c, proj2[:, 1, NA_W + c * CW:NA_W + c * CW + CW])
            dve.wait_ge(key_turned, 1)
            dve.tensor_copy(krT[:, :], bank[7][0:ROPE, 2 * P:4 * P]).then_inc(key_copied, 1)
            attend("mla")
            norm_turn("yna", UNIT0["out2"])
            norm_turn("ymla", UNIT0["out2"])

            def add_square(stage):
                with dve.Fori(0, 2) as i:
                    for c in range(2):
                        blk = UNIT0[stage] // 4 + i * 2
                        pumps(blk, 4 * c, 4)
                        add_out(blk, 4 * c + 3, CHUNK0[stage] // 2 + i, c, i * (2 * CW) + c * CW)

            add_square("out2")
            norm_turn("hmem", UNIT0["xq"])
            with dve.Fori(0, 2) as i:
                for c in range(2):
                    blk = UNIT0["xq"] // 4 + i * 2
                    pumps(blk, 4 * c, 4)
                    copy_out(blk, 4 * c + 3, c, xq[:, 1, bass.ds(i * (2 * CW) + c * CW, CW)], norm="hmem")
            attend("cross")
            norm_turn("ocross", UNIT0["xo"])
            add_square("xo")
            norm_turn("hffn", UNIT0["ffn2"])
            ffn("ffn2", FCH, lambda blk, j, hq, c, col, third, n: add_out(blk, j, hq, c, col))
            stats("final", STAT0["final"], PAIR0["hffn"] + 8, D)
            dve.wait_ge(ld["final"], 16)
            for t in range(RT):
                dve.scalar_tensor_tensor(out=x[:, t, :], in0=x[:, t, :], scalar=rstd[:, t:t + 1], in1=wide_b[:, :],
                                         op0=ALU.mult, op1=ALU.mult).then_inc(out_rows_ready, 1)


_INS = ["x", "c", "w_ada", "b_ada", "norm1_w", "w_in", "ssm_a_re", "ssm_a_im", "ssm_log_dt", "ssm_b_re", "ssm_b_im",
        "ssm_c_re", "ssm_c_im", "ssm_d", "ssm_w_glu", "q_norm_w", "k_norm_w", "w_out", "norm2_w", "w_ffn_gate",
        "w_ffn_up", "w_ffn_down", "mem_2", "ln_mix_2", "w_in_2", "q_norm_2", "kv_norm_2", "w_uq_2", "w_ukv_2",
        "na_rpb_2", "na_out_norm_2", "mla_out_norm_2", "w_out_2", "ln_mem_2", "mem_norm_2", "w_xq_2", "w_xk_2",
        "w_xv_2", "w_xo_2", "ln_ffn_2", "w_gate_2", "w_up_2", "w_down_2", "final_norm_2"]


def shape_constants():
    import numpy as np

    t, s = np.arange(S)[:, None], np.arange(S)[None, :]
    d = t - s
    count = ((d >= 0) & (d <= 128)).astype(np.float32) + ((d >= 0) & (d % 4 == 0)) + ((d >= 0) & (d % 16 == 0))
    dist = np.where(count > 0, d, 1e33)
    col = np.arange(GRID_W)
    start = np.clip(col - NA_COLS // 2, 0, GRID_W - NA_COLS)[:, None]
    window = (col[None, :] >= start) & (col[None, :] < start + NA_COLS)
    inv = 1.0 / (np.float32(10000.0) ** (np.arange(0, ROPE, 2, dtype=np.float32) / ROPE))
    ang = np.arange(S, dtype=np.float32)[:, None] * inv[None, :].astype(np.float32)
    tables = {"dist": dist, "mult": count, "colmask": np.tile(np.where(window, 0.0, -1e30), (2, NA_ROWS)),
              "cos": np.cos(ang), "sin": np.sin(ang), "iota": np.tile(np.arange(S), (P, 1)),
              "parity": np.stack([np.arange(P) // GC % 2 == 0, np.arange(P) // GC % 2 == 1], 1)}
    return {"const_" + n: np.ascontiguousarray(a, dtype=np.float32) for n, a in tables.items()}


def kernel(**inputs):
    import numpy as np
    import concourse.bacc as bacc
    from concourse.bass_utils import run_bass_kernel_spmd

    nc = bacc.Bacc("TRN2", target_bir_lowering=False, num_devices=1)
    arrays = {"in_" + n: np.ascontiguousarray(inputs[n]) for n in _INS}
    arrays.update(shape_constants())
    aps = {n: nc.dram_tensor(n, a.shape, mybir.dt.from_np(a.dtype), kind="ExternalInput").ap() for n, a in arrays.items()}
    out = nc.dram_tensor("out", (1, S, D), F32, kind="ExternalOutput").ap()
    build(nc, {n.removeprefix("in_"): a for n, a in aps.items()}, out)
    r = run_bass_kernel_spmd(nc, [arrays], core_ids=[0])
    return r.results[0]["out"]
```
